# Optimizing a Trainium2 kernel written in Bass

```python
import math
import jax, jax.numpy as jnp
from jax import lax
import numpy as np

D_MODEL = 1024
BATCH = 1
SEQ = 128
DEPTH = 2
DEC_BATCH = 1
DEC_SEQ = 1024
PAST_LEN = 256

GRID_W = 64
N_AB = (DEPTH + 1) // 2
N_C = DEPTH // 2
DIFF_HEADS = 8
DIFF_QK = 32
DIFF_V = 2 * DIFF_QK
DIFF_WIDTH = DIFF_HEADS * DIFF_V
DIFF_QW = DIFF_HEADS * 2 * DIFF_QK
ROPE_PAIRS = DIFF_QK // 4
ROPE_BASE = 10000.0
Q_BLOCK = 128
RWKV_HEADS = 8
RWKV_HS = 64
RWKV_WIDTH = RWKV_HEADS * RWKV_HS
DECAY_LORA = 64
ICL_LORA = 64
GATE_LORA = 128
RWKV_IN = 3 * RWKV_WIDTH + DECAY_LORA + ICL_LORA + GATE_LORA
AB_IN = 2 * DIFF_QW + DIFF_WIDTH + RWKV_IN
AB_OUT = DIFF_WIDTH + RWKV_WIDTH
HYENA_ORDER = 2
BANDS = 16
FILTER_EMB = 1 + 2 * BANDS
FILTER_WIDTH = 64
FILTER_OUT = HYENA_ORDER * 2 * D_MODEL
MAX_DECAY = math.log(1e-2) / 0.3
MIN_DECAY = math.log(1e-2) / 1.5
D_FF = ((8 * D_MODEL // 3 + 255) // 256) * 256
RMS_EPS = 1e-6
GN_EPS = 64e-5

kernel_name = 'hybrid_diffattn_rwkv7_hyena_prefix_dit_step'

def _lambda_init(l):
    return 0.8 - 0.6 * math.exp(-0.3 * l)

def _layer_slice(stack, i):
    return {n: a[i] for n, a in stack.items()}

def _rmsnorm(x, g):
    xf = x.astype(jnp.float32)
    y = xf * lax.rsqrt(jnp.mean(xf * xf, axis=-1, keepdims=True) + RMS_EPS)
    return y.astype(x.dtype) * g

def _ada(cond, w, b):
    m = jax.nn.silu(cond) @ w + b
    return [t[:, None, :] for t in jnp.split(m, 6, axis=-1)]

def _ffn_sub(x, shift, scale, gate, g, w1, w3, w2):
    h = _rmsnorm(x, g) * (1 + scale) + shift
    return x + gate * ((jax.nn.silu(h @ w1) * (h @ w3)) @ w2)

def _axial_rope(L):
    n_rows = L // GRID_W
    row = jnp.repeat(jnp.arange(n_rows, dtype=jnp.float32), GRID_W)
    col = jnp.tile(jnp.arange(GRID_W, dtype=jnp.float32), n_rows)
    inv = ROPE_BASE ** (-jnp.arange(ROPE_PAIRS, dtype=jnp.float32) / ROPE_PAIRS)
    ar = row[:, None] * inv[None]
    ac = col[:, None] * inv[None]
    ang = jnp.concatenate([ar, ar, ac, ac], axis=-1)
    return jnp.cos(ang), jnp.sin(ang)

def _apply_rope(x, cos, sin):
    xs = x.reshape(x.shape[:-1] + (2, 2, ROPE_PAIRS))
    rot = jnp.stack([-xs[..., 1, :], xs[..., 0, :]], axis=-2).reshape(x.shape)
    c = cos.astype(x.dtype)[None, :, None, None, :]
    s = sin.astype(x.dtype)[None, :, None, None, :]
    return x * c + rot * s

def _diff_attend(q, k, v, lam):
    B, H, _, Lq, dq = q.shape
    nblk = Lq // Q_BLOCK
    qb = jnp.moveaxis(q.reshape(B, H, 2, nblk, Q_BLOCK, dq), 3, 0)
    scale = dq ** -0.5

    def one(qi):
        s = jnp.einsum('bhmqd,bhmkd->bhmqk', qi, k).astype(jnp.float32) * scale
        p = jax.nn.softmax(s, axis=-1)
        p = p[:, :, 0] - lam * p[:, :, 1]
        return jnp.einsum('bhqk,bhkd->bhqd', p.astype(v.dtype), v)

    o = lax.map(one, qb)
    return jnp.moveaxis(o, 0, 2).reshape(B, H, Lq, v.shape[-1])

def _head_rms(o, g):
    of = o.astype(jnp.float32)
    y = of * lax.rsqrt(jnp.mean(of * of, axis=-1, keepdims=True) + 1e-5)
    return y.astype(o.dtype) * g

def _center_shift(p, mu):
    prev = jnp.pad(p, ((0, 0), (1, 0), (0, 0)))[:, :-1]
    nxt = jnp.pad(p, ((0, 0), (0, 1), (0, 0)))[:, 1:]
    return p + mu[0] * (prev - p) + mu[1] * (nxt - p)

def _rwkv_scan(r, w, k, v, kk, b, s0, reverse):
    xs = tuple(jnp.moveaxis(t.astype(jnp.float32), 1, 0) for t in (r, w, k, v, kk, b))

    def step(S, inp):
        r_t, w_t, k_t, v_t, kk_t, b_t = inp
        sa = jnp.einsum('bhvk,bhk->bhv', S, -kk_t)
        S = S * w_t[:, :, None, :] + sa[..., None] * b_t[:, :, None, :] + v_t[..., None] * k_t[:, :, None, :]
        return S, jnp.einsum('bhvk,bhk->bhv', S, r_t)

    S, y = lax.scan(step, s0.astype(jnp.float32), xs, reverse=reverse)
    return jnp.moveaxis(y, 0, 1), S

def _rwkv_mix(rw, lp, s0f, s0b):
    B, L, _ = rw.shape
    W = RWKV_WIDTH
    rw = _center_shift(rw, lp['mu'])
    r, k, v = rw[..., :W], rw[..., W:2 * W], rw[..., 2 * W:3 * W]
    o = 3 * W
    wd = rw[..., o:o + DECAY_LORA]
    ad = rw[..., o + DECAY_LORA:o + DECAY_LORA + ICL_LORA]
    gd = rw[..., o + DECAY_LORA + ICL_LORA:]
    g = jax.nn.sigmoid(gd) @ lp['g_up']
    hd = lambda t: t.reshape(B, L, RWKV_HEADS, RWKV_HS)
    kk = hd((k * lp['k_k']).astype(jnp.float32))
    kk = kk / jnp.maximum(jnp.sqrt(jnp.sum(kk * kk, axis=-1, keepdims=True)), 1e-12)
    outs, states = [], []
    for d, s0 in enumerate((s0f, s0b)):
        w = -jax.nn.softplus(-(lp['w0'][d] + jnp.tanh(wd) @ lp['w_up'][d])) - 0.5
        decay = jnp.exp(-jnp.exp(w.astype(jnp.float32)))
        a = jax.nn.sigmoid(lp['a0'][d] + ad @ lp['a_up'][d])
        kd = k * (1 + (a - 1) * lp['k_a'])
        yd, sd = _rwkv_scan(hd(r), hd(decay), hd(kd), hd(v), kk, kk * hd(a).astype(jnp.float32), s0, d == 1)
        bonus = jnp.sum(hd(r) * hd(kd) * lp['r_k'], axis=-1, keepdims=True) * hd(v)
        outs.append(yd + bonus.astype(jnp.float32))
        states.append(sd)
    y = outs[0] + outs[1]
    mu = jnp.mean(y, axis=-1, keepdims=True)
    var = jnp.mean(jnp.square(y - mu), axis=-1, keepdims=True)
    y = ((y - mu) * lax.rsqrt(var + GN_EPS)).reshape(B, L, W).astype(rw.dtype)
    y = (y * lp['ln_g'] + lp['ln_b']) * g
    return y, states[0].astype(rw.dtype), states[1].astype(rw.dtype)

def _ab_mixer(h, lp, lam_init, rope, k_ctx, v_ctx, s0f, s0b):
    B, L, _ = h.shape
    p = h @ lp['w_in']
    q = p[..., :DIFF_QW].reshape(B, L, DIFF_HEADS, 2, DIFF_QK)
    k = p[..., DIFF_QW:2 * DIFF_QW].reshape(B, L, DIFF_HEADS, 2, DIFF_QK)
    v = p[..., 2 * DIFF_QW:2 * DIFF_QW + DIFF_WIDTH].reshape(B, L, DIFF_HEADS, DIFF_V)
    rw = p[..., 2 * DIFF_QW + DIFF_WIDTH:]
    if rope is not None:
        q = _apply_rope(q, rope[0], rope[1])
        k = _apply_rope(k, rope[0], rope[1])
    q = q.transpose(0, 2, 3, 1, 4)
    k = k.transpose(0, 2, 3, 1, 4)
    v = v.transpose(0, 2, 1, 3)
    if k_ctx is None:
        keys, vals = k, v
    else:
        keys = jnp.concatenate([k_ctx, k], axis=3)
        vals = jnp.concatenate([v_ctx, v], axis=2)
    lv = lp['lam'].astype(jnp.float32)
    lam = jnp.exp(jnp.sum(lv[0] * lv[1])) - jnp.exp(jnp.sum(lv[2] * lv[3])) + lam_init
    o = _diff_attend(q, keys, vals, lam)
    o = _head_rms(o, lp['subln_g']) * (1 - lam_init)
    o = o.transpose(0, 2, 1, 3).reshape(B, L, DIFF_WIDTH)
    if s0f is None:
        s0f = jnp.zeros((B, RWKV_HEADS, RWKV_HS, RWKV_HS), jnp.float32)
        s0b = s0f
    r_out, sf, sb = _rwkv_mix(rw, lp, s0f, s0b)
    out = jnp.concatenate([o, r_out], axis=-1) @ lp['w_out']
    return out, k, v, sf, sb

def _short_conv(z, w, b):
    L = z.shape[1]
    zp = jnp.pad(z, ((0, 0), (1, 1), (0, 0)))
    return zp[:, :L] * w[0] + zp[:, 1:L + 1] * w[1] + zp[:, 2:] * w[2] + b

def _hyena_filters(L, lp):
    f32 = jnp.float32
    t = jnp.linspace(0.0, 1.0, L, dtype=f32)[:, None]
    wpos = 2.0 * math.pi * jnp.arange(L, dtype=f32)[:, None] / L
    f = jnp.linspace(1e-4, BANDS - 1, BANDS, dtype=f32)[None]
    z = jnp.concatenate([t, jnp.cos(f * wpos), -jnp.sin(f * wpos)], axis=-1)
    fr = lp['f_freq'].astype(f32)
    hdn = jnp.sin(fr[0] * (z @ lp['f_w0'].astype(f32) + lp['f_b0'].astype(f32)))
    hdn = jnp.sin(fr[1] * (hdn @ lp['f_w1'].astype(f32) + lp['f_b1'].astype(f32)))
    hdn = jnp.sin(fr[2] * (hdn @ lp['f_w2'].astype(f32) + lp['f_b2'].astype(f32)))
    filt = (hdn @ lp['f_w3'].astype(f32)).reshape(L, HYENA_ORDER, 2, D_MODEL)
    deltas = jnp.abs(jnp.linspace(MIN_DECAY, MAX_DECAY, D_MODEL, dtype=f32))
    window = jnp.exp(-t * deltas[None])
    return filt * window[:, None, None, :]

def _bidir_long_conv(u, h_fwd, h_bwd, bias):
    L = u.shape[1]
    kern = jnp.concatenate([h_fwd, jnp.zeros((1, h_fwd.shape[1]), h_fwd.dtype), h_bwd[:0:-1]], axis=0)
    uf32 = u.astype(jnp.float32)
    uf = jnp.fft.rfft(uf32, n=2 * L, axis=1)
    kf = jnp.fft.rfft(kern, axis=0)
    y = jnp.fft.irfft(uf * kf[None], n=2 * L, axis=1)[:, :L]
    return (y + uf32 * bias.astype(jnp.float32)).astype(u.dtype)

def _hyena_mixer(h, lp):
    L = h.shape[1]
    z = _short_conv(h @ lp['w_in'] + lp['b_in'], lp['conv_w'], lp['conv_b'])
    x1, x2, v = jnp.split(z, 3, axis=-1)
    filt = _hyena_filters(L, lp)
    u = x1 * _bidir_long_conv(v, filt[:, 0, 0], filt[:, 0, 1], lp['bias'][0])
    u = x2 * _bidir_long_conv(u, filt[:, 1, 0], filt[:, 1, 1], lp['bias'][1])
    return u @ lp['w_out'] + lp['b_out']

def setup_inputs(seed: int = 0) -> dict:
    key = jax.random.key(seed)
    ks = iter(jax.random.split(key, 64))
    D = D_MODEL

    def nrm(shape, scale):
        return jax.random.normal(next(ks), shape, jnp.float32) * scale

    def unif(shape, lo, hi):
        return jax.random.uniform(next(ks), shape, jnp.float32, lo, hi)

    return {
        'x_prompt': nrm((BATCH, SEQ, D), 1.0),
        'x_sample': nrm((DEC_BATCH, DEC_SEQ, D), 1.0),
        'cache_diff_k': nrm((DEC_BATCH, N_AB, DIFF_HEADS, 2, PAST_LEN, DIFF_QK), 1.0),
        'cache_diff_v': nrm((DEC_BATCH, N_AB, DIFF_HEADS, PAST_LEN, DIFF_V), 1.0),
        'state_rwkv_fwd': nrm((DEC_BATCH, N_AB, RWKV_HEADS, RWKV_HS, RWKV_HS), 0.5),
        'state_rwkv_bwd': nrm((DEC_BATCH, N_AB, RWKV_HEADS, RWKV_HS, RWKV_HS), 0.5),
        'c': nrm((DEC_BATCH, D), 1.0),
        'c_ctx': nrm((D,), 1.0),
        'ada_w': nrm((DEPTH, D, 6 * D), 0.5 * D ** -0.5),
        'ada_b': nrm((DEPTH, 6 * D), 0.02),
        'norm1_g': 1.0 + nrm((DEPTH, D), 0.05),
        'norm2_g': 1.0 + nrm((DEPTH, D), 0.05),
        'ffn_w1': nrm((DEPTH, D, D_FF), D ** -0.5),
        'ffn_w3': nrm((DEPTH, D, D_FF), D ** -0.5),
        'ffn_w2': nrm((DEPTH, D_FF, D), D_FF ** -0.5),
        'final_g': 1.0 + nrm((D,), 0.05),
        'ab_w_in': nrm((N_AB, D, AB_IN), D ** -0.5),
        'ab_w_out': nrm((N_AB, AB_OUT, D), AB_OUT ** -0.5),
        'diff_lambda': nrm((N_AB, 4, DIFF_QK), 0.1),
        'diff_subln_g': 1.0 + nrm((N_AB, DIFF_V), 0.05),
        'rwkv_mu': unif((N_AB, 2, RWKV_IN), 0.0, 0.5),
        'rwkv_w0': unif((N_AB, 2, RWKV_WIDTH), -6.0, 1.0),
        'rwkv_w_up': nrm((N_AB, 2, DECAY_LORA, RWKV_WIDTH), 0.1),
        'rwkv_a0': nrm((N_AB, 2, RWKV_WIDTH), 0.5),
        'rwkv_a_up': nrm((N_AB, 2, ICL_LORA, RWKV_WIDTH), 0.1),
        'rwkv_g_up': nrm((N_AB, GATE_LORA, RWKV_WIDTH), GATE_LORA ** -0.5),
        'rwkv_k_k': 0.85 + nrm((N_AB, RWKV_WIDTH), 0.05),
        'rwkv_k_a': 1.0 + nrm((N_AB, RWKV_WIDTH), 0.05),
        'rwkv_r_k': nrm((N_AB, RWKV_HEADS, RWKV_HS), 0.1),
        'rwkv_ln_g': 1.0 + nrm((N_AB, RWKV_WIDTH), 0.05),
        'rwkv_ln_b': nrm((N_AB, RWKV_WIDTH), 0.02),
        'hy_w_in': nrm((N_C, D, 3 * D), D ** -0.5),
        'hy_b_in': nrm((N_C, 3 * D), 0.02),
        'hy_conv_w': nrm((N_C, 3, 3 * D), 0.5),
        'hy_conv_b': nrm((N_C, 3 * D), 0.02),
        'hy_f_w0': nrm((N_C, FILTER_EMB, FILTER_WIDTH), FILTER_EMB ** -0.5),
        'hy_f_b0': nrm((N_C, FILTER_WIDTH), 0.1),
        'hy_f_w1': nrm((N_C, FILTER_WIDTH, FILTER_WIDTH), FILTER_WIDTH ** -0.5),
        'hy_f_b1': nrm((N_C, FILTER_WIDTH), 0.1),
        'hy_f_w2': nrm((N_C, FILTER_WIDTH, FILTER_WIDTH), FILTER_WIDTH ** -0.5),
        'hy_f_b2': nrm((N_C, FILTER_WIDTH), 0.1),
        'hy_f_w3': nrm((N_C, FILTER_WIDTH, FILTER_OUT), 0.01),
        'hy_f_freq': 1.0 + nrm((N_C, 3, FILTER_WIDTH), 0.1),
        'hy_bias': nrm((N_C, HYENA_ORDER, D), 0.5),
        'hy_w_out': nrm((N_C, D, D), D ** -0.5),
        'hy_b_out': nrm((N_C, D), 0.02),
    }

def reference(x_prompt, x_sample, cache_diff_k, cache_diff_v, state_rwkv_fwd, state_rwkv_bwd, c, c_ctx,
              ada_w, ada_b, norm1_g, norm2_g, ffn_w1, ffn_w3, ffn_w2, final_g,
              ab_w_in, ab_w_out, diff_lambda, diff_subln_g, rwkv_mu, rwkv_w0, rwkv_w_up, rwkv_a0, rwkv_a_up,
              rwkv_g_up, rwkv_k_k, rwkv_k_a, rwkv_r_k, rwkv_ln_g, rwkv_ln_b,
              hy_w_in, hy_b_in, hy_conv_w, hy_conv_b, hy_f_w0, hy_f_b0, hy_f_w1, hy_f_b1, hy_f_w2, hy_f_b2,
              hy_f_w3, hy_f_freq, hy_bias, hy_w_out, hy_b_out):
    ab = dict(w_in=ab_w_in, w_out=ab_w_out, lam=diff_lambda, subln_g=diff_subln_g, mu=rwkv_mu,
              w0=rwkv_w0, w_up=rwkv_w_up, a0=rwkv_a0, a_up=rwkv_a_up, g_up=rwkv_g_up, k_k=rwkv_k_k,
              k_a=rwkv_k_a, r_k=rwkv_r_k, ln_g=rwkv_ln_g, ln_b=rwkv_ln_b)
    hy = dict(w_in=hy_w_in, b_in=hy_b_in, conv_w=hy_conv_w, conv_b=hy_conv_b, f_w0=hy_f_w0, f_b0=hy_f_b0,
              f_w1=hy_f_w1, f_b1=hy_f_b1, f_w2=hy_f_w2, f_b2=hy_f_b2, f_w3=hy_f_w3, f_freq=hy_f_freq,
              bias=hy_bias, w_out=hy_w_out, b_out=hy_b_out)

    x = x_prompt
    new_k, new_v, new_sf, new_sb = [], [], [], []
    for l in range(DEPTH):
        sh1, sc1, gt1, sh2, sc2, gt2 = _ada(c_ctx[None], ada_w[l], ada_b[l])
        h = _rmsnorm(x, norm1_g[l]) * (1 + sc1) + sh1
        if l % 2 == 0:
            out, kc, vc, sf, sb = _ab_mixer(h, _layer_slice(ab, l // 2), _lambda_init(l),
                                            None, None, None, None, None)
            new_k.append(kc)
            new_v.append(vc)
            new_sf.append(sf)
            new_sb.append(sb)
        else:
            out = _hyena_mixer(h, _layer_slice(hy, l // 2))
        x = x + gt1 * out
        x = _ffn_sub(x, sh2, sc2, gt2, norm2_g[l], ffn_w1[l], ffn_w3[l], ffn_w2[l])
    y_prompt = _rmsnorm(x, final_g)
    new_diff_k = jnp.stack(new_k, axis=1)
    new_diff_v = jnp.stack(new_v, axis=1)
    new_rwkv_fwd = jnp.stack(new_sf, axis=1)
    new_rwkv_bwd = jnp.stack(new_sb, axis=1)

    rope = _axial_rope(x_sample.shape[1])
    x = x_sample
    for l in range(DEPTH):
        sh1, sc1, gt1, sh2, sc2, gt2 = _ada(c, ada_w[l], ada_b[l])
        h = _rmsnorm(x, norm1_g[l]) * (1 + sc1) + sh1
        if l % 2 == 0:
            i = l // 2
            out, _, _, _, _ = _ab_mixer(h, _layer_slice(ab, i), _lambda_init(l), rope,
                                        cache_diff_k[:, i], cache_diff_v[:, i],
                                        state_rwkv_fwd[:, i], state_rwkv_bwd[:, i])
        else:
            out = _hyena_mixer(h, _layer_slice(hy, l // 2))
        x = x + gt1 * out
        x = _ffn_sub(x, sh2, sc2, gt2, norm2_g[l], ffn_w1[l], ffn_w3[l], ffn_w2[l])
    y_sample = _rmsnorm(x, final_g)

    return (y_prompt, y_sample, new_diff_k, new_diff_v, new_rwkv_fwd, new_rwkv_bwd)


_drawn_inputs = setup_inputs


def setup_inputs(seed=0):
    import zlib

    import numpy as np

    out = dict(_drawn_inputs(seed))
    spreads = {}
    factors = {'cache_diff_k': 3.198,
     'state_rwkv_fwd': 8.0,
     'state_rwkv_bwd': 8.0,
     'norm2_g': 2.929,
     'diff_lambda': 8.0,
     'diff_subln_g': 3.462,
     'rwkv_r_k': 8.0,
     'rwkv_ln_g': 8.0,
     'rwkv_ln_b': 8.0,
     'hy_b_in': 3.14,
     'hy_b_out': 8.0,
     'hy_conv_b': 3.206}
    for name, (base, spread) in spreads.items():
        noise = np.random.default_rng([zlib.crc32(name.encode()), seed]).standard_normal(out[name].shape)
        drawn = base * np.exp(spread * noise) if base else spread * noise
        out[name] = __import__('jax').numpy.asarray(drawn.astype(out[name].dtype))
    for name, factor in factors.items():
        out[name] = (out[name] * factor).astype(out[name].dtype)
    return out
```

```python
import math
from contextlib import ExitStack

import numpy as np

import concourse.bass as bass
from concourse import mybir

F32 = mybir.dt.float32
ALU = mybir.AluOpType
ACT = mybir.ActivationFunctionType
AX = mybir.AxisListType
ds = bass.ds

D = 1024
KT = D // 128
NP_, NL = 128, 1024
T = NP_ + NL
TC = T // 3
PAST = 256
HEADS, DQ, DV = 8, 32, 64
AB_IN = 3328
RW_TILES = 14
FF = 2816
FT = FF // 128
C = 64
LAM_INIT = 0.2
GROUPS = ((0, NP_), (NP_, NL))

ROWS = [("ada_b", 96), ("norm1", 16), ("norm2", 16), ("final", 8), ("mu", 28), ("w0", 8), ("a0", 8),
        ("k_k", 4), ("k_a", 4), ("r_k", 4), ("ln_g", 4), ("ln_b", 4), ("b_in", 24), ("conv_w", 72),
        ("conv_b", 24), ("hbias", 16), ("b_out", 8), ("subln", 1)]
COL, _n = {}, 0
for _name, _rows in ROWS:
    COL[_name] = _n
    _n += _rows
PV_TILES = -(-_n // 128)

CBLK = [("ident", 128), ("blockones", 128), ("mask_f", 128), ("mask_b", 128), ("lt", 64), ("gt", 64),
        ("ident2", 64), ("scan", 256), ("rot", 128), ("nz", 1), ("pad", 7)]
CCOL, _n = {}, 0
for _name, _w in CBLK:
    CCOL[_name] = (_n, _w)
    _n += _w
CW = _n

X0, H0, BIG, WB, CST = 0, 9216, 18432, 43776, 47872
PV0 = CST + CW
MOD0 = PV0 + 128 * PV_TILES
ONE0 = MOD0 + 192
COEF0 = ONE0 + 128
SM0 = COEF0 + 16
RK0 = SM0 + 64
END = RK0 + 512


def trip(eng, n):
    return eng.Fori(0, n) if n > 1 else _Once()


class _Once:
    def __enter__(self):
        return 0

    def __exit__(self, *a):
        return False


class Kit:

    def __init__(self, nc, ctx, arena, psum):
        self.nc, self.ctx, self.arena, self.psum = nc, ctx, arena, psum
        self.sems = []
        self.X = self.tiles(X0, KT, T)
        self.H = self.tiles(H0, KT, T)
        self.ident = self.const("ident")
        self.ones = self.at(ONE0, 128)
        self.pv = self.at(PV0, 128 * PV_TILES)
        self.mod = self.at(MOD0, 192).rearrange("p (l m g) -> p l m g", l=2, g=2)

    def at(self, off, n):
        return self.arena[:, off:off + n]

    def tiles(self, off, n, w):
        return self.arena[:, off:off + n * w].rearrange("p (k n) -> p k n", k=n)

    def const(self, name):
        o, w = CCOL[name]
        return self.at(CST + o, w)

    def col(self, name, j=0, n=1):
        return self.pv[:, COL[name] + j:COL[name] + j + n]

    def bank(self, b, n=512):
        return self.psum[:, b * 512:b * 512 + n]

    def sem(self, name):
        self.sems.append(self.nc.alloc_semaphore(name=name))
        return self.sems[-1]

    def reuse_semaphores(self):
        self.nc.clear_and_free_semaphores(self.sems)
        self.nc.all_engine_barrier()
        self.sems = []


def stage_setup(k, A, consts):
    nc = k.nc
    stg = k.tiles(WB, PV_TILES, 128)
    cond = k.at(WB + 1024, 128)
    condT = k.at(WB + 1200, 16)
    condS = k.at(WB + 1216, 16)
    xin = [k.at(BIG + j * D, D) for j in range(2)]
    NS = 4
    slab = [k.tiles(BIG + 2048 + j * KT * 512, KT, 512) for j in range(NS)]
    ones_set, params_in, cond_in = k.sem("ones_set"), k.sem("params_in"), k.sem("cond_in")
    x_in = [k.sem(f"x_in{j}") for j in range(2)]
    stg_zero = k.sem("staging_zeroed")
    par_t, par_c = k.sem("params_turned"), k.sem("params_copied")
    cond_s = k.sem("cond_silu")
    x_turned, x_copied = k.sem("x_turned"), k.sem("x_copied")
    slab_in = [k.sem(f"ada_slab_in{j}") for j in range(NS)]
    mod_ready, mod_done = k.sem("mod_ready"), k.sem("mod_done")
    ada = A["ada_w"].rearrange("l (k p) n -> p l k n", p=128)
    NSL = 6 * D // 512
    row_loads = [("ada_b", A["ada_b"].rearrange("l (m p) -> (l m) p", p=128), 96),
                 ("norm1", A["norm1_g"].rearrange("l (m p) -> (l m) p", p=128), 16),
                 ("norm2", A["norm2_g"].rearrange("l (m p) -> (l m) p", p=128), 16),
                 ("final", A["final_g"].rearrange("(m p) -> m p", p=128), 8),
                 ("mu", A["rwkv_mu"].rearrange("l d (m p) -> (l d m) p", p=128), 28),
                 ("w0", A["rwkv_w0"].rearrange("l d (m p) -> (l d m) p", p=128), 8),
                 ("a0", A["rwkv_a0"].rearrange("l d (m p) -> (l d m) p", p=128), 8),
                 ("k_k", A["rwkv_k_k"].rearrange("l (m p) -> (l m) p", p=128), 4),
                 ("k_a", A["rwkv_k_a"].rearrange("l (m p) -> (l m) p", p=128), 4),
                 ("r_k", A["rwkv_r_k"].rearrange("l (m h) p -> (l m) (h p)", h=2), 4),
                 ("ln_g", A["rwkv_ln_g"].rearrange("l (m p) -> (l m) p", p=128), 4),
                 ("ln_b", A["rwkv_ln_b"].rearrange("l (m p) -> (l m) p", p=128), 4),
                 ("b_in", A["hy_b_in"].rearrange("l (m p) -> (l m) p", p=128), 24),
                 ("conv_w", A["hy_conv_w"].rearrange("l j (m p) -> (l j m) p", p=128), 72),
                 ("conv_b", A["hy_conv_b"].rearrange("l (m p) -> (l m) p", p=128), 24),
                 ("hbias", A["hy_bias"].rearrange("l o (m p) -> (l o m) p", p=128), 16),
                 ("b_out", A["hy_b_out"].rearrange("l (m p) -> (l m) p", p=128), 8)]
    plan = []
    for name, src, n in row_loads:
        r, done = COL[name], 0
        while done < n:
            m = min(n - done, 128 - (r + done) % 128)
            plan.append(((r + done) // 128, (r + done) % 128, m, src[done:done + m, :]))
            done += m
    sub = COL["subln"]
    plan.append((sub // 128, sub % 128, 1, None))

    with nc.Block() as block:
        @block.sync
        def _(sp):
            sp.dma_start(k.at(CST, CW), consts["cblk"]).then_inc(params_in, 16)
            sp.wait_ge(stg_zero, 1)
            for t, r, m, src in plan:
                if src is None:
                    for h in range(2):
                        sp.dma_start(stg[r:r + 1, t, h * DV:(h + 1) * DV], A["diff_subln_g"]).then_inc(params_in, 16)
                else:
                    sp.dma_start(stg[r:r + m, t, :], src).then_inc(params_in, 16)
            sp.dma_start(cond[0:8, :], A["c_ctx"].rearrange("(m p) -> m p", p=128)).then_inc(cond_in, 16)
            sp.dma_start(cond[8:16, :], A["c"].rearrange("b (m p) -> (b m) p", p=128)).then_inc(cond_in, 16)
            for t in range(9):
                if t >= 2:
                    sp.wait_ge(x_turned, 2 * (t - 1))
                src = A["x_prompt"][0] if t == 0 else A["x_sample"][0, (t - 1) * 128:t * 128, :]
                sp.dma_start(xin[t % 2], src).then_inc(x_in[t % 2], 16)

        n_loads = 1 + len(plan) + 1

        @block.gpsimd
        def _(pool):
            for s in range(2 * NSL):
                if s >= NS:
                    pool.wait_ge(mod_ready, 4 * (s - NS + 1))
                pool.dma_start(slab[s % NS], ada[:, s // NSL, :, (s % NSL) * 512:(s % NSL + 1) * 512]).then_inc(slab_in[s % NS], 16)

        @block.tensor
        def _(pe):
            pe.wait_ge(params_in, 16 * n_loads)
            pe.wait_ge(cond_in, 32)
            for t in range(PV_TILES):
                last = pe.transpose(k.bank(0)[:, t * 128:(t + 1) * 128], stg[:, t, :], k.ident)
            last = pe.transpose(k.bank(1)[:, 0:16], cond[0:16, :], k.ident[0:16, 0:16])
            last.then_inc(par_t, 1)
            for t in range(9):
                pe.wait_ge(x_in[t % 2], 16 * (t // 2 + 1))
                for h in range(2):
                    b = (2 * t + h) % 4
                    if 2 * t + h >= 4:
                        pe.wait_ge(x_copied, 2 * t + h - 3)
                    for q in range(4):
                        kt = 4 * h + q
                        last = pe.transpose(k.bank(2 + b)[:, q * 128:(q + 1) * 128], xin[t % 2][:, kt * 128:(kt + 1) * 128], k.ident)
                    last.then_inc(x_turned, 1)
            pe.wait_ge(cond_s, 2)
            for s in range(2 * NSL):
                pe.wait_ge(slab_in[s % NS], 16 * (s // NS + 1))
                for m in range(4):
                    n = 4 * s + m
                    for kt in range(KT):
                        last = pe.matmul(k.bank(6)[:, 2 * n:2 * n + 2], slab[s % NS][:, kt, m * 128:(m + 1) * 128],
                                         condS[:, kt:kt + 9:8], start=(kt == 0), stop=(kt == KT - 1))
                    last.then_inc(mod_ready, 1)

        @block.scalar
        def _(act):
            act.wait_ge(par_t, 1)
            act.activation(condT[:, 0:16], k.bank(1)[:, 0:16], ACT.Sigmoid).then_inc(cond_s, 1)

        @block.vector
        def _(dve):
            dve.memset(stg[:, PV_TILES - 1, :], 0.0).then_inc(stg_zero, 1)
            dve.memset(k.ones, 1.0)
            dve.wait_ge(par_t, 1)
            dve.tensor_copy(k.pv, k.bank(0)[:, 0:128 * PV_TILES])
            dve.wait_ge(cond_s, 1)
            dve.tensor_tensor(condS, k.bank(1)[:, 0:16], condT, ALU.mult).then_inc(cond_s, 1)
            for t in range(9):
                for h in range(2):
                    n = 2 * t + h
                    dve.wait_ge(x_turned, n + 1)
                    dve.tensor_copy(k.X[:, 4 * h:4 * h + 4, t * 128:(t + 1) * 128],
                                    k.bank(2 + n % 4).rearrange("p (q n) -> p q n", q=4)).then_inc(x_copied, 1)
            dve.wait_ge(mod_ready, 8 * NSL)
            bias = k.col("ada_b", 0, 96).rearrange("p (l m) -> p l m", l=2)
            for g in range(2):
                dve.tensor_tensor(k.mod[:, :, :, g], k.bank(6)[:, 0:192].rearrange("p (l m g) -> p l m g", l=2, g=2)[:, :, :, g],
                                  bias, ALU.add)


def stage_norm(k, gain, layer, sub, dst, tag):
    nc = k.nc
    sq = k.tiles(BIG, 2, T)
    root, rstd = k.at(BIG + 2 * T, T), k.at(BIG + 3 * T, T)
    coef = k.at(COEF0, 16).rearrange("p (m g) -> p m g", g=2)
    sq_ready, sq_used = k.sem(f"{tag}_squares"), k.sem(f"{tag}_squares_summed")
    rooted, rstd_ready, scaled = k.sem(f"{tag}_root"), k.sem(f"{tag}_rstd"), k.sem(f"{tag}_scaled")
    eps = k.at(SM0 + 1, 1)
    eps_set = k.sem(f"{tag}_eps")
    coef_set = k.sem(f"{tag}_coef")
    with nc.Block() as block:
        @block.tensor
        def _(pe):
            for kt in range(KT):
                pe.wait_ge(sq_ready, kt + 1)
                for tc in range(3):
                    last = pe.matmul(k.bank(tc, TC), k.ones, sq[:, kt % 2, tc * TC:(tc + 1) * TC],
                                     start=(kt == 0), stop=(kt == KT - 1))
                last.then_inc(sq_used, 1)

        @block.scalar
        def _(act):
            for kt in range(KT):
                if kt >= 2:
                    act.wait_ge(sq_used, kt - 1)
                act.activation(sq[:, kt % 2, :], k.X[:, kt, :], ACT.Square).then_inc(sq_ready, 1)
            act.wait_ge(sq_used, KT)
            act.wait_ge(eps_set, 1)
            for tc in range(3):
                act.activation(root[:, tc * TC:(tc + 1) * TC], k.bank(tc, TC), ACT.Sqrt, bias=eps, scale=1.0 / D).then_inc(rooted, 1)
            act.wait_ge(coef_set, 2)
            for kt in range(KT):
                act.wait_ge(scaled, kt + 1)
                for g, (c0, n) in enumerate(GROUPS):
                    v = dst[:, kt, c0:c0 + n]
                    if layer is None:
                        act.activation(v, v, ACT.Identity, scale=coef[:, kt, g:g + 1])
                    else:
                        act.activation(v, v, ACT.Identity, scale=coef[:, kt, g:g + 1],
                                       bias=k.mod[:, layer, 24 * sub + kt, g:g + 1])

        @block.vector
        def _(dve):
            dve.memset(eps, 1e-6).then_inc(eps_set, 1)
            for g in range(2):
                if layer is None:
                    dve.tensor_copy(coef[:, :, g], gain).then_inc(coef_set, 1)
                else:
                    dve.scalar_tensor_tensor(out=coef[:, :, g], in0=k.mod[:, layer, 24 * sub + 8:24 * sub + 16, g],
                                             scalar=1.0, in1=gain, op0=ALU.add, op1=ALU.mult).then_inc(coef_set, 1)
            for tc in range(3):
                dve.wait_ge(rooted, tc + 1)
                dve.reciprocal(rstd[:, tc * TC:(tc + 1) * TC], root[:, tc * TC:(tc + 1) * TC]).then_inc(rstd_ready, 1)
            dve.wait_ge(rstd_ready, 3)
            for kt in range(KT):
                dve.tensor_tensor(dst[:, kt, :], k.X[:, kt, :], rstd, ALU.mult).then_inc(scaled, 1)


def stage_gemm(k, tag, src, n_k, wview, tiles, slab_at, evac, store=None, after=None):
    nc = k.nc
    slab = [k.tiles(slab_at + j * n_k * 128, n_k, 128) for j in range(2)]
    slab_in = [k.sem(f"{tag}_slab_in{j}") for j in range(2)]
    acc_ready, acc_free = k.sem(f"{tag}_acc_ready"), k.sem(f"{tag}_acc_free")
    stored = [k.sem(f"{tag}_stored{j}") for j in range(2)] if store else None
    row_ready = k.sem(f"{tag}_row_ready") if after else None
    n = tiles // 2
    with nc.Block() as block:
        @block.sync
        def _(sp):
            for j in range(2):
                sp.dma_start(slab[j], wview[:, :, j * 128:(j + 1) * 128]).then_inc(slab_in[j], 16)
            with sp.Fori(1, n) as i:
                for j in range(2):
                    off = sp.snap((i * 2 + j) * 128)
                    used = sp.snap((i * 2 + (j - 1)) * 3)
                    sp.wait_ge(acc_ready, used)
                    sp.dma_start(slab[j], wview[:, :, ds(off, 128)]).then_inc(slab_in[j], 16)

        @block.tensor
        def _(pe):
            with pe.Fori(0, n) as i:
                for j in range(2):
                    pe.wait_ge(slab_in[j], (i + 1) * 16)
                    for tc in range(3):
                        pe.wait_ge(acc_free, i * 6 + (j * 3 + tc + 1))
                        for kt in range(n_k):
                            last = pe.matmul(k.bank(tc, TC), slab[j][:, kt, :], src(kt)[:, tc * TC:(tc + 1) * TC],
                                             start=(kt == 0), stop=(kt == n_k - 1))
                        last.then_inc(acc_ready, 1)

        @block.vector
        def _(dve):
            dve.sem_inc(acc_free, 3)
            with dve.Fori(0, n) as i:
                for j in range(2):
                    for tc in range(3):
                        if store and not after and tc == 0:
                            dve.wait_ge(stored[j], i * 16 + 16)
                        dve.wait_ge(acc_ready, i * 6 + (j * 3 + tc + 1))
                        evac(dve, i * 2 + j, j, tc, k.bank(tc, TC)).then_inc(acc_free, 1)
                    if after:
                        dve.drain()
                        dve.wait_ge(stored[j], i * 16 + 16)
                        after(dve, i * 2 + j, j).then_inc(row_ready, 1)

        if store:
            @block.scalar
            def _(act):
                for j in range(2):
                    act.sem_inc(stored[j], 16)
                with act.Fori(0, n) as i:
                    for j in range(2):
                        dst, row = store(act, i * 2 + j, j)
                        if after:
                            done = act.snap(i * 2 + (j + 1))
                            act.wait_ge(row_ready, done)
                        else:
                            done = act.snap(i * 6 + (j * 3 + 6))
                            act.wait_ge(acc_free, done)
                        act.dma_start(dst, row).then_inc(stored[j], 16)
                for j in range(2):
                    act.wait_ge(stored[j], 16 * (n + 1))


def evac_residual(k, layer, sub, bias=None):
    def evac(dve, m, j, tc, acc):
        first = tc * TC
        spans = [(0, 0, NP_), (1, NP_, TC - NP_)] if tc == 0 else [(1, 0, TC)]
        for g, c0, n in spans:
            x = k.X[:, m, first + c0:first + c0 + n]
            gate = k.mod[:, layer, 24 * sub + 16 + m, g:g + 1]
            if bias is None:
                last = dve.scalar_tensor_tensor(out=x, in0=acc[:, c0:c0 + n], scalar=gate, in1=x, op0=ALU.mult, op1=ALU.add)
            else:
                tmp = k.at(WB + 2048 + 512 * (tc if g else 3), n)
                dve.tensor_scalar(tmp, acc[:, c0:c0 + n], k.pv[:, ds(m + bias, 1)], gate, ALU.add, ALU.mult)
                dve.drain()
                last = dve.tensor_tensor(x, tmp, x, ALU.add)
        return last
    return evac


def stage_ffn(k, A, layer):
    nc = k.nc
    tag = f"ffn{layer}"
    act_t = k.tiles(BIG, FT, T)
    slab = {(w, j): k.tiles(WB + (2 * w + j) * 1024, KT, 128) for w in range(2) for j in range(2)}
    views = [A["ffn_w1"][layer].rearrange("(k p) n -> p k n", p=128), A["ffn_w3"][layer].rearrange("(k p) n -> p k n", p=128)]
    slab_in = {(w, j): k.sem(f"{tag}_w{2 * w + 1}_in{j}") for w in range(2) for j in range(2)}
    acc_ready, silu_ready, acc_free = k.sem(f"{tag}_acc_ready"), k.sem(f"{tag}_silu_ready"), k.sem(f"{tag}_acc_free")
    n = FT // 2
    with nc.Block() as block:
        @block.sync
        def _(sp):
            for j in range(2):
                for w in range(2):
                    sp.dma_start(slab[w, j], views[w][:, :, j * 128:(j + 1) * 128]).then_inc(slab_in[w, j], 16)
            with sp.Fori(1, n) as i:
                for j in range(2):
                    off = sp.snap((i * 2 + j) * 128)
                    used = sp.snap((i * 2 + (j - 1)) * 3)
                    sp.wait_ge(acc_ready, used)
                    for w in range(2):
                        sp.dma_start(slab[w, j], views[w][:, :, ds(off, 128)]).then_inc(slab_in[w, j], 16)

        @block.tensor
        def _(pe):
            with pe.Fori(0, n) as i:
                for j in range(2):
                    for w in range(2):
                        pe.wait_ge(slab_in[w, j], (i + 1) * 16)
                    for tc in range(3):
                        pe.wait_ge(acc_free, i * 6 + (j * 3 + tc + 1))
                        for w in range(2):
                            for kt in range(KT):
                                last = pe.matmul(k.bank(3 * w + tc, TC), slab[w, j][:, kt, :], k.H[:, kt, tc * TC:(tc + 1) * TC],
                                                 start=(kt == 0), stop=(kt == KT - 1))
                        last.then_inc(acc_ready, 1)

        @block.scalar
        def _(act):
            with act.Fori(0, n) as i:
                for j in range(2):
                    for tc in range(3):
                        act.wait_ge(acc_ready, i * 6 + (j * 3 + tc + 1))
                        act.activation(act_t[:, i * 2 + j, tc * TC:(tc + 1) * TC], k.bank(tc, TC), ACT.Silu).then_inc(silu_ready, 1)

        @block.vector
        def _(dve):
            dve.sem_inc(acc_free, 3)
            with dve.Fori(0, n) as i:
                for j in range(2):
                    for tc in range(3):
                        dve.wait_ge(silu_ready, i * 6 + (j * 3 + tc + 1))
                        v = act_t[:, i * 2 + j, tc * TC:(tc + 1) * TC]
                        dve.tensor_tensor(v, k.bank(3 + tc, TC), v, ALU.mult).then_inc(acc_free, 1)

    stage_gemm(k, tag + "_down", lambda kt: act_t[:, kt, :], FT, A["ffn_w2"][layer].rearrange("(k p) n -> p k n", p=128),
               KT, H0, evac_residual(k, layer, 1))


def stage_out(k, A, Y, rows=None):
    nc = k.nc
    row = [k.at(BIG + 4 * T + j * D, D) for j in range(2)]
    turned, copied = k.sem("y_turned"), k.sem("y_copied")
    stored = [k.sem(f"y_stored{j}") for j in range(2)]
    with nc.Block() as block:
        @block.tensor
        def _(pe):
            for n in range(18):
                if n >= 4:
                    pe.wait_ge(copied, n - 3)
                for q in range(4):
                    last = pe.transpose(k.bank(n % 4)[:, q * 128:(q + 1) * 128], k.H[:, 4 * (n % 2) + q, (n // 2) * 128:(n // 2 + 1) * 128], k.ident)
                last.then_inc(turned, 1)

        @block.vector
        def _(dve):
            for n in range(18):
                t = n // 2
                dve.wait_ge(turned, n + 1)
                if t >= 2 and n % 2 == 0:
                    dve.wait_ge(stored[t % 2], 16 * (t // 2))
                dve.tensor_copy(row[t % 2][:, (n % 2) * 512:(n % 2 + 1) * 512], k.bank(n % 4)).then_inc(copied, 1)

        @block.sync
        def _(sp):
            for t in range(9):
                sp.wait_ge(copied, 2 * t + 2)
                dst = Y["y_prompt"][0] if t == 0 else Y["y_sample"][0, (t - 1) * 128:t * 128, :]
                sp.dma_start(dst, row[t % 2]).then_inc(stored[t % 2], 16)
            for j in range(2):
                sp.wait_ge(stored[j], 16 * (5 - j))

QK0, KC0, V0, RW0 = BIG, BIG + 9216, BIG + 14336, BIG + 19968
OA0 = BIG + 19968
PKT = (PAST + NL) // 128


def stage_project(k, A, Y, scratch):
    nc = k.nc
    w = A["ab_w_in"][0].rearrange("(k p) n -> p k n", p=128)
    qk = k.tiles(QK0, 8, T)
    stage_gemm(k, "qk", lambda kt: k.H[:, kt, :], KT, w[:, :, 0:1024], 8, WB,
               lambda dve, m, j, tc, acc: dve.tensor_copy(qk[:, m, tc * TC:(tc + 1) * TC], acc))
    ring = k.tiles(RW0, 2, T)
    rw_d = scratch["rw_d"]
    stage_gemm(k, "rw", lambda kt: k.H[:, kt, :], KT, w[:, :, 1536:AB_IN], RW_TILES, WB,
               lambda dve, m, j, tc, acc: dve.tensor_copy(ring[:, j, tc * TC:(tc + 1) * TC], acc),
               store=lambda act, m, j: (rw_d[ds(m, 1), :, :].rearrange("m p t -> (m p) t"), ring[:, j, :]))
    wv = k.tiles(KC0, KT, 512)
    v = k.tiles(V0, PKT + 1, 512)
    wv_in, v_ready, v_copied = k.sem("wv_in"), k.sem("v_ready"), k.sem("v_copied")
    ctx_v_in, newv = k.sem("ctx_v_in"), k.sem("new_v_stored")
    with nc.Block() as block:
        @block.sync
        def _(sp):
            sp.dma_start(wv, w[:, :, 1024:1536]).then_inc(wv_in, 16)
            for t in range(PAST // 128):
                sp.dma_start(v[:, t, :].rearrange("p (h d) -> p h d", h=HEADS),
                             A["cache_diff_v"][0, 0, :, t * 128:(t + 1) * 128, :].rearrange("h p d -> p h d")).then_inc(ctx_v_in, 16)
            sp.wait_ge(v_copied, 1)
            sp.dma_start(Y["new_v"][0, 0].rearrange("h p d -> p h d"),
                         v[:, PKT, :].rearrange("p (h d) -> p h d", h=HEADS)).then_inc(newv, 16)
            sp.wait_ge(newv, 16)
            sp.wait_ge(ctx_v_in, 32)

        @block.tensor
        def _(pe):
            pe.wait_ge(wv_in, 16)
            for t in range(9):
                if t >= 2:
                    pe.wait_ge(v_copied, t - 1)
                for kt in range(KT):
                    last = pe.matmul(k.bank(t % 2), k.H[:, kt, t * 128:(t + 1) * 128], wv[:, kt, :],
                                     start=(kt == 0), stop=(kt == KT - 1))
                last.then_inc(v_ready, 1)

        @block.vector
        def _(dve):
            for t in range(9):
                dve.wait_ge(v_ready, t + 1)
                at = PKT if t == 0 else PAST // 128 + t - 1
                dve.tensor_copy(v[:, at, :], k.bank(t % 2)).then_inc(v_copied, 1)


def stage_keys(k, A, Y, consts):
    nc = k.nc
    qk, kc = k.tiles(QK0, 8, T), k.tiles(KC0, 4, PAST + NL)
    cos, sin = k.at(H0, NL), k.at(H0 + NL, NL)
    cosp = [k.at(H0 + 2 * NL + j * 512, 512) for j in range(2)]
    sinp = [k.at(H0 + 3 * NL + j * 512, 512) for j in range(2)]
    rows = k.tiles(H0 + 4 * NL, 2, 512)
    newk = k.at(H0 + 5 * NL, 512)
    lam_row, lam_p = k.at(H0 + 6 * NL, 128), k.at(H0 + 6 * NL + 128, 64)
    nlam = k.at(SM0, 1)
    lam_e, lam_s = k.at(SM0 + 2, 2), k.at(SM0 + 4, 2)
    tab_in, row_in, lam_in = k.sem("rope_in"), k.sem("key_rows_in"), k.sem("lambda_in")
    turned, copied = k.sem("keys_turned"), k.sem("keys_copied")
    rot_ready, cos_ready, roped = k.sem("rot_ready"), k.sem("cos_ready"), k.sem("roped")
    sin_ready = k.sem("sin_ready")
    lam_bc, lam_dot, lam_exp = k.sem("lambda_rows"), k.sem("lambda_dot"), k.sem("lambda_exp")
    nk_out = k.sem("new_k_stored")
    units = [(m, h) for m in range(8) for h in range(2)]
    with nc.Block() as block:
        @block.sync
        def _(sp):
            sp.dma_start(cos, consts["rope"][0]).then_inc(tab_in, 16)
            sp.dma_start(sin, consts["rope"][1]).then_inc(tab_in, 16)
            for t in range(2):
                sp.dma_start(rows[:, t, :].rearrange("p (g d) -> p g d", g=16),
                             A["cache_diff_k"][0, 0, :, :, t * 128:(t + 1) * 128, :].rearrange("h m p d -> p (h m) d")).then_inc(row_in, 16)
            sp.dma_start(lam_row[0:1, :], A["diff_lambda"].rearrange("l a b -> l (a b)")).then_inc(lam_in, 16)
            sp.wait_ge(copied, 3)
            sp.dma_start(Y["new_k"][0, 0].rearrange("h m p d -> p (h m) d"), newk.rearrange("p (g d) -> p g d", g=16)).then_inc(nk_out, 16)
            sp.wait_ge(nk_out, 16)

        @block.tensor
        def _(pe):
            pe.wait_ge(row_in, 32)
            for t in range(2):
                for q in range(4):
                    last = pe.transpose(k.bank(t)[:, q * 128:(q + 1) * 128], rows[:, t, q * 128:(q + 1) * 128], k.ident)
                last.then_inc(turned, 1)
            for q in range(4):
                last = pe.transpose(k.bank(2)[:, q * 128:(q + 1) * 128], qk[:, 4 + q, 0:NP_], k.ident)
            last.then_inc(turned, 1)
            pe.wait_ge(lam_in, 16)
            pe.matmul(k.bank(3)[:, 0:128], k.ones[0:1, :], lam_row[0:1, :], start=True, stop=True).then_inc(lam_bc, 1)
            for n, (m, h) in enumerate(units):
                if n >= 2:
                    pe.wait_ge(sin_ready, n - 1)
                pe.matmul(k.bank(4 + n % 2), k.const("rot"), qk[:, m, NP_ + 512 * h:NP_ + 512 * (h + 1)],
                          start=True, stop=True).then_inc(rot_ready, 1)

        @block.gpsimd
        def _(pool):
            pool.wait_ge(tab_in, 32)
            for n, (m, h) in enumerate(units):
                if n >= 2:
                    pool.wait_ge(roped, n - 1)
                pool.tensor_tensor(cosp[n % 2], qk[:, m, NP_ + 512 * h:NP_ + 512 * (h + 1)], cos[:, 512 * h:512 * (h + 1)],
                                   ALU.mult).then_inc(cos_ready, 1)

        @block.scalar
        def _(act):
            act.wait_ge(lam_dot, 2)
            act.activation(lam_e, lam_s, ACT.Exp).then_inc(lam_exp, 1)

        @block.vector
        def _(dve):
            for t in range(2):
                dve.wait_ge(turned, t + 1)
                dve.tensor_copy(kc[:, :, t * 128:(t + 1) * 128], k.bank(t).rearrange("p (q n) -> p q n", q=4)).then_inc(copied, 1)
            dve.wait_ge(turned, 3)
            dve.tensor_copy(newk, k.bank(2)).then_inc(copied, 1)
            dve.wait_ge(lam_bc, 1)
            dve.tensor_copy(lam_row, k.bank(3)[:, 0:128])
            dve.drain()
            lv = lam_row.rearrange("p (a b c) -> p a b c", a=2, b=2)
            dve.tensor_tensor(lam_p.rearrange("p (a c) -> p a c", a=2), lv[:, :, 0, :], lv[:, :, 1, :], ALU.mult).then_inc(lam_dot, 1)
            dve.wait_ge(lam_dot, 1)
            dve.tensor_reduce(lam_s, lam_p.rearrange("p (a c) -> p a c", a=2), AX.X, ALU.add).then_inc(lam_dot, 1)
            dve.wait_ge(lam_exp, 1)
            dve.tensor_scalar(nlam, lam_e[:, 1:2], lam_e[:, 0:1], -LAM_INIT, ALU.subtract, ALU.add)
            dve.wait_ge(tab_in, 32)
            for n, (m, h) in enumerate(units):
                dve.wait_ge(rot_ready, n + 1)
                dve.tensor_tensor(sinp[n % 2], k.bank(4 + n % 2), sin[:, 512 * h:512 * (h + 1)], ALU.mult).then_inc(sin_ready, 1)
                dve.wait_ge(sin_ready, n + 1)
                dve.wait_ge(cos_ready, n + 1)
                dst = qk[:, m, NP_ + 512 * h:NP_ + 512 * (h + 1)] if m < 4 else kc[:, m - 4, PAST + 512 * h:PAST + 512 * (h + 1)]
                dve.tensor_tensor(dst, sinp[n % 2], cosp[n % 2], ALU.add).then_inc(roped, 1)


def stage_attend(k, latent):
    nc = k.nc
    tag = "lat" if latent else "ctx"
    qk, kc, v = k.tiles(QK0, 8, T), k.tiles(KC0, 4, PAST + NL), k.tiles(V0, PKT + 1, 512)
    oa = k.tiles(OA0, 4, T)
    steps, nkt, vt0, q0 = (NL // 128, PKT, 0, NP_) if latent else (1, 1, PKT, 0)
    nk = nkt * 128
    spans = [(c, min(512, nk - c)) for c in range(0, nk, 512)]
    groups = [range(g, min(g + 4, nkt)) for g in range(0, nkt, 4)]
    NG = len(groups)
    prob = [[k.at(H0 + (2 * b + m) * 1280, nk) for m in range(2)] for b in range(2)]
    pt = [k.tiles(H0 + 5120 + b * 1280, nkt, 128) for b in range(2)]
    qs = k.tiles(H0 + 7680, 4, 128)
    st = k.at(SM0 + 8, 16)
    nmax, rsum, rcp = st[:, 0:4], st[:, 4:8], st[:, 8:12]
    nlam = k.at(SM0, 1)
    S = lambda name: k.sem(f"{tag}_{name}")
    qs_ready, score_ready, max_ready, exp_done = S("q_scaled"), S("scores"), S("max"), S("exp")
    p_ready, turned, pt_copied, pv_ready, oa_done = S("probs"), S("turned"), S("turned_copied"), S("pv"), S("out_copied")

    def keys(h, m, c, n):
        b = 32 * (2 * (h % 2) + m)
        src = kc[b:b + 32, h // 2, c:c + n] if latent else qk[b:b + 32, 4 + h // 2, c:c + n]
        return qs[b:b + 32, h // 2, :], src

    with nc.Block() as block:
        @block.tensor
        def _(pe):
            def turn_and_weigh(i, h):
                pe.wait_ge(p_ready, i * 8 + (h + 1))

                def weigh(g):
                    pe.wait_ge(pt_copied, i * 8 * NG + (h * NG + g + 1 + 1))
                    if h == 0 and g == 0:
                        pe.wait_ge(oa_done, i + 1)
                    for kt in groups[g]:
                        last = pe.matmul(k.bank(7)[64 * (h % 2):64 * (h % 2) + 64, (h // 2) * 128:(h // 2 + 1) * 128],
                                         v[:, vt0 + kt, h * DV:(h + 1) * DV], pt[h % 2][:, kt, :],
                                         start=(kt == 0), stop=(kt == nkt - 1))
                    return last
                for g, tiles in enumerate(groups):
                    pe.wait_ge(pt_copied, i * 8 * NG + (h * NG + g + 1))
                    for n, kt in enumerate(tiles):
                        last = pe.transpose(k.bank(6)[:, n * 128:(n + 1) * 128], prob[h % 2][0][:, kt * 128:(kt + 1) * 128], k.ident)
                    last.then_inc(turned, 1)
                    if g:
                        weigh(g - 1)
                last = weigh(NG - 1)
                if h == HEADS - 1:
                    last.then_inc(pv_ready, 1)

            with trip(pe, steps) as i:
                pe.wait_ge(qs_ready, i + 1)
                for h in range(HEADS):
                    for m in range(2):
                        pe.wait_ge(exp_done, i * 16 + (2 * h + m + 1))
                        for c, n in spans:
                            last = pe.matmul(k.psum[:, 1536 * m + c:1536 * m + c + n], *keys(h, m, c, n), start=True, stop=True)
                        last.then_inc(score_ready, 1)
                    if h:
                        turn_and_weigh(i, h - 1)
                turn_and_weigh(i, HEADS - 1)

        @block.scalar
        def _(act):
            act.sem_inc(exp_done, 2)
            act.sem_inc(pt_copied, 1)
            act.sem_inc(oa_done, 1)

            def copies(i, h):
                for g, tiles in enumerate(groups):
                    act.wait_ge(turned, i * 8 * NG + (h * NG + g + 1))
                    n = len(tiles)
                    act.activation(pt[h % 2][:, tiles[0]:tiles[0] + n, :],
                                   k.bank(6)[:, 0:n * 128].rearrange("p (n q) -> p n q", n=n), ACT.Copy).then_inc(pt_copied, 1)

            with trip(act, steps) as i:
                q = qk[:, 0:4, ds(i * 128 + q0, 128)] if latent else qk[:, 0:4, 0:128]
                act.activation(qs, q, ACT.Copy, scale=DQ ** -0.5).then_inc(qs_ready, 1)
                for h in range(HEADS):
                    for m in range(2):
                        act.wait_ge(max_ready, i * 16 + (2 * h + m + 1))
                        act.activation(prob[h % 2][m], k.psum[:, 1536 * m:1536 * m + nk], ACT.Exp,
                                       bias=nmax[:, 2 * (h % 2) + m:2 * (h % 2) + m + 1],
                                       accum_out=rsum[:, 2 * (h % 2) + m:2 * (h % 2) + m + 1]).then_inc(exp_done, 1)
                    if h:
                        copies(i, h - 1)
                copies(i, HEADS - 1)
                act.wait_ge(pv_ready, i + 1)
                dst = oa[:, :, ds(i * 128 + q0, 128)] if latent else oa[:, :, 0:128]
                act.activation(dst, k.bank(7).rearrange("p (t n) -> p t n", t=4), ACT.Copy).then_inc(oa_done, 1)

        @block.vector
        def _(dve):
            with trip(dve, steps) as i:
                for h in range(HEADS):
                    b = 2 * (h % 2)
                    for m in range(2):
                        dve.wait_ge(score_ready, i * 16 + (2 * h + m + 1))
                        dve.tensor_reduce(nmax[:, b + m:b + m + 1], k.psum[:, 1536 * m:1536 * m + nk], AX.X, ALU.max,
                                          negate=True).then_inc(max_ready, 1)
                    dve.wait_ge(exp_done, i * 16 + (2 * h + 4))
                    dve.reciprocal(rcp[:, b:b + 2], rsum[:, b:b + 2])
                    dve.drain()
                    dve.tensor_scalar(rcp[:, b + 1:b + 2], rcp[:, b + 1:b + 2], nlam, None, ALU.mult)
                    dve.tensor_scalar(prob[h % 2][0], prob[h % 2][0], rcp[:, b:b + 1], None, ALU.mult)
                    dve.drain()
                    dve.scalar_tensor_tensor(out=prob[h % 2][0], in0=prob[h % 2][1], scalar=rcp[:, b + 1:b + 2],
                                             in1=prob[h % 2][0], op0=ALU.mult, op1=ALU.add).then_inc(p_ready, 1)


def stage_head_norm(k):
    nc = k.nc
    oa = k.tiles(OA0, 4, T)
    sq, root, rcp = k.tiles(H0, 4, T), k.at(H0 + 4 * T, T), k.at(H0 + 5 * T, T)
    eps, gain = k.at(SM0 + 1, 1), k.at(SM0 + 6, 1)
    sq_ready, sum_ready, rooted, inv = k.sem("hn_squares"), k.sem("hn_sums"), k.sem("hn_root"), k.sem("hn_inverse")
    eps_set, normed = k.sem("hn_eps"), k.sem("hn_normed")
    with nc.Block() as block:
        @block.scalar
        def _(act):
            for t in range(4):
                act.activation(sq[:, t, :], oa[:, t, :], ACT.Square).then_inc(sq_ready, 1)
            act.wait_ge(eps_set, 2)
            for t in range(4):
                act.wait_ge(sum_ready, t + 1)
                if t:
                    act.wait_ge(inv, t)
                for tc in range(3):
                    last = act.activation(root[:, tc * TC:(tc + 1) * TC], k.bank(3 * (t % 2) + tc, TC), ACT.Sqrt, bias=eps, scale=1.0 / DV)
                last.then_inc(rooted, 1)

        @block.tensor
        def _(pe):
            for t in range(4):
                pe.wait_ge(sq_ready, t + 1)
                if t >= 2:
                    pe.wait_ge(rooted, t - 1)
                for tc in range(3):
                    last = pe.matmul(k.bank(3 * (t % 2) + tc, TC), k.const("blockones"), sq[:, t, tc * TC:(tc + 1) * TC], start=True, stop=True)
                last.then_inc(sum_ready, 1)

        @block.vector
        def _(dve):
            dve.memset(eps, 1e-5).then_inc(eps_set, 1)
            dve.tensor_scalar(gain, k.col("subln"), 1.0 - LAM_INIT, None, ALU.mult).then_inc(eps_set, 1)
            dve.wait_ge(eps_set, 2)
            for t in range(4):
                dve.wait_ge(rooted, t + 1)
                if t:
                    dve.wait_ge(normed, t)
                dve.reciprocal(rcp, root).then_inc(inv, 1)
                dve.wait_ge(inv, t + 1)
                dve.scalar_tensor_tensor(out=oa[:, t, :], in0=oa[:, t, :], scalar=gain, in1=rcp,
                                         op0=ALU.mult, op1=ALU.mult).then_inc(normed, 1)




RS0, KK0, YA0, Z1, Z2 = 0, 16128, 20736, 25344, 43008
U = 8
DECAY = -math.exp(-0.5)


class Steps:

    def __init__(self, sem, names):
        self.sem, self.names, self.per = sem, list(names), len(names)

    def start(self, eng):
        eng.sem_inc(self.sem, self.per)

    def here(self, i, name):
        return i * self.per + (self.per + self.names.index(name) + 1)

    def before(self, i, name):
        return i * self.per + (self.names.index(name) + 1)


def rwkv_bufs(k):
    b, at = {}, Z1
    for name, n in [("sw", 512), ("sa", 512), ("L", 512), ("Lx", 512), ("e1", 512), ("e0", 512), ("ei", 512),
                    ("kd", 512), ("bon", 512), ("bkt", 1024), ("uv", 1024), ("g", 2048), ("m", 512), ("xm", 1024),
                    ("tmp", 512), ("tmp2", 512), ("st", 1024), ("vc", 512), ("lc", 128)]:
        b[name] = k.at(at, n)
        at += n
    assert at <= OA0
    at = Z2
    for name, n in [("wu", 1024), ("ar", 1024), ("bk", 1024), ("w1", 512), ("s", 512)]:
        b[name] = k.at(at, n)
        at += n
    assert at <= CST
    return b


def stage_rwkv_pre(k, A, scratch):
    nc = k.nc
    rs, kk, ya = k.tiles(RS0, RW_TILES, T), k.tiles(KK0, 4, T), k.tiles(YA0, 4, T)
    raw = k.tiles(Z1, 2, T)
    c0 = k.at(Z1 + 2 * T, RW_TILES)
    sq, root = k.tiles(Z1 + 3 * T, 2, T), k.tiles(Z1 + 5 * T, 2, T)
    b = rwkv_bufs(k)
    wu = b["wu"].rearrange("p (d n) -> p d n", d=2)
    rk = k.at(RK0, 512).rearrange("p (m n) -> p m n", m=4)
    spilled, raw_in, wu_in = k.sem("x_spilled"), [k.sem(f"raw_in{j}") for j in range(2)], k.sem("wu_in")
    c0_set, scaled, shifted = k.sem("c0_set"), k.sem("raw_scaled"), k.sem("raw_shifted")
    kk_raw, kk_sq, kk_sum, kk_root, kk_inv = (k.sem(f"kk_{n}") for n in ("raw", "squares", "sums", "root", "inverse"))
    with nc.Block() as block:
        @block.sync
        def _(sp):
            sp.dma_start(scratch["x_d"], k.at(X0, KT * T)).then_inc(spilled, 16)
            for d in range(2):
                sp.dma_start(wu[0:64, d, :], A["rwkv_w_up"][0, d]).then_inc(wu_in, 16)
                sp.dma_start(wu[64:128, d, :], A["rwkv_a_up"][0, d]).then_inc(wu_in, 16)
            for j in range(2):
                sp.dma_start(raw[:, j, :], scratch["rw_d"][j]).then_inc(raw_in[j], 16)
            with sp.Fori(1, RW_TILES // 2) as i:
                for j in range(2):
                    m = sp.snap(i * 2 + j)
                    used = sp.snap(i * 2 + (j - 1))
                    sp.wait_ge(shifted, used)
                    sp.dma_start(raw[:, j, :], scratch["rw_d"][ds(m, 1), :, :].rearrange("m p t -> (m p) t")).then_inc(raw_in[j], 16)
            sp.wait_ge(wu_in, 64)

        @block.scalar
        def _(act):
            act.wait_ge(spilled, 16)
            act.wait_ge(c0_set, 2)
            with act.Fori(0, RW_TILES // 2) as i:
                for j in range(2):
                    act.wait_ge(raw_in[j], i * 16 + 16)
                    act.activation(rs[:, i * 2 + j, :], raw[:, j, :], ACT.Copy, scale=c0[:, ds(i * 2 + j, 1)]).then_inc(scaled, 1)
            act.wait_ge(shifted, RW_TILES)
            act.activation(rs[0:64, 12, :], rs[0:64, 12, :], ACT.Tanh)
            act.activation(rs[:, 13, :], rs[:, 13, :], ACT.Sigmoid)
            for t in range(4):
                if t >= 2:
                    act.wait_ge(kk_sum, t - 1)
                act.wait_ge(kk_raw, t + 1)
                act.activation(sq[:, t % 2, :], kk[:, t, :], ACT.Square).then_inc(kk_sq, 1)
            for t in range(4):
                act.wait_ge(kk_sum, t + 1)
                if t >= 2:
                    act.wait_ge(kk_inv, t - 1)
                for tc in range(3):
                    last = act.activation(root[:, t % 2, tc * TC:(tc + 1) * TC], k.bank(3 * (t % 2) + tc, TC), ACT.Sqrt)
                last.then_inc(kk_root, 1)

        @block.tensor
        def _(pe):
            for t in range(4):
                pe.wait_ge(kk_sq, t + 1)
                if t >= 2:
                    pe.wait_ge(kk_root, t - 1)
                for tc in range(3):
                    last = pe.matmul(k.bank(3 * (t % 2) + tc, TC), k.const("blockones"), sq[:, t % 2, tc * TC:(tc + 1) * TC], start=True, stop=True)
                last.then_inc(kk_sum, 1)

        @block.vector
        def _(dve):
            mu = k.col("mu", 0, 28)
            dve.tensor_tensor(c0, mu[:, 0:14], mu[:, 14:28], ALU.add).then_inc(c0_set, 1)
            dve.wait_ge(c0_set, 1)
            dve.tensor_scalar(c0, c0, -1.0, 1.0, ALU.mult, ALU.add).then_inc(c0_set, 1)
            for t in range(4):
                dve.tensor_scalar(rk[:, t, :], k.const("blockones"), k.col("r_k", t), None, ALU.mult)
            with dve.Fori(0, RW_TILES // 2) as i:
                for j in range(2):
                    dve.wait_ge(scaled, i * 2 + (j + 1))
                    for g, (a, n) in enumerate(GROUPS):
                        dve.scalar_tensor_tensor(out=rs[:, i * 2 + j, a + 1:a + n], in0=raw[:, j, a:a + n - 1],
                                                 scalar=k.pv[:, ds(i * 2 + (j + COL["mu"]), 1)],
                                                 in1=rs[:, i * 2 + j, a + 1:a + n], op0=ALU.mult, op1=ALU.add)
                    dve.drain()
                    for g, (a, n) in enumerate(GROUPS):
                        last = dve.scalar_tensor_tensor(out=rs[:, i * 2 + j, a:a + n - 1], in0=raw[:, j, a + 1:a + n],
                                                        scalar=k.pv[:, ds(i * 2 + (j + COL["mu"] + 14), 1)],
                                                        in1=rs[:, i * 2 + j, a:a + n - 1], op0=ALU.mult, op1=ALU.add)
                    last.then_inc(shifted, 1)
            dve.wait_ge(shifted, RW_TILES)
            for t in range(4):
                dve.tensor_scalar(kk[:, t, :], rs[:, 4 + t, :], k.col("k_k", t), None, ALU.mult).then_inc(kk_raw, 1)
            for t in range(4):
                dve.wait_ge(kk_root, t + 1)
                dve.tensor_scalar(root[:, t % 2, :], root[:, t % 2, :], 1e-12, None, ALU.max)
                dve.drain()
                dve.reciprocal(root[:, t % 2, :], root[:, t % 2, :])
                dve.drain()
                dve.tensor_tensor(kk[:, t, :], kk[:, t, :], root[:, t % 2, :], ALU.mult).then_inc(kk_inv, 1)
            dve.memset(k.at(YA0, 4 * T), 0.0)


def stage_rwkv(k, A, Y, latent):
    nc = k.nc
    tag = "rl" if latent else "rc"
    first, tokens = GROUPS[1] if latent else GROUPS[0]
    chunks = tokens // C
    rs, kk, ya = k.tiles(RS0, RW_TILES, T), k.tiles(KK0, 4, T), k.tiles(YA0, 4, T)
    b = rwkv_bufs(k)
    u64 = lambda v: v.rearrange("p (u t) -> p u t", t=C)
    sw, sa, L, Lx, e1, e0, ei, kd, bon, m, tmp, tmp2, vc, lc, w1, s = (u64(b[n]) for n in (
        "sw", "sa", "L", "Lx", "e1", "e0", "ei", "kd", "bon", "m", "tmp", "tmp2", "vc", "lc", "w1", "s"))
    bkt, uv = u64(b["bkt"]), u64(b["uv"])
    ar, bk, xm, g = (b[n].rearrange("p (u t) -> p u t", t=2 * C) for n in ("ar", "bk", "xm", "g"))
    st = u64(b["st"])
    wu = b["wu"].rearrange("p (d n) -> p d n", d=2)
    rk = k.at(RK0, 512).rearrange("p (m n) -> p m n", m=4)
    id2, ident = k.const("ident2"), k.ident
    pb = lambda bank, n=1: k.psum[:, bank * 512:(bank + n) * 512]
    half = lambda h: slice(64 * h, 64 * h + 64)
    units = [(u, h) for u in range(U) for h in range(2)]
    slot = lambda u, h: 8 * h + u
    b_cols = lambda h: slice(64 * (1 - h), 64 * (1 - h) + 64)
    k_cols = lambda h: slice(64 * h, 64 * h + 64)
    lvl = range(6)

    pe_s = Steps(k.sem(f"{tag}_pe_step"), ["lora", "vturn", "bonus", "n0", "gram", "bkt"] + [f"level{n}" for n in lvl] + ["w1", "u", "y", "s"])
    act_s = Steps(k.sem(f"{tag}_act_step"), ["sig", "vcopy", "exp", "bktcopy"] + [f"m{n}" for n in range(1, 6)] + ["w1", "ucopy"])
    dve_s = Steps(k.sem(f"{tag}_dve_step"), ["bias", "logs", "bon", "ark", "bonus", "n0", "gmask"] + [f"x{n}" for n in lvl] + ["s", "y"])
    pool_s = Steps(k.sem(f"{tag}_pool_step"), ["v0", "lora0", "v1", "copied"])
    pe_passed = k.sem(f"{tag}_pe_waits_passed")
    st_in, st_turned, st_set, st_out = (k.sem(f"{tag}_{n}") for n in ("state_in", "state_turned", "state_set", "state_out"))
    fin_turned, fin_copied = k.sem(f"{tag}_final_turned"), k.sem(f"{tag}_final_copied")

    def cols(i, d):
        if d == 0:
            return ds(i * C + first, C)
        return ds(i * (-C) + (first + tokens - C), C)

    with nc.Block() as block:
        @block.sync
        def _(sp):
            if latent:
                for d, n in enumerate(("state_rwkv_fwd", "state_rwkv_bwd")):
                    sp.dma_start(st[:, 4 * d:4 * d + 4, :], A[n][0, 0].rearrange("(p h) v c -> (h v) p c", h=2)).then_inc(st_in, 16)
            else:
                sp.wait_ge(fin_copied, 1)
                for d, n in enumerate(("new_f", "new_b")):
                    sp.dma_start(Y[n][0, 0].rearrange("(p h) v c -> (h v) p c", h=2), st[:, 4 * d:4 * d + 4, :]).then_inc(st_out, 16)
                sp.wait_ge(st_out, 32)

        @block.gpsimd
        def _(pool):
            pool_s.start(pool)
            with pool.Fori(0, chunks) as i:
                pool.wait_ge(pe_s.sem, pe_s.before(i, "vturn"))
                pool.wait_ge(dve_s.sem, dve_s.before(i, "bonus"))
                for d in range(2):
                    pool.tensor_copy(vc[:, 4 * d:4 * d + 4, :], rs[:, 8:12, cols(i, d)]).then_inc(pool_s.sem, 1)
                    pool.tensor_copy(lc[:, d, :], rs[:, 12, cols(i, d)]).then_inc(pool_s.sem, 1)

        @block.tensor
        def _(pe):
            pe_s.start(pe)
            if latent:
                pe.wait_ge(st_in, 32)
                for u, h in units:
                    last = pe.matmul(pb(7)[half(h), u * C:(u + 1) * C], st[half(h), u, :], id2[half(h), :], start=True, stop=True)
                last.then_inc(st_turned, 1)
            pe.wait_ge(st_set, 1)
            with pe.Fori(0, chunks) as i:
                pe.wait_ge(pool_s.sem, pool_s.here(i, "copied"))
                pe.wait_ge(dve_s.sem, dve_s.before(i, "x5"))
                pe.sem_inc(pe_passed, 1)
                for u in range(U):
                    d, p = divmod(u, 4)
                    pe.matmul(pb(0)[:, u * C:(u + 1) * C], wu[0:64, d, p * 128:(p + 1) * 128], lc[0:64, d, :], start=True, stop=True)
                    last = pe.matmul(pb(1)[:, u * C:(u + 1) * C], wu[64:128, d, p * 128:(p + 1) * 128], lc[64:128, d, :], start=True, stop=True)
                last.then_inc(pe_s.sem, 1)
                pe.wait_ge(act_s.sem, act_s.before(i, "ucopy"))
                pe.sem_inc(pe_passed, 1)
                for u, h in units:
                    last = pe.matmul(pb(2)[half(h), u * C:(u + 1) * C], vc[half(h), u, :], id2[half(h), :], start=True, stop=True)
                last.then_inc(pe_s.sem, 1)
                pe.wait_ge(dve_s.sem, dve_s.before(i, "y"))
                pe.wait_ge(dve_s.sem, dve_s.here(i, "bon"))
                pe.sem_inc(pe_passed, 1)
                for u in range(U):
                    last = pe.matmul(pb(6)[:, u * C:(u + 1) * C], rk[:, u % 4, :], bon[:, u, :], start=True, stop=True)
                last.then_inc(pe_s.sem, 1)
                pe.wait_ge(dve_s.sem, dve_s.here(i, "ark"))
                pe.wait_ge(act_s.sem, act_s.before(i, "w1"))
                pe.sem_inc(pe_passed, 1)
                for u, h in units:
                    pe.matmul(pb(4)[half(h), u * C:(u + 1) * C], bk[half(h), u, b_cols(h)], ar[half(h), u, 0:C], start=True, stop=True)
                    last = pe.matmul(pb(5)[half(h), u * C:(u + 1) * C], ar[half(h), u, 0:C], bk[half(h), u, b_cols(h)], start=True, stop=True)
                last.then_inc(pe_s.sem, 1)
                pe.wait_ge(act_s.sem, act_s.here(i, "vcopy"))
                pe.sem_inc(pe_passed, 1)
                for u, h in units:
                    n = slot(u, h)
                    last = pe.matmul(pb(0, 4)[:, n * 128:(n + 1) * 128], bk[half(h), u, :], ar[half(h), u, :], start=True, stop=True)
                last.then_inc(pe_s.sem, 1)
                pe.wait_ge(dve_s.sem, dve_s.here(i, "bonus"))
                pe.sem_inc(pe_passed, 1)
                for u, h in units:
                    n = slot(u, h)
                    last = pe.transpose(pb(6, 2)[:, n * C:(n + 1) * C], bk[half(h), u, :], id2[half(h), :])
                last.then_inc(pe_s.sem, 1)
                pe.wait_ge(dve_s.sem, dve_s.here(i, "gmask"))
                pe.sem_inc(pe_passed, 1)
                for n in lvl:
                    if n:
                        pe.wait_ge(act_s.sem, act_s.here(i, f"m{n}"))
                        pe.wait_ge(dve_s.sem, dve_s.here(i, f"x{n - 1}"))
                        pe.sem_inc(pe_passed, 1)
                    lo, hi = (C if n == 0 else 0), (C if n == 5 else 2 * C)
                    for u, h in units:
                        last = pe.matmul(pb(0, 2)[half(h), u * 128 + lo:u * 128 + hi], m[half(h), u, :], xm[half(h), u, lo:hi], start=True, stop=True)
                        if n < 5:
                            last = pe.matmul(pb(4)[half(h), u * C:(u + 1) * C], xm[half(h), u, C:2 * C], m[half(h), u, :], start=True, stop=True)
                    last.then_inc(pe_s.sem, 1)
                pe.wait_ge(dve_s.sem, dve_s.here(i, "x5"))
                pe.sem_inc(pe_passed, 1)
                for u, h in units:
                    n = slot(u, h)
                    pe.matmul(pb(5)[half(h), u * C:(u + 1) * C], g[half(h), n, 0:C], uv[half(h), n, :], start=True, stop=False)
                    last = pe.matmul(pb(5)[half(h), u * C:(u + 1) * C], ar[half(h), u, 0:C], s[half(h), u, :], start=False, stop=True)
                last.then_inc(pe_s.sem, 1)
                pe.wait_ge(act_s.sem, act_s.here(i, "w1"))
                pe.sem_inc(pe_passed, 1)
                for u, h in units:
                    last = pe.matmul(pb(3)[half(1 - h), u * C:(u + 1) * C], xm[half(h), u, 0:C], w1[half(h), u, :], start=True, stop=True)
                last.then_inc(pe_s.sem, 1)
                pe.wait_ge(act_s.sem, act_s.here(i, "ucopy"))
                pe.sem_inc(pe_passed, 1)
                for u, h in units:
                    n = slot(u, h)
                    pe.matmul(pb(6)[half(h), u * C:(u + 1) * C], uv[:, n, :], g[:, n, C:2 * C], start=True, stop=False)
                    last = pe.matmul(pb(6)[half(h), u * C:(u + 1) * C], s[half(h), u, :], ar[half(h), u, C:2 * C], start=False, stop=True)
                last.then_inc(pe_s.sem, 1)
                for u, h in units:
                    n = slot(u, h)
                    last = pe.matmul(pb(7)[half(h), u * C:(u + 1) * C], bkt[:, n, :], uv[:, n, :], start=True, stop=True)
                last.then_inc(pe_s.sem, 1)
            if not latent:
                pe.wait_ge(dve_s.sem, dve_s.here(chunks - 1, "y"))
                for u, h in units:
                    last = pe.matmul(pb(7)[half(h), u * C:(u + 1) * C], s[half(h), u, :], id2[half(h), :], start=True, stop=True)
                last.then_inc(fin_turned, 1)

        @block.scalar
        def _(act):
            act_s.start(act)
            with act.Fori(0, chunks) as i:
                act.wait_ge(dve_s.sem, dve_s.here(i, "bias"))
                act.activation(sw, sw, ACT.Sigmoid)
                act.activation(sa, sa, ACT.Sigmoid).then_inc(act_s.sem, 1)
                act.wait_ge(pe_s.sem, pe_s.here(i, "vturn"))
                act.activation(uv[half(0), 0:8, :], u64(pb(2))[half(0), :, :], ACT.Copy)
                act.activation(uv[half(1), 8:16, :], u64(pb(2))[half(1), :, :], ACT.Copy).then_inc(act_s.sem, 1)
                act.wait_ge(dve_s.sem, dve_s.here(i, "logs"))
                act.activation(e1, L, ACT.Exp)
                act.activation(e0, Lx, ACT.Exp)
                act.activation(ei, L, ACT.Exp, scale=-1.0).then_inc(act_s.sem, 1)
                act.wait_ge(pe_s.sem, pe_s.here(i, "bkt"))
                act.activation(bkt, u64(pb(6, 2)), ACT.Copy).then_inc(act_s.sem, 1)
                for n in range(1, 6):
                    act.wait_ge(pe_s.sem, pe_s.here(i, f"level{n - 1}"))
                    act.activation(m, u64(pb(4)), ACT.Copy).then_inc(act_s.sem, 1)
                act.wait_ge(pe_s.sem, pe_s.here(i, "w1"))
                act.activation(w1, u64(pb(5)), ACT.Copy, scale=-1.0).then_inc(act_s.sem, 1)
                act.wait_ge(pe_s.sem, pe_s.here(i, "u"))
                act.activation(uv[half(1), 0:8, :], u64(pb(3))[half(1), :, :], ACT.Copy)
                act.activation(uv[half(0), 8:16, :], u64(pb(3))[half(0), :, :], ACT.Copy).then_inc(act_s.sem, 1)

        @block.vector
        def _(dve):
            def bc(col, n=4):
                return col.rearrange("p (u o) -> p u o", o=1).broadcast_to([128, n, C])

            def rows(v, n):
                return v.rearrange("p (o t) -> p o t", o=1).broadcast_to([128, n, v.shape[1]])

            dve_s.start(dve)
            if latent:
                dve.wait_ge(st_turned, 1)
                dve.tensor_copy(s, u64(pb(7))).then_inc(st_set, 1)
            else:
                dve.memset(b["s"], 0.0).then_inc(st_set, 1)
            with dve.Fori(0, chunks) as i:
                dve.wait_ge(pe_s.sem, pe_s.here(i, "lora"))
                dve.tensor_tensor(sw, u64(pb(0)), bc(k.col("w0", 0, 8), 8), ALU.add)
                dve.tensor_tensor(sa, u64(pb(1)), bc(k.col("a0", 0, 8), 8), ALU.add).then_inc(dve_s.sem, 1)
                dve.wait_ge(act_s.sem, act_s.here(i, "sig"))
                dve.tensor_scalar(sw, sw, DECAY, None, ALU.mult)
                dve.drain()
                dve.tensor_tensor_scan(b["L"][:, 0:256], k.const("scan"), b["sw"][:, 0:256], 0.0, ALU.mult, ALU.add)
                dve.tensor_tensor_scan(b["L"][:, 511:255:-1], k.const("scan"), b["sw"][:, 511:255:-1], 0.0, ALU.mult, ALU.add)
                dve.drain()
                dve.tensor_tensor(Lx, L, sw, ALU.subtract).then_inc(dve_s.sem, 1)
                for d in range(2):
                    q = slice(4 * d, 4 * d + 4)
                    dve.scalar_tensor_tensor(out=kd[:, q, :], in0=sa[:, q, :], scalar=-1.0, in1=bc(k.col("k_a", 0, 4)), op0=ALU.add, op1=ALU.mult)
                    dve.tensor_tensor(sa[:, q, :], sa[:, q, :], kk[:, :, cols(i, d)], ALU.mult)
                    dve.drain()
                    dve.scalar_tensor_tensor(out=kd[:, q, :], in0=kd[:, q, :], scalar=1.0, in1=rs[:, 4:8, cols(i, d)], op0=ALU.add, op1=ALU.mult)
                    dve.drain()
                    last = dve.tensor_tensor(bon[:, q, :], kd[:, q, :], rs[:, 0:4, cols(i, d)], ALU.mult)
                last.then_inc(dve_s.sem, 1)
                dve.wait_ge(act_s.sem, act_s.here(i, "exp"))
                for d in range(2):
                    q = slice(4 * d, 4 * d + 4)
                    dve.tensor_tensor(ar[:, q, 0:C], e0[:, q, :], kk[:, :, cols(i, d)], ALU.mult)
                    dve.tensor_tensor(ar[:, q, C:2 * C], e1[:, q, :], rs[:, 0:4, cols(i, d)], ALU.mult)
                for h in range(2):
                    dve.tensor_tensor(bk[half(h), :, b_cols(h)], sa[half(h), :, :], ei[half(h), :, :], ALU.mult)
                    last = dve.tensor_tensor(bk[half(h), :, k_cols(h)], kd[half(h), :, :], ei[half(h), :, :], ALU.mult)
                last.then_inc(dve_s.sem, 1)
                dve.wait_ge(pe_s.sem, pe_s.here(i, "bonus"))
                dve.tensor_tensor(tmp, u64(pb(6)), vc, ALU.mult)
                for d in range(2):
                    dve.drain()
                    last = dve.tensor_tensor(ya[:, :, cols(i, d)], ya[:, :, cols(i, d)], tmp[:, 4 * d:4 * d + 4, :], ALU.add)
                last.then_inc(dve_s.sem, 1)
                dve.wait_ge(pe_s.sem, pe_s.here(i, "n0"))
                for d in range(2):
                    q = slice(4 * d, 4 * d + 4)
                    up, low = (k.const("lt"), k.const("gt")) if d == 0 else (k.const("gt"), k.const("lt"))
                    dve.tensor_tensor(m[:, q, :], u64(pb(5))[:, q, :], rows(low, 4), ALU.mult)
                    dve.tensor_tensor(xm[:, q, C:2 * C], u64(pb(4))[:, q, :], rows(up, 4), ALU.mult)
                dve.drain()
                dve.tensor_tensor(xm[:, :, 0:C], xm[:, :, C:2 * C], rows(id2, 8), ALU.add).then_inc(dve_s.sem, 1)
                dve.wait_ge(pe_s.sem, pe_s.here(i, "gram"))
                for h in range(2):
                    for d in range(2):
                        last = dve.tensor_tensor(g[:, 8 * h + 4 * d:8 * h + 4 * d + 4, :], pb(2 * h + d).rearrange("p (n t) -> p n t", t=128),
                                                 rows(k.const("mask_b" if d else "mask_f"), 4), ALU.mult)
                last.then_inc(dve_s.sem, 1)
                for n in lvl:
                    dve.wait_ge(pe_s.sem, pe_s.here(i, f"level{n}"))
                    acc = pb(0, 2).rearrange("p (u t) -> p u t", t=2 * C)
                    if n < 5:
                        last = dve.tensor_copy(xm[:, :, C:2 * C], acc[:, :, C:2 * C])
                    if n:
                        last = dve.tensor_tensor(xm[:, :, 0:C], acc[:, :, 0:C], xm[:, :, 0:C], ALU.add)
                    last.then_inc(dve_s.sem, 1)
                dve.wait_ge(pe_s.sem, pe_s.here(i, "s"))
                dve.tensor_tensor(tmp, u64(pb(7)), s, ALU.add)
                dve.drain()
                for d in range(2):
                    q = slice(4 * d, 4 * d + 4)
                    end = e1[:, q, C - 1:C] if d == 0 else e1[:, q, 0:1]
                    last = dve.tensor_tensor(s[:, q, :], tmp[:, q, :], end.broadcast_to([128, 4, C]), ALU.mult)
                last.then_inc(dve_s.sem, 1)
                for d in range(2):
                    dve.drain()
                    last = dve.tensor_tensor(ya[:, :, cols(i, d)], u64(pb(6))[:, 4 * d:4 * d + 4, :], ya[:, :, cols(i, d)], ALU.add)
                last.then_inc(dve_s.sem, 1)
            if not latent:
                dve.wait_ge(fin_turned, 1)
                dve.tensor_copy(st[:, 0:8, :], u64(pb(7))).then_inc(fin_copied, 1)


def stage_rwkv_post(k, A, scratch):
    nc = k.nc
    ya, rs = k.tiles(YA0, 4, T), k.tiles(RS0, RW_TILES, T)
    out = k.tiles(OA0 + 4 * T, 4, T)
    gup = k.at(Z1, 512)
    sq, root = k.tiles(Z1 + 1024, 2, T), k.tiles(Z1 + 1024 + 2 * T, 2, T)
    eps = k.at(SM0 + 1, 1)
    S = lambda n: k.sem(f"gn_{n}")
    gup_in, summed, centred, squared, var_ready, rooted, normed, gate_ready, done = (S(n) for n in (
        "gup_in", "summed", "centred", "squared", "var", "root", "normed", "gate", "done"))
    eps_set, scaled = S("eps"), S("scaled")
    with nc.Block() as block:
        @block.sync
        def _(sp):
            sp.dma_start(gup, A["rwkv_g_up"][0]).then_inc(gup_in, 16)

        @block.tensor
        def _(pe):
            pe.wait_ge(gup_in, 16)
            for t in range(4):
                if t:
                    pe.wait_ge(centred, t)
                for tc in range(3):
                    last = pe.matmul(k.bank(tc, TC), k.const("blockones"), ya[:, t, tc * TC:(tc + 1) * TC], start=True, stop=True)
                last.then_inc(summed, 1)
                pe.wait_ge(squared, t + 1)
                if t:
                    pe.wait_ge(done, t)
                for tc in range(3):
                    last = pe.matmul(k.bank(3 + tc, TC), k.const("blockones"), sq[:, t % 2, tc * TC:(tc + 1) * TC], start=True, stop=True)
                last.then_inc(var_ready, 1)
                pe.wait_ge(rooted, t + 1)
                for tc in range(3):
                    last = pe.matmul(k.bank(3 + tc, TC), gup[:, t * 128:(t + 1) * 128], rs[:, 13, tc * TC:(tc + 1) * TC], start=True, stop=True)
                last.then_inc(gate_ready, 1)

        @block.scalar
        def _(act):
            act.wait_ge(eps_set, 1)
            for t in range(4):
                act.wait_ge(centred, t + 1)
                act.activation(sq[:, t % 2, :], ya[:, t, :], ACT.Square).then_inc(squared, 1)
                act.wait_ge(var_ready, t + 1)
                for tc in range(3):
                    last = act.activation(root[:, t % 2, tc * TC:(tc + 1) * TC], k.bank(3 + tc, TC), ACT.Sqrt, bias=eps, scale=1.0 / C)
                last.then_inc(rooted, 1)
                act.wait_ge(normed, t + 1)
                act.activation(ya[:, t, :], ya[:, t, :], ACT.Identity, scale=k.col("ln_g", t), bias=k.col("ln_b", t)).then_inc(scaled, 1)

        @block.vector
        def _(dve):
            dve.memset(eps, 64e-5).then_inc(eps_set, 1)
            for t in range(4):
                dve.wait_ge(summed, t + 1)
                for tc in range(3):
                    v = ya[:, t, tc * TC:(tc + 1) * TC]
                    last = dve.scalar_tensor_tensor(out=v, in0=k.bank(tc, TC), scalar=-1.0 / C, in1=v, op0=ALU.mult, op1=ALU.add)
                last.then_inc(centred, 1)
                dve.wait_ge(rooted, t + 1)
                dve.reciprocal(root[:, t % 2, :], root[:, t % 2, :])
                dve.drain()
                dve.tensor_tensor(ya[:, t, :], ya[:, t, :], root[:, t % 2, :], ALU.mult).then_inc(normed, 1)
                dve.wait_ge(scaled, t + 1)
                dve.wait_ge(gate_ready, t + 1)
                for tc in range(3):
                    c = slice(tc * TC, (tc + 1) * TC)
                    last = dve.tensor_tensor(out[:, t, c], k.bank(3 + tc, TC), ya[:, t, c], ALU.mult)
                last.then_inc(done, 1)


def stage_mixer_out(k, A, scratch):
    back = k.sem("x_back")
    with k.nc.Block() as block:
        @block.sync
        def _(sp):
            sp.dma_start(k.at(X0, KT * T), scratch["x_d"]).then_inc(back, 16)
            sp.wait_ge(back, 16)
    heads = k.tiles(OA0, 8, T)
    stage_gemm(k, "mix", lambda kt: heads[:, kt, :], KT, A["ab_w_out"][0].rearrange("(k p) n -> p k n", p=128),
               KT, H0, evac_residual(k, 0, 0))


HL = NL // 2
HKT = HL // 128
Q = 256
QT = Q // 128
ROUNDS = D // Q
(FT0, IT0, UT0, SS0, DD0, AB0, OC0, UK0, PR0, FB0, WIN0, VX0, U10, TI0, HD0, W30, DQ0, HW0, TC0, PT0, PU0, PS0, PD0, PK0, PA0,
 HY_END) = [int(x) for x in np.cumsum([0, 8192, 8192, 2048, 2048, 2048, 4096, 1024, 2048, 1024, 1024, 512, 6912, 2304, 1024, 1152,
                                        512, 256, 200, 16, 512, 256, 256, 256, 1024, 512])]
assert HY_END <= CST
TWO_PI = 2.0 * math.pi
TWO_PI_HI = 6.28125
TWO_PI_LO = TWO_PI - TWO_PI_HI
MAGIC = 1.5 * 2.0 ** 23


def stage_hyena_in(k, A, scratch):
    raw, z = k.tiles(BIG, 2, T), k.tiles(BIG + 2 * T, 2, T)
    z_d = scratch["z_d"]

    def evac(dve, m, j, tc, acc):
        return dve.tensor_scalar(raw[:, j, tc * TC:(tc + 1) * TC], acc, k.pv[:, ds(m + COL["b_in"], 1)], None, ALU.add)

    def after(dve, m, j):
        tap = lambda n: k.pv[:, ds(m + (COL["conv_w"] + 24 * n), 1)]
        dve.tensor_scalar(z[:, j, :], raw[:, j, :], tap(1), k.pv[:, ds(m + COL["conv_b"], 1)], ALU.mult, ALU.add)
        dve.drain()
        for a, n in GROUPS:
            dve.scalar_tensor_tensor(out=z[:, j, a + 1:a + n], in0=raw[:, j, a:a + n - 1], scalar=tap(0),
                                     in1=z[:, j, a + 1:a + n], op0=ALU.mult, op1=ALU.add)
        dve.drain()
        for a, n in GROUPS:
            last = dve.scalar_tensor_tensor(out=z[:, j, a:a + n - 1], in0=raw[:, j, a + 1:a + n], scalar=tap(2),
                                            in1=z[:, j, a:a + n - 1], op0=ALU.mult, op1=ALU.add)
        return last

    stage_gemm(k, "hz", lambda kt: k.H[:, kt, :], KT, A["hy_w_in"][0].rearrange("(k p) n -> p k n", p=128), 24, WB, evac,
               store=lambda act, m, j: (z_d[ds(m, 1), :, :].rearrange("m p t -> (m p) t"), z[:, j, :]), after=after)


def stage_filter_features(k, A, consts, scratch):
    nc = k.nc
    feat = k.at(UT0, T)
    arg, turns = k.at(AB0, T), k.at(AB0 + T, T)
    arg2 = k.at(AB0 + 2 * T, T)
    hd = k.at(HD0, T)
    w = [k.at(HW0 + 64 * n, 64) for n in range(3)]
    cols = k.at(HW0 + 192, 6)
    spilled, w_in, tab_in = k.sem("x_spilled1"), k.sem("filter_w_in"), k.sem("tables_in")
    summed, reduced, sined = k.sem("filter_sums"), k.sem("filter_args"), k.sem("filter_sines")
    with nc.Block() as block:
        @block.sync
        def _(sp):
            sp.dma_start(scratch["x_d"], k.at(X0, KT * T)).then_inc(spilled, 16)
            sp.dma_start(feat[0:33, :], consts["feat"]).then_inc(w_in, 16)
            for n in range(3):
                sp.dma_start(w[n][0:(33 if n == 0 else 64), :], A[f"hy_f_w{n}"][0]).then_inc(w_in, 16)
                sp.dma_start(cols[0:64, n:n + 1], A[f"hy_f_b{n}"].rearrange("l p -> p l")).then_inc(w_in, 16)
                sp.dma_start(cols[0:64, 3 + n:4 + n], A["hy_f_freq"][:, n, :].rearrange("l p -> p l")).then_inc(w_in, 16)
            sp.wait_ge(spilled, 16)
            sp.dma_start(k.at(FT0, 8192), consts["dft"]).then_inc(tab_in, 16)
            sp.dma_start(k.at(IT0, 8192), consts["idft"]).then_inc(tab_in, 16)
            sp.dma_start(k.at(PT0, 512), consts["pdft"]).then_inc(tab_in, 16)
            sp.dma_start(k.at(TC0, 9), consts["steps"]).then_inc(tab_in, 16)
            sp.wait_ge(tab_in, 64)

        @block.tensor
        def _(pe):
            pe.wait_ge(w_in, 160)
            for n in range(3):
                if n:
                    pe.wait_ge(sined, n)
                src = feat[0:33, :] if n == 0 else hd[0:64, :]
                for tc in range(3):
                    last = pe.matmul(k.bank(tc, TC)[0:64, :], w[n][0:src.shape[0], :], src[:, tc * TC:(tc + 1) * TC], start=True, stop=True)
                last.then_inc(summed, 1)

        @block.scalar
        def _(act):
            for n in range(3):
                act.wait_ge(reduced, n + 1)
                act.activation(hd[0:64, :], arg[0:64, :], ACT.Sin).then_inc(sined, 1)
            act.wait_ge(sined, 3)
            act.activation(hd[64:128, :], hd[0:64, :], ACT.Copy)

        @block.vector
        def _(dve):
            q = slice(0, 64)
            for n in range(3):
                dve.wait_ge(summed, n + 1)
                for tc in range(3):
                    dve.tensor_scalar(arg2[q, tc * TC:(tc + 1) * TC], k.bank(tc, TC)[q, :], cols[q, n:n + 1], cols[q, 3 + n:4 + n], ALU.add, ALU.mult)
                dve.drain()
                dve.tensor_scalar(turns[q, :], arg2[q, :], 1.0 / TWO_PI, MAGIC, ALU.mult, ALU.add)
                dve.drain()
                dve.tensor_scalar(turns[q, :], turns[q, :], -MAGIC, None, ALU.add)
                dve.drain()
                dve.scalar_tensor_tensor(out=arg2[q, :], in0=turns[q, :], scalar=-TWO_PI_HI, in1=arg2[q, :], op0=ALU.mult, op1=ALU.add)
                dve.drain()
                dve.scalar_tensor_tensor(out=arg2[q, :], in0=turns[q, :], scalar=-TWO_PI_LO, in1=arg2[q, :], op0=ALU.mult, op1=ALU.add)
                dve.drain()
                dve.tensor_scalar(arg[q, :], arg2[q, :], 3.1415925, -3.1415925, ALU.min, ALU.max).then_inc(reduced, 1)


def stage_hyena(k, A, consts, scratch):
    nc = k.nc
    ft = k.at(FT0, 8192).rearrange("p (c o k n) -> p c o k n", c=2, o=2, k=HKT)
    it = k.at(IT0, 8192).rearrange("p (c o k n) -> p c o k n", c=2, o=2, k=HKT)
    ptab = k.tiles(PT0, 4, 128)
    ut, ss, dd = k.tiles(UT0, 8, Q), k.tiles(SS0, 8, Q), k.tiles(DD0, 8, Q)
    ab = k.at(AB0, 4096).rearrange("p (c o f n) -> p c o f n", c=2, o=2, f=HKT)
    oc, uk, pr = k.tiles(OC0, 4, Q), k.tiles(UK0, 8, Q), k.tiles(PR0, 4, Q)
    fb = [k.tiles(FB0 + 512 * j, 2, Q) for j in range(2)]
    win = k.tiles(WIN0, 2, Q)
    vx, u1, ti = k.tiles(VX0, 3 * QT, T), k.tiles(U10, QT, T), k.tiles(TI0, 2, 512)
    hd, w3, dq, tcol = k.at(HD0, T), k.tiles(W30, 2, Q), k.at(DQ0, Q), k.at(TC0, 9)
    pu, ps, pd = k.at(PU0, Q), k.at(PS0, Q), k.at(PD0, Q)
    pk, pa = k.tiles(PK0, 4, Q), k.tiles(PA0, 2, Q)
    z_d = scratch["z_d"]
    ACC = ("Co", "Ce", "So", "Se", "Ko", "Ke", "Do", "De")
    pe_n, act_n, dve_n = [], [], []
    for o in range(2):
        pe_n += [f"{o}ptok", f"{o}pfilt", f"{o}pfreq", f"{o}pinv"] + [f"{o}{n}{t}" for t in range(8) for n in ("tok", "filt")]
        pe_n += [f"{o}f{f}{a}" for f in range(HKT) for a in ACC] + [f"{o}inv{n}" for n in range(2 * QT)]
        act_n += [f"{o}pwin", f"{o}ptok"]
        for t in range(8):
            act_n += [f"{o}tok{t}", f"{o}win{t}"]
        act_n += [f"{o}f{f}{a}" for f in range(HKT) for a in ACC[0::2]]
        dve_n += [f"{o}pfilt", f"{o}pfreq", f"{o}pinv"] + [f"{o}filt{t}" for t in range(8)]
        for f in range(HKT):
            dve_n += [f"{o}f{f}{a}" for a in ACC[1::2]] + [f"{o}f{f}ab"]
        dve_n += [f"{o}inv{n}" for n in range(2 * QT)]
    pe_s, act_s, dve_s = Steps(k.sem("hy_pe_step"), pe_n), Steps(k.sem("hy_act_step"), act_n), Steps(k.sem("hy_dve_step"), dve_n)
    passed = k.sem("hy_sp_passed")
    hb = lambda i, o, m: k.pv[:, ds(i * QT + (COL["hbias"] + 8 * o + m), 1)]
    in_sem, stored = k.sem("hy_round_in"), k.sem("hy_stored")
    LOADS = 3 * QT + 2 * 2 + 1
    half = lambda o: slice(64 * o, 64 * o + 64)
    even_odd = lambda a, o: slice(NP_ + o + 2 * a, NP_ + o + 2 * a + 255, 2)
    bank = k.bank

    with nc.Block() as block:
        @block.sync
        def _(sp):
            with sp.Fori(0, ROUNDS) as i:
                c0 = sp.snap(i * Q)
                rows = [sp.snap(i * QT + (m + 8 * part)) for part in (2, 0, 1) for m in range(QT)]
                done = sp.snap(dve_s.here(i, f"1inv{2 * QT - 1}"))
                n_stored = sp.snap(i * (16 * QT) + 16 * QT)
                outs = [sp.snap(i * QT + (m + 16)) for m in range(QT)]
                for n, r in enumerate(rows):
                    sp.dma_start(vx[:, n, :], z_d[ds(r, 1), :, :].rearrange("m p t -> (m p) t")).then_inc(in_sem, 16)
                w3v = A["hy_f_w3"][0].rearrange("p (o d n) -> p o d n", o=2, d=2)
                for o in range(2):
                    for d in range(2):
                        sp.dma_start(w3[half(o), d, :], w3v[:, o, d, ds(c0, Q)]).then_inc(in_sem, 16)
                sp.dma_start(dq, consts["deltas"][:, ds(c0, Q)]).then_inc(in_sem, 16)
                sp.wait_ge(dve_s.sem, done)
                for m in range(QT):
                    sp.dma_start(z_d[ds(outs[m], 1), :, :].rearrange("m p t -> (m p) t"), vx[:, m, :]).then_inc(stored, 16)
                sp.wait_ge(stored, n_stored)
                sp.sem_inc(passed, 1)

        @block.tensor
        def _(pe):
            pe_s.start(pe)
            with pe.Fori(0, ROUNDS) as i:
                pe.wait_ge(in_sem, i * (16 * LOADS) + 16 * LOADS)
                for o in range(2):
                    u = vx if o == 0 else u1
                    if o:
                        pe.wait_ge(dve_s.sem, dve_s.here(i, f"0inv{2 * QT - 1}"))
                    else:
                        pe.wait_ge(dve_s.sem, dve_s.before(i, f"1inv{2 * QT - 1}"))
                    for m in range(QT):
                        last = pe.transpose(bank(0)[:, m * 128:(m + 1) * 128], u[:, m, 0:NP_], k.ident)
                    last.then_inc(pe_s.sem, 1)
                    for d in range(2):
                        last = pe.matmul(bank(1)[:, d * Q:(d + 1) * Q], hd[half(o), 0:NP_], w3[half(o), d, :], start=True, stop=True)
                    last.then_inc(pe_s.sem, 1)
                    pe.wait_ge(act_s.sem, act_s.here(i, f"{o}ptok"))
                    pe.wait_ge(dve_s.sem, dve_s.here(i, f"{o}pfilt"))
                    for n, (tab, v) in enumerate([(0, pu), (1, pu), (0, ps), (1, pd)]):
                        last = pe.matmul(bank(2 + n)[:, 0:Q], ptab[:, tab, :], v, start=True, stop=True)
                    last.then_inc(pe_s.sem, 1)
                    pe.wait_ge(dve_s.sem, dve_s.here(i, f"{o}pfreq"))
                    for m in range(QT):
                        for c in range(2):
                            last = pe.matmul(bank(6)[:, m * 128:(m + 1) * 128], pa[:, c, m * 128:(m + 1) * 128], ptab[:, 2 + c, :],
                                             start=(c == 0), stop=(c == 1))
                    last.then_inc(pe_s.sem, 1)
                    for t in range(8):
                        par, kt = divmod(t, HKT)
                        if t >= 2:
                            pe.wait_ge(act_s.sem, act_s.here(i, f"{o}tok{t - 2}"))
                        elif t == 0:
                            pe.wait_ge(dve_s.sem, dve_s.here(i, f"{o}pfreq"))
                        for m in range(QT):
                            last = pe.transpose(bank(2 + t % 2)[:, m * 128:(m + 1) * 128], u[:, m, even_odd(kt * 128, par)], k.ident)
                        last.then_inc(pe_s.sem, 1)
                        if t >= 2:
                            pe.wait_ge(dve_s.sem, dve_s.here(i, f"{o}filt{t - 2}"))
                        for d in range(2):
                            last = pe.matmul(bank(t % 2)[:, d * Q:(d + 1) * Q], hd[half(o), even_odd(kt * 128, par)], w3[half(o), d, :], start=True, stop=True)
                        last.then_inc(pe_s.sem, 1)
                    pe.wait_ge(act_s.sem, act_s.here(i, f"{o}tok7"))
                    pe.wait_ge(dve_s.sem, dve_s.here(i, f"{o}filt7"))
                    for f in range(HKT):
                        for n, a in enumerate(ACC):
                            if f:
                                s_, nm = (act_s, a) if n % 2 == 0 else (dve_s, a)
                                pe.wait_ge(s_.sem, s_.here(i, f"{o}f{f - 1}{nm}"))
                            c, par = int(a[0] in "SD"), int(a[1] == "o")
                            src = {"C": ut, "S": ut, "K": ss, "D": dd}[a[0]]
                            for kt in range(HKT):
                                last = pe.matmul(bank(n)[:, 0:Q], ft[:, c, par, kt, f * 128:(f + 1) * 128], src[:, par * HKT + kt, :],
                                                 start=(kt == 0), stop=(kt == HKT - 1))
                            last.then_inc(pe_s.sem, 1)
                    pe.wait_ge(dve_s.sem, dve_s.here(i, f"{o}f{HKT - 1}ab"))
                    for n in range(2 * QT):
                        m, par = divmod(n, 2)
                        for c in range(2):
                            for f in range(HKT):
                                last = pe.matmul(bank(n), ab[:, c, par, f, m * 128:(m + 1) * 128], it[:, c, par, f, :],
                                                 start=(c == 0 and f == 0), stop=(c == 1 and f == HKT - 1))
                        last.then_inc(pe_s.sem, 1)

        @block.scalar
        def _(act):
            act_s.start(act)
            with act.Fori(0, ROUNDS) as i:
                act.wait_ge(in_sem, i * (16 * LOADS) + 16 * LOADS)
                for o in range(2):
                    if o:
                        act.wait_ge(dve_s.sem, dve_s.here(i, "0pfilt"))
                    act.activation(win[:, 0, :], dq, ACT.Exp, scale=tcol[:, 8:9]).then_inc(act_s.sem, 1)
                    act.wait_ge(pe_s.sem, pe_s.here(i, f"{o}ptok"))
                    act.activation(pu, bank(0)[:, 0:Q], ACT.Copy).then_inc(act_s.sem, 1)
                    act.wait_ge(dve_s.sem, dve_s.here(i, f"{o}pfilt"))
                    for t in range(8):
                        act.wait_ge(pe_s.sem, pe_s.here(i, f"{o}tok{t}"))
                        act.activation(ut[:, t, :], bank(2 + t % 2)[:, 0:Q], ACT.Copy).then_inc(act_s.sem, 1)
                        if t >= 2:
                            act.wait_ge(dve_s.sem, dve_s.here(i, f"{o}filt{t - 2}"))
                        act.activation(win[:, t % 2, :], dq, ACT.Exp, scale=tcol[:, t:t + 1]).then_inc(act_s.sem, 1)
                    for f in range(HKT):
                        for n, a in enumerate(ACC[0::2]):
                            act.wait_ge(pe_s.sem, pe_s.here(i, f"{o}f{f}{a}"))
                            if f:
                                act.wait_ge(dve_s.sem, dve_s.here(i, f"{o}f{f - 1}{ACC[2 * n + 1]}"))
                            act.activation(oc[:, n, :], bank(2 * n)[:, 0:Q], ACT.Copy).then_inc(act_s.sem, 1)

        @block.vector
        def _(dve):
            tt = dve.tensor_tensor
            dve_s.start(dve)
            with dve.Fori(0, ROUNDS) as i:
                dve.wait_ge(in_sem, i * (16 * LOADS) + 16 * LOADS)
                for o in range(2):
                    u = vx[:, 0:QT, :] if o == 0 else u1
                    out = u1 if o == 0 else vx[:, 0:QT, :]
                    x = vx[:, QT * (1 + o):QT * (2 + o), :]

                    def windowed(psum_bank, w, buf, hs, hdif, first):
                        tt(buf, psum_bank.rearrange("p (d n) -> p d n", d=2),
                           w.rearrange("p (o n) -> p o n", o=1).broadcast_to([128, 2, Q]), ALU.mult)
                        dve.drain()
                        if first:
                            dve.tensor_scalar(buf[:, 1, :], buf[:, 1, :], k.const("nz"), None, ALU.mult)
                            dve.drain()
                        tt(hs, buf[:, 0, :], buf[:, 1, :], ALU.add)
                        return tt(hdif, buf[:, 0, :], buf[:, 1, :], ALU.subtract)

                    dve.wait_ge(pe_s.sem, pe_s.here(i, f"{o}pfilt"))
                    dve.wait_ge(act_s.sem, act_s.here(i, f"{o}pwin"))
                    windowed(bank(1), win[:, 0, :], fb[0], ps, pd, True).then_inc(dve_s.sem, 1)
                    dve.wait_ge(pe_s.sem, pe_s.here(i, f"{o}pfreq"))
                    for n in range(4):
                        dve.tensor_copy(pk[:, n, :], bank(2 + n)[:, 0:Q])
                    dve.drain()
                    tt(pa[:, 0, :], pk[:, 2, :], pk[:, 0, :], ALU.mult)
                    tt(pr[:, 0, :], pk[:, 3, :], pk[:, 1, :], ALU.mult)
                    tt(pa[:, 1, :], pk[:, 2, :], pk[:, 1, :], ALU.mult)
                    tt(pr[:, 1, :], pk[:, 3, :], pk[:, 0, :], ALU.mult)
                    dve.drain()
                    tt(pa[:, 0, :], pa[:, 0, :], pr[:, 0, :], ALU.subtract)
                    tt(pa[:, 1, :], pa[:, 1, :], pr[:, 1, :], ALU.add).then_inc(dve_s.sem, 1)
                    dve.wait_ge(pe_s.sem, pe_s.here(i, f"{o}pinv"))
                    for m in range(QT):
                        dve.scalar_tensor_tensor(out=ti[:, m, 0:NP_], in0=u[:, m, 0:NP_], scalar=hb(i, o, m), in1=bank(6)[:, m * 128:(m + 1) * 128],
                                                 op0=ALU.mult, op1=ALU.add)
                    dve.drain()
                    for m in range(QT):
                        last = tt(out[:, m, 0:NP_], ti[:, m, 0:NP_], x[:, m, 0:NP_], ALU.mult)
                    last.then_inc(dve_s.sem, 1)

                    for t in range(8):
                        dve.wait_ge(pe_s.sem, pe_s.here(i, f"{o}filt{t}"))
                        dve.wait_ge(act_s.sem, act_s.here(i, f"{o}win{t}"))
                        windowed(bank(t % 2), win[:, t % 2, :], fb[t % 2], ss[:, t, :], dd[:, t, :], t == 0).then_inc(dve_s.sem, 1)
                    for f in range(HKT):
                        for n, a in enumerate(ACC[1::2]):
                            dve.wait_ge(act_s.sem, act_s.here(i, f"{o}f{f}{ACC[2 * n]}"))
                            dve.wait_ge(pe_s.sem, pe_s.here(i, f"{o}f{f}{a}"))
                            ev, od = bank(2 * n + 1)[:, 0:Q], oc[:, n, :]
                            tt(uk[:, 2 * n, :], ev, od, ALU.add)
                            if a[0] in "CK":
                                last = tt(uk[:, 2 * n + 1, :], ev, od, ALU.subtract)
                            else:
                                last = dve.scalar_tensor_tensor(out=uk[:, 2 * n + 1, :], in0=ev, scalar=-1.0, in1=od, op0=ALU.mult, op1=ALU.add)
                            last.then_inc(dve_s.sem, 1)
                        dve.drain()
                        uc, us, kc, dk = (uk[:, 2 * n:2 * n + 2, :] for n in range(4))
                        yc, ys = pr[:, 0:2, :], pr[:, 2:4, :]
                        x1, x2 = fb[0], fb[1]
                        tt(yc, kc, uc, ALU.mult)
                        tt(x1, dk, us, ALU.mult)
                        tt(ys, kc, us, ALU.mult)
                        tt(x2, dk, uc, ALU.mult)
                        dve.drain()
                        tt(yc, yc, x1, ALU.subtract)
                        tt(ys, ys, x2, ALU.add)
                        dve.drain()
                        tt(ab[:, 0, 0, f, :], yc[:, 0, :], yc[:, 1, :], ALU.add)
                        tt(ab[:, 0, 1, f, :], yc[:, 0, :], yc[:, 1, :], ALU.subtract)
                        tt(ab[:, 1, 0, f, :], ys[:, 0, :], ys[:, 1, :], ALU.subtract)
                        tt(ab[:, 1, 1, f, :], ys[:, 0, :], ys[:, 1, :], ALU.add).then_inc(dve_s.sem, 1)
                    for n in range(2 * QT):
                        m, par = divmod(n, 2)
                        st = slice(NP_ + par, NP_ + par + 2 * HL - 1, 2)
                        dve.wait_ge(pe_s.sem, pe_s.here(i, f"{o}inv{n}"))
                        dve.scalar_tensor_tensor(out=ti[:, n % 2, :], in0=u[:, m, st], scalar=hb(i, o, m), in1=bank(n), op0=ALU.mult, op1=ALU.add)
                        dve.drain()
                        tt(out[:, m, st], ti[:, n % 2, :], x[:, m, st], ALU.mult).then_inc(dve_s.sem, 1)


def stage_hyena_out(k, A, scratch):
    back = k.sem("hy_back")
    with k.nc.Block() as block:
        @block.sync
        def _(sp):
            sp.dma_start(k.at(X0, KT * T), scratch["x_d"]).then_inc(back, 16)
            for m in range(KT):
                sp.dma_start(k.H[:, m, :], scratch["z_d"][16 + m]).then_inc(back, 16)
            sp.wait_ge(back, 16 * (KT + 1))
    stage_gemm(k, "hyo", lambda kt: k.H[:, kt, :], KT, A["hy_w_out"][0].rearrange("(k p) n -> p k n", p=128),
               KT, WB, evac_residual(k, 1, 0, COL["b_out"]))


def build(nc, A, consts, Y, scratch):
    with ExitStack() as ctx:
        arena = ctx.enter_context(nc.sbuf_tensor("arena", [128, END], F32))
        psum = ctx.enter_context(nc.psum_tensor("acc", [128, 4096], F32))
        k = Kit(nc, ctx, arena, psum)
        stage_setup(k, A, consts)
        stage_norm(k, k.col("norm1", 0, 8), 0, 0, k.H, "n1_0")
        stage_project(k, A, Y, scratch)
        stage_keys(k, A, Y, consts)
        stage_attend(k, latent=False)
        stage_attend(k, latent=True)
        stage_head_norm(k)
        k.reuse_semaphores()
        stage_rwkv_pre(k, A, scratch)
        stage_rwkv(k, A, Y, latent=False)
        stage_rwkv(k, A, Y, latent=True)
        stage_rwkv_post(k, A, scratch)
        k.reuse_semaphores()
        stage_mixer_out(k, A, scratch)
        stage_norm(k, k.col("norm2", 0, 8), 0, 1, k.H, "n2_0")
        stage_ffn(k, A, 0)
        stage_norm(k, k.col("norm1", 8, 8), 1, 0, k.H, "n1_1")
        k.reuse_semaphores()
        stage_hyena_in(k, A, scratch)
        stage_filter_features(k, A, consts, scratch)
        stage_hyena(k, A, consts, scratch)
        k.reuse_semaphores()
        stage_hyena_out(k, A, scratch)
        stage_norm(k, k.col("norm2", 8, 8), 1, 1, k.H, "n2_1")
        stage_ffn(k, A, 1)
        stage_norm(k, k.col("final", 0, 8), None, 0, k.H, "n_f")
        stage_out(k, A, Y)


_INS = ["x_prompt", "x_sample", "cache_diff_k", "cache_diff_v", "state_rwkv_fwd", "state_rwkv_bwd", "c", "c_ctx",
        "ada_w", "ada_b", "norm1_g", "norm2_g", "ffn_w1", "ffn_w3", "ffn_w2", "final_g",
        "ab_w_in", "ab_w_out", "diff_lambda", "diff_subln_g", "rwkv_mu", "rwkv_w0", "rwkv_w_up", "rwkv_a0", "rwkv_a_up",
        "rwkv_g_up", "rwkv_k_k", "rwkv_k_a", "rwkv_r_k", "rwkv_ln_g", "rwkv_ln_b",
        "hy_w_in", "hy_b_in", "hy_conv_w", "hy_conv_b", "hy_f_w0", "hy_f_b0", "hy_f_w1", "hy_f_b1", "hy_f_w2", "hy_f_b2",
        "hy_f_w3", "hy_f_freq", "hy_bias", "hy_w_out", "hy_b_out"]
_OUTS = [("y_prompt", (1, 128, 1024)), ("y_sample", (1, 1024, 1024)), ("new_k", (1, 1, 8, 2, 128, 32)),
         ("new_v", (1, 1, 8, 128, 64)), ("new_f", (1, 1, 8, 64, 64)), ("new_b", (1, 1, 8, 64, 64))]
_SCRATCH = [("rw_d", (RW_TILES, 128, T)), ("x_d", (128, KT * T)), ("z_d", (24, 128, T))]


def shape_constants():
    c = {}
    blk = np.zeros((128, CW), np.float32)

    def put(name, v):
        o, w = CCOL[name]
        blk[:, o:o + w] = v

    p = np.arange(128)
    put("ident", np.eye(128))
    put("blockones", (p[:, None] // 64 == p[None] // 64))
    s, t = p[:, None] % 64, p[None] % 64
    late = p[None] // 64
    put("mask_f", np.where(late, s <= t, s < t))
    put("mask_b", np.where(late, s >= t, s > t))
    j = np.arange(64)[None]
    put("lt", -1.0 * (p[:, None] % 64 < j))
    put("gt", -1.0 * (p[:, None] % 64 > j))
    put("ident2", p[:, None] % 64 == j)
    put("scan", (np.arange(256)[None] % 64 != 0) * np.ones((128, 1)))
    rot = np.zeros((128, 128))
    for m in range(128):
        if (m // 8) % 2 == 0:
            rot[m + 8, m] = -1.0
        else:
            rot[m - 8, m] = 1.0
    put("rot", rot)
    put("nz", (p[:, None] != 0))
    c["cblk"] = blk
    tt = np.arange(NL)
    inv = 10000.0 ** (-np.arange(8, dtype=np.float32) / 8)
    ar, ac = (tt // 64)[:, None] * inv[None], (tt % 64)[:, None] * inv[None]
    ang = np.concatenate([ar, ar, ac, ac], 1).T.astype(np.float32).astype(np.float64)
    c["rope"] = np.stack([np.tile(np.cos(ang), (4, 1)), np.tile(np.sin(ang), (4, 1))]).astype(np.float32)
    def table(length, steps, freqs):
        phase = (np.outer(steps, 2 * freqs + 1) % (4 * length)) * (math.pi / (2 * length))
        return np.cos(phase), np.sin(phase)

    a, f = np.arange(HL), np.arange(HL)
    fwd = [[None] * 2 for _ in range(2)]
    for par in range(2):
        fwd[0][par], fwd[1][par] = table(NL, 2 * a + par, f)
    lay = lambda m: m.reshape(HKT, 128, HL).transpose(1, 0, 2)
    c["dft"] = np.stack([[lay(fwd[q][par]) for par in range(2)] for q in range(2)]).transpose(2, 0, 1, 3, 4).reshape(128, -1).astype(np.float32)
    c["idft"] = np.stack([[lay(fwd[q][par].T / NL) for par in range(2)] for q in range(2)]).transpose(2, 0, 1, 3, 4).reshape(128, -1).astype(np.float32)
    pc, psn = table(NP_, np.arange(NP_), np.arange(NP_))
    c["pdft"] = np.concatenate([pc, psn, pc.T / NP_, psn.T / NP_], 1).astype(np.float32)
    feat = []
    for length in (NP_, NL):
        t = np.linspace(0.0, 1.0, length)[None]
        wpos = 2.0 * math.pi * np.arange(length)[None] / length
        fr = np.linspace(1e-4, 15, 16)[:, None]
        feat.append(np.concatenate([t, np.cos(fr * wpos), -np.sin(fr * wpos)], 0))
    c["feat"] = np.concatenate(feat, 1).astype(np.float32)
    cols = [-(2 * (128 * (n % HKT) + p) + n // HKT) / (NL - 1) for n in range(8)] + [-p / (NP_ - 1)]
    c["steps"] = np.stack(cols, 1).astype(np.float32)
    lo, hi = math.log(1e-2) / 1.5, math.log(1e-2) / 0.3
    c["deltas"] = np.broadcast_to(np.abs(np.linspace(lo, hi, D))[None], (128, D)).astype(np.float32)
    return c


def kernel(**inputs):
    import numpy as _np
    import concourse.bacc as _bacc
    from concourse import mybir as _mybir
    from concourse.bass_utils import run_bass_kernel_spmd as _run

    nc = _bacc.Bacc("TRN2", target_bir_lowering=False, num_devices=1)
    f32 = _mybir.dt.float32
    arrays, A, consts, Y, scratch = {}, {}, {}, {}, {}
    for name in _INS:
        a = _np.ascontiguousarray(inputs[name])
        arrays[f"in_{name}"] = a
        A[name] = nc.dram_tensor(f"in_{name}", a.shape, f32, kind="ExternalInput").ap()
    for name, a in shape_constants().items():
        arrays[f"const_{name}"] = a
        consts[name] = nc.dram_tensor(f"const_{name}", a.shape, f32, kind="ExternalInput").ap()
    for name, shape in _OUTS:
        Y[name] = nc.dram_tensor(f"out_{name}", shape, f32, kind="ExternalOutput").ap()
    for name, shape in _SCRATCH:
        scratch[name] = nc.dram_tensor(f"scratch_{name}", shape, f32, kind="Internal").ap()
    build(nc, A, consts, Y, scratch)
    r = _run(nc, [arrays], core_ids=[0])
    return tuple(r.results[0][f"out_{name}"] for name, _ in _OUTS)
```

```python
import math
from contextlib import ExitStack

import numpy as np

import concourse.bass as bass
from concourse import mybir

F32 = mybir.dt.float32
ALU = mybir.AluOpType
ACT = mybir.ActivationFunctionType
AX = mybir.AxisListType
ds = bass.ds

D = 1024
KT = D // 128
ADA_FIRST = 4
NP_, NL = 128, 1024
T = NP_ + NL
TC = T // 3
PAST = 256
HEADS, DQ, DV = 8, 32, 64
AB_IN = 3328
RW_TILES = 14
FF = 2816
FT = FF // 128
C = 64
LAM_INIT = 0.2
GROUPS = ((0, NP_), (NP_, NL))

ROWS = [("ada_b", 96), ("norm1", 16), ("norm2", 16), ("final", 8), ("mu", 28), ("w0", 8), ("a0", 8),
        ("k_k", 4), ("k_a", 4), ("r_k", 4), ("ln_g", 4), ("ln_b", 4), ("b_in", 24), ("conv_w", 72),
        ("conv_b", 24), ("hbias", 16), ("b_out", 8), ("subln", 1)]
COL, _n = {}, 0
for _name, _rows in ROWS:
    COL[_name] = _n
    _n += _rows
PV_TILES = -(-_n // 128)

CBLK = [("ident", 128), ("blockones", 128), ("mask_f", 128), ("mask_b", 128), ("lt", 64), ("gt", 64),
        ("ident2", 64), ("scan", 256), ("rot", 128), ("nz", 1), ("pad", 7)]
CCOL, _n = {}, 0
for _name, _w in CBLK:
    CCOL[_name] = (_n, _w)
    _n += _w
CW = _n

X0, H0, BIG, WB, CST = 0, 9216, 18432, 43776, 47872
PV0 = CST + CW
MOD0 = PV0 + 128 * PV_TILES
ONE0 = MOD0 + 192
COEF0 = ONE0 + 128
SM0 = COEF0 + 16
RK0 = SM0 + 64
DIAG0 = RK0 + 512
END = DIAG0 + 2048


def trip(eng, n):
    return eng.Fori(0, n) if n > 1 else _Once()


class _Once:
    def __enter__(self):
        return 0

    def __exit__(self, *a):
        return False


class Kit:

    def __init__(self, nc, ctx, arena, psum):
        self.nc, self.ctx, self.arena, self.psum = nc, ctx, arena, psum
        self.sems = []
        self.X = self.tiles(X0, KT, T)
        self.H = self.tiles(H0, KT, T)
        self.ident = self.const("ident")
        self.ones = self.at(ONE0, 128)
        self.condS = self.at(SM0 + 40, 16)
        self.pv = self.at(PV0, 128 * PV_TILES)
        self.mod = self.at(MOD0, 192).rearrange("p (l m g) -> p l m g", l=2, g=2)

    def at(self, off, n):
        return self.arena[:, off:off + n]

    def tiles(self, off, n, w):
        return self.arena[:, off:off + n * w].rearrange("p (k n) -> p k n", k=n)

    def const(self, name):
        o, w = CCOL[name]
        return self.at(CST + o, w)

    def col(self, name, j=0, n=1):
        return self.pv[:, COL[name] + j:COL[name] + j + n]

    def ada_acc(self, j, g):
        return self.at(ADA_ACC0 + (2 * j + g) * 512, 512)

    def bank(self, b, n=512):
        return self.psum[:, b * 512:b * 512 + n]

    def sem(self, name):
        self.sems.append(self.nc.alloc_semaphore(name=name))
        return self.sems[-1]

    def reuse_semaphores(self):
        self.nc.clear_and_free_semaphores(self.sems)
        self.nc.all_engine_barrier()
        self.sems = []


def stage_setup(k, A, consts):
    nc = k.nc
    stg = k.tiles(WB, PV_TILES, 128)
    cond = k.at(WB + 1024, 128)
    condT = k.at(WB + 1200, 16)
    condS = k.condS
    NX = 4
    xin = [k.at(BIG + j * D, D) for j in range(NX)]
    slab = [k.tiles(BIG + NX * D + j * KT * 512, KT, 512) for j in range(ADA_FIRST)]
    ones_set, params_in, cond_in = k.sem("ones_set"), k.sem("params_in"), k.sem("cond_in")
    x_in = [k.sem(f"x_in{j}") for j in range(NX)]
    stg_zero, consts_in = k.sem("staging_zeroed"), k.sem("consts_in")
    par_t, par_c = k.sem("params_turned"), k.sem("params_copied")
    cond_s = k.sem("cond_silu")
    x_turned, x_copied = k.sem("x_turned"), k.sem("x_copied")
    slab_in = [k.sem(f"ada_slab_in{j}") for j in range(ADA_FIRST)]
    mod_ready, ada_weighed = k.sem("mod_ready"), k.sem("ada_weighed")
    ada = A["ada_w"].rearrange("l (k p) n -> p l k n", p=128)
    row_loads = [("ada_b", A["ada_b"].rearrange("l (m p) -> (l m) p", p=128), 96),
                 ("norm1", A["norm1_g"].rearrange("l (m p) -> (l m) p", p=128), 16),
                 ("norm2", A["norm2_g"].rearrange("l (m p) -> (l m) p", p=128), 16),
                 ("final", A["final_g"].rearrange("(m p) -> m p", p=128), 8),
                 ("mu", A["rwkv_mu"].rearrange("l d (m p) -> (l d m) p", p=128), 28),
                 ("w0", A["rwkv_w0"].rearrange("l d (m p) -> (l d m) p", p=128), 8),
                 ("a0", A["rwkv_a0"].rearrange("l d (m p) -> (l d m) p", p=128), 8),
                 ("k_k", A["rwkv_k_k"].rearrange("l (m p) -> (l m) p", p=128), 4),
                 ("k_a", A["rwkv_k_a"].rearrange("l (m p) -> (l m) p", p=128), 4),
                 ("r_k", A["rwkv_r_k"].rearrange("l (m h) p -> (l m) (h p)", h=2), 4),
                 ("ln_g", A["rwkv_ln_g"].rearrange("l (m p) -> (l m) p", p=128), 4),
                 ("ln_b", A["rwkv_ln_b"].rearrange("l (m p) -> (l m) p", p=128), 4),
                 ("b_in", A["hy_b_in"].rearrange("l (m p) -> (l m) p", p=128), 24),
                 ("conv_w", A["hy_conv_w"].rearrange("l j (m p) -> (l j m) p", p=128), 72),
                 ("conv_b", A["hy_conv_b"].rearrange("l (m p) -> (l m) p", p=128), 24),
                 ("hbias", A["hy_bias"].rearrange("l o (m p) -> (l o m) p", p=128), 16),
                 ("b_out", A["hy_b_out"].rearrange("l (m p) -> (l m) p", p=128), 8)]
    plan = []
    for name, src, n in row_loads:
        r, done = COL[name], 0
        while done < n:
            m = min(n - done, 128 - (r + done) % 128)
            plan.append(((r + done) // 128, (r + done) % 128, m, src[done:done + m, :]))
            done += m
    sub = COL["subln"]
    plan.append((sub // 128, sub % 128, 1, None))

    with nc.Block() as block:
        @block.sync
        def _(sp):
            sp.dma_start(k.at(CST, CW), consts["cblk"]).then_inc(consts_in, 16)
            x_tile = lambda t: A["x_prompt"][0] if t == 0 else A["x_sample"][0, (t - 1) * 128:t * 128, :]
            for t in range(NX):
                sp.dma_start(xin[t], x_tile(t)).then_inc(x_in[t], 16)
            sp.wait_ge(stg_zero, 1)
            for t, r, m, src in plan:
                if src is None:
                    for h in range(2):
                        sp.dma_start(stg[r:r + 1, t, h * DV:(h + 1) * DV], A["diff_subln_g"]).then_inc(params_in, 16)
                else:
                    sp.dma_start(stg[r:r + m, t, :], src).then_inc(params_in, 16)
            for t in range(NX, 9):
                sp.wait_ge(x_turned, 2 * (t - NX + 1))
                sp.dma_start(xin[t % NX], x_tile(t)).then_inc(x_in[t % NX], 16)

        n_loads = len(plan) + 1

        @block.tensor
        def _(pe):
            def turn_x(t):
                pe.wait_ge(x_in[t % NX], 16 * (t // NX + 1))
                for h in range(2):
                    b = (2 * t + h) % 4
                    if 2 * t + h >= 4:
                        pe.wait_ge(x_copied, 2 * t + h - 3)
                    for q in range(4):
                        kt = 4 * h + q
                        last = pe.transpose(k.bank(2 + b)[:, q * 128:(q + 1) * 128], xin[t % NX][:, kt * 128:(kt + 1) * 128], k.ident)
                    last.then_inc(x_turned, 1)

            pe.wait_ge(consts_in, 16)
            for t in range(NX):
                turn_x(t)
            pe.wait_ge(params_in, 16 * n_loads)
            pe.wait_ge(cond_in, 32)
            for t in range(PV_TILES):
                last = pe.transpose(k.bank(0)[:, t * 128:(t + 1) * 128], stg[:, t, :], k.ident)
            last = pe.transpose(k.bank(1)[:, 0:16], cond[0:16, :], k.ident[0:16, 0:16])
            last.then_inc(par_t, 1)
            for t in range(NX, 9):
                turn_x(t)
            for s in range(ADA_FIRST):
                pe.wait_ge(ada_weighed, s + 1)
                last = ada_sums(k, pe, [k.ada_acc(s % 2, g) for g in range(2)], k.bank(6)[:, 8 * s:8 * s + 8])
                last.then_inc(mod_ready, 1)

        @block.scalar
        def _(act):
            act.dma_start(cond[0:8, :], A["c_ctx"].rearrange("(m p) -> m p", p=128)).then_inc(cond_in, 16)
            act.dma_start(cond[8:16, :], A["c"].rearrange("b (m p) -> (b m) p", p=128)).then_inc(cond_in, 16)
            for s in range(ADA_FIRST):
                act.dma_start(slab[s], ada[:, 0, :, s * 512:(s + 1) * 512]).then_inc(slab_in[s], 16)
            act.wait_ge(par_t, 1)
            act.activation(condT[:, 0:16], k.bank(1)[:, 0:16], ACT.Sigmoid).then_inc(cond_s, 1)

        @block.vector
        def _(dve):
            dve.memset(stg[:, PV_TILES - 1, :], 0.0).then_inc(stg_zero, 1)
            dve.memset(k.ones, 1.0)
            def copy_x(t):
                for h in range(2):
                    n = 2 * t + h
                    dve.wait_ge(x_turned, n + 1)
                    dve.tensor_copy(k.X[:, 4 * h:4 * h + 4, t * 128:(t + 1) * 128],
                                    k.bank(2 + n % 4).rearrange("p (q n) -> p q n", q=4)).then_inc(x_copied, 1)
            for t in range(NX):
                copy_x(t)
            dve.wait_ge(par_t, 1)
            dve.tensor_copy(k.pv, k.bank(0)[:, 0:128 * PV_TILES])
            dve.wait_ge(cond_s, 1)
            dve.tensor_tensor(condS, k.bank(1)[:, 0:16], condT, ALU.mult).then_inc(cond_s, 1)
            for t in range(NX, 9):
                copy_x(t)
            dve.wait_ge(cond_s, 2)
            for s in range(ADA_FIRST):
                dve.wait_ge(slab_in[s], 16)
                if s >= 2:
                    dve.wait_ge(mod_ready, s - 1)
                ada_weigh(k, dve, slab[s], s % 2, range(KT)).then_inc(ada_weighed, 1)
            dve.wait_ge(mod_ready, ADA_FIRST)
            add_ada_bias(k, dve, 0, 4 * ADA_FIRST)


def ada_weigh(k, dve, slab, j, kts):
    for kt in kts:
        if kt:
            dve.drain()
        for g in range(2):
            acc, scale = k.ada_acc(j, g), k.condS[:, 8 * g + kt:8 * g + kt + 1]
            if kt:
                last = dve.scalar_tensor_tensor(out=acc, in0=slab[:, kt, :], scalar=scale, in1=acc, op0=ALU.mult, op1=ALU.add)
            else:
                last = dve.tensor_scalar(acc, slab[:, kt, :], scale, None, ALU.mult)
    return last


def ada_sums(k, pe, accs, out):
    for m in range(4):
        for g in range(2):
            last = pe.matmul(out[:, 2 * m + g:2 * m + g + 1], accs[g][:, m * 128:(m + 1) * 128], k.ones[:, 0:1], start=True, stop=True)
    return last


def add_ada_bias(k, dve, a, b):
    acc = k.bank(6)[:, 0:192].rearrange("p (n g) -> p n g", g=2)
    mod = k.mod.rearrange("p l m g -> p (l m) g")
    for g in range(2):
        dve.tensor_tensor(mod[:, a:b, g], acc[:, a:b, g], k.col("ada_b", a, b - a), ALU.add)


class Norm:

    def __init__(self, k, gain, layer, sub, dst, tag):
        self.k, self.gain, self.layer, self.sub, self.dst = k, gain, layer, sub, dst
        at = BIG + 18 * T
        self.sq, self.root, self.rstd = k.tiles(at, 2, T), k.at(at + 2 * T, T), k.at(at + 3 * T, T)
        self.coef = k.at(COEF0, 16).rearrange("p (m g) -> p m g", g=2)
        self.eps = k.at(SM0 + 1, 1)
        self.squares, self.summed, self.rooted = k.sem(f"{tag}_squares"), k.sem(f"{tag}_squares_summed"), k.sem(f"{tag}_root")
        self.scaled, self.set, self.ready = k.sem(f"{tag}_scaled"), k.sem(f"{tag}_coef"), k.sem(f"{tag}_chunk_ready")

    def tensor(self, pe):
        k = self.k
        for kt in range(KT):
            pe.wait_ge(self.squares, kt + 1)
            for tc in range(3):
                last = pe.matmul(k.bank(tc, TC), k.ones, self.sq[:, kt % 2, tc * TC:(tc + 1) * TC],
                                 start=(kt == 0), stop=(kt == KT - 1))
            last.then_inc(self.summed, 1)

    def scalar(self, act):
        k = self.k
        for kt in range(KT):
            if kt >= 2:
                act.wait_ge(self.summed, kt - 1)
            act.activation(self.sq[:, kt % 2, :], k.X[:, kt, :], ACT.Square).then_inc(self.squares, 1)
        act.wait_ge(self.summed, KT)
        act.wait_ge(self.set, 3)
        for tc in range(3):
            act.activation(self.root[:, tc * TC:(tc + 1) * TC], k.bank(tc, TC), ACT.Sqrt, bias=self.eps, scale=1.0 / D).then_inc(self.rooted, 1)
        for tc in range(3):
            for kt in range(KT):
                act.wait_ge(self.scaled, tc * KT + kt + 1)
                for g, c0, n in ((0, 0, NP_), (1, NP_, TC - NP_)) if tc == 0 else ((1, tc * TC, TC),):
                    v = self.dst[:, kt, c0:c0 + n]
                    if self.layer is None:
                        last = act.activation(v, v, ACT.Identity, scale=self.coef[:, kt, g:g + 1])
                    else:
                        last = act.activation(v, v, ACT.Identity, scale=self.coef[:, kt, g:g + 1],
                                              bias=k.mod[:, self.layer, 24 * self.sub + kt, g:g + 1])
            last.then_inc(self.ready, 1)

    def vector(self, dve):
        k = self.k
        dve.memset(self.eps, 1e-6).then_inc(self.set, 1)
        for g in range(2):
            if self.layer is None:
                dve.tensor_copy(self.coef[:, :, g], self.gain).then_inc(self.set, 1)
            else:
                dve.scalar_tensor_tensor(out=self.coef[:, :, g], in0=k.mod[:, self.layer, 24 * self.sub + 8:24 * self.sub + 16, g],
                                         scalar=1.0, in1=self.gain, op0=ALU.add, op1=ALU.mult).then_inc(self.set, 1)
        for tc in range(3):
            c = slice(tc * TC, (tc + 1) * TC)
            dve.wait_ge(self.rooted, tc + 1)
            dve.reciprocal(self.rstd[:, c], self.root[:, c])
            dve.drain()
            for kt in range(KT):
                dve.tensor_tensor(self.dst[:, kt, c], k.X[:, kt, c], self.rstd[:, c], ALU.mult).then_inc(self.scaled, 1)


def stage_norm(k, norm):
    with k.nc.Block() as block:
        @block.tensor
        def _(pe):
            norm.tensor(pe)

        @block.scalar
        def _(act):
            norm.scalar(act)

        @block.vector
        def _(dve):
            norm.vector(dve)


def stage_gemm(k, tag, src, n_k, wview, tiles, slab_at, evac, store=None, after=None, ada=None, ada_tiles=0, norm=None,
               x_from=None, src_from=(), x_to=None):
    nc = k.nc
    slab = [k.tiles(slab_at + j * n_k * 128, n_k, 128) for j in range(2)]
    slab_in = [k.sem(f"{tag}_slab_in{j}") for j in range(2)]
    acc_ready, acc_free = k.sem(f"{tag}_acc_ready"), k.sem(f"{tag}_acc_free")
    stored = [k.sem(f"{tag}_stored{j}") for j in range(2)] if store else None
    row_ready = k.sem(f"{tag}_row_ready") if after else None
    x_gone = k.sem(f"{tag}_x_stored")
    src_in, x_back = k.sem(f"{tag}_source_in"), k.sem(f"{tag}_x_back")
    n = tiles // 2
    n_ada = ada_tiles // 2
    assert not ada or n_ada in (n, n - 1)
    if ada:
        ada_w, ada_first = ada
        ada_slab = [k.tiles(at, KT, 512) for at in (KC0, V0)]
        ada_in = [k.sem(f"{tag}_ada_in{j}") for j in range(2)]
        ada_used, ada_weighed = k.sem(f"{tag}_ada_summed"), k.sem(f"{tag}_ada_weighed")
        accs = [[k.ada_acc(j, g) for g in range(2)] for j in range(2)]
    with nc.Block() as block:
        @block.sync
        def _(sp):
            for j in range(2):
                sp.dma_start(slab[j], wview[:, :, j * 128:(j + 1) * 128]).then_inc(slab_in[j], 16)
                if ada:
                    sp.dma_start(ada_slab[j], ada_w[:, :, j * 512:(j + 1) * 512]).then_inc(ada_in[j], 16)

            def load(i, with_ada):
                for j in range(2):
                    off = sp.snap((i * 2 + j) * 128)
                    used = sp.snap((i * 2 + (j - 1)) * 3)
                    if with_ada:
                        ada_off = sp.snap((i * 2 + j) * 512)
                        ada_free = sp.snap(i * 2 + (j - 1))
                    sp.wait_ge(acc_ready, used)
                    sp.dma_start(slab[j], wview[:, :, ds(off, 128)]).then_inc(slab_in[j], 16)
                    if with_ada:
                        sp.wait_ge(ada_weighed, ada_free)
                        sp.dma_start(ada_slab[j], ada_w[:, :, ds(ada_off, 512)]).then_inc(ada_in[j], 16)
            m = n_ada if ada else n
            with sp.Fori(1, m) as i:
                load(i, ada is not None)
            if m < n:
                for j in range(2):
                    sp.wait_ge(acc_ready, (m * 2 + j - 1) * 3)
                    sp.dma_start(slab[j], wview[:, :, (m * 2 + j) * 128:(m * 2 + j + 1) * 128]).then_inc(slab_in[j], 16)

        @block.tensor
        def _(pe):
            if norm:
                norm.tensor(pe)
            if src_from:
                pe.wait_ge(src_in, 16 * len(src_from))

            def products(i, with_ada):
                for j in range(2):
                    pe.wait_ge(slab_in[j], (i + 1) * 16)
                    for tc in range(3):
                        if norm and j == 0:
                            pe.wait_ge(norm.ready, tc + 1)
                        pe.wait_ge(acc_free, i * 6 + (j * 3 + tc + 1))
                        for kt in range(n_k):
                            last = pe.matmul(k.bank(tc, TC), slab[j][:, kt, :], src(kt)[:, tc * TC:(tc + 1) * TC],
                                             start=(kt == 0), stop=(kt == n_k - 1))
                        last.then_inc(acc_ready, 1)
                    if with_ada:
                        pe.wait_ge(ada_weighed, i * 2 + (j + 1))
                        ada_sums(k, pe, accs[j], k.psum[:, ds(i * 16 + (6 * 512 + 8 * (ada_first + j)), 8)]).then_inc(ada_used, 1)
            m = n_ada if ada else n
            with pe.Fori(0, m) as i:
                products(i, ada is not None)
            if m < n:
                products(m, False)

        @block.vector
        def _(dve):
            dve.sem_inc(acc_free, 3)
            if norm:
                norm.vector(dve)
            if x_from is not None:
                dve.wait_ge(x_back, 16)
            if ada:
                dve.sem_inc(ada_used, 2)

            def steps(i, with_ada):
                for j in range(2):
                    for tc in range(3):
                        if with_ada:
                            if tc == 0:
                                dve.wait_ge(ada_in[j], (i + 1) * 16)
                                dve.wait_ge(ada_used, i * 2 + (j + 1))
                            last = ada_weigh(k, dve, ada_slab[j], j, range(3 * tc, min(3 * tc + 3, KT)))
                            if tc == 2:
                                last.then_inc(ada_weighed, 1)
                        if store and not after and tc == 0:
                            dve.wait_ge(stored[j], i * 16 + 16)
                        dve.wait_ge(acc_ready, i * 6 + (j * 3 + tc + 1))
                        evac(dve, i * 2 + j, j, tc, k.bank(tc, TC)).then_inc(acc_free, 1)
                    if after:
                        dve.drain()
                        dve.wait_ge(stored[j], i * 16 + 16)
                        after(dve, i * 2 + j, j).then_inc(row_ready, 1)
            m = n_ada if ada else n
            with dve.Fori(0, m) as i:
                steps(i, ada is not None)
            if m < n:
                steps(m, False)

        if x_to is not None:
            @block.gpsimd
            def _(pool):
                pool.dma_start(x_to, k.at(X0, KT * T)).then_inc(x_gone, 16)
                pool.wait_ge(x_gone, 16)

        if x_from is not None:
            @block.scalar
            def _(act):
                for tile, there in src_from:
                    act.dma_start(tile, there).then_inc(src_in, 16)
                act.dma_start(k.at(X0, KT * T), x_from).then_inc(x_back, 16)

        if norm and not store:
            @block.scalar
            def _(act):
                norm.scalar(act)

        if store:
            @block.scalar
            def _(act):
                if norm:
                    norm.scalar(act)
                for j in range(2):
                    act.sem_inc(stored[j], 16)
                with act.Fori(0, n) as i:
                    for j in range(2):
                        dst, row = store(act, i * 2 + j, j)
                        if after:
                            done = act.snap(i * 2 + (j + 1))
                            act.wait_ge(row_ready, done)
                        else:
                            done = act.snap(i * 6 + (j * 3 + 6))
                            act.wait_ge(acc_free, done)
                        act.dma_start(dst, row).then_inc(stored[j], 16)
                for j in range(2):
                    act.wait_ge(stored[j], 16 * (n + 1))


def evac_residual(k, layer, sub, bias=None):
    def evac(dve, m, j, tc, acc):
        first = tc * TC
        spans = [(0, 0, NP_), (1, NP_, TC - NP_)] if tc == 0 else [(1, 0, TC)]
        for g, c0, n in spans:
            x = k.X[:, m, first + c0:first + c0 + n]
            gate = k.mod[:, layer, 24 * sub + 16 + m, g:g + 1]
            if bias is None:
                last = dve.scalar_tensor_tensor(out=x, in0=acc[:, c0:c0 + n], scalar=gate, in1=x, op0=ALU.mult, op1=ALU.add)
            else:
                tmp = k.at(WB + 2048 + 512 * (tc if g else 3), n)
                dve.tensor_scalar(tmp, acc[:, c0:c0 + n], k.pv[:, ds(m + bias, 1)], gate, ALU.add, ALU.mult)
                dve.drain()
                last = dve.tensor_tensor(x, tmp, x, ALU.add)
        return last
    return evac


def stage_ffn(k, A, layer, norm):
    nc = k.nc
    tag = f"ffn{layer}"
    act_t = k.tiles(BIG, FT, T)
    slab = {(w, j): k.tiles(WB + (2 * w + j) * 1024, KT, 128) for w in range(2) for j in range(2)}
    views = [A["ffn_w1"][layer].rearrange("(k p) n -> p k n", p=128), A["ffn_w3"][layer].rearrange("(k p) n -> p k n", p=128)]
    slab_in = {(w, j): k.sem(f"{tag}_w{2 * w + 1}_in{j}") for w in range(2) for j in range(2)}
    acc_ready, silu_ready, acc_free = k.sem(f"{tag}_acc_ready"), k.sem(f"{tag}_silu_ready"), k.sem(f"{tag}_acc_free")
    n = FT // 2
    with nc.Block() as block:
        @block.sync
        def _(sp):
            for j in range(2):
                for w in range(2):
                    sp.dma_start(slab[w, j], views[w][:, :, j * 128:(j + 1) * 128]).then_inc(slab_in[w, j], 16)
            with sp.Fori(1, n) as i:
                for j in range(2):
                    off = sp.snap((i * 2 + j) * 128)
                    used = sp.snap((i * 2 + (j - 1)) * 3)
                    sp.wait_ge(acc_ready, used)
                    for w in range(2):
                        sp.dma_start(slab[w, j], views[w][:, :, ds(off, 128)]).then_inc(slab_in[w, j], 16)

        @block.tensor
        def _(pe):
            norm.tensor(pe)
            with pe.Fori(0, n) as i:
                for j in range(2):
                    for w in range(2):
                        pe.wait_ge(slab_in[w, j], (i + 1) * 16)
                    for tc in range(3):
                        if j == 0:
                            pe.wait_ge(norm.ready, tc + 1)
                        pe.wait_ge(acc_free, i * 6 + (j * 3 + tc + 1))
                        for w in range(2):
                            for kt in range(KT):
                                last = pe.matmul(k.bank(3 * w + tc, TC), slab[w, j][:, kt, :], k.H[:, kt, tc * TC:(tc + 1) * TC],
                                                 start=(kt == 0), stop=(kt == KT - 1))
                        last.then_inc(acc_ready, 1)

        @block.scalar
        def _(act):
            norm.scalar(act)
            with act.Fori(0, n) as i:
                for j in range(2):
                    for tc in range(3):
                        act.wait_ge(acc_ready, i * 6 + (j * 3 + tc + 1))
                        act.activation(act_t[:, i * 2 + j, tc * TC:(tc + 1) * TC], k.bank(tc, TC), ACT.Silu).then_inc(silu_ready, 1)

        @block.vector
        def _(dve):
            dve.sem_inc(acc_free, 3)
            norm.vector(dve)
            with dve.Fori(0, n) as i:
                for j in range(2):
                    for tc in range(3):
                        dve.wait_ge(silu_ready, i * 6 + (j * 3 + tc + 1))
                        v = act_t[:, i * 2 + j, tc * TC:(tc + 1) * TC]
                        dve.tensor_tensor(v, k.bank(3 + tc, TC), v, ALU.mult).then_inc(acc_free, 1)

    stage_gemm(k, tag + "_down", lambda kt: act_t[:, kt, :], FT, A["ffn_w2"][layer].rearrange("(k p) n -> p k n", p=128),
               KT, H0, evac_residual(k, layer, 1))


def stage_out(k, A, Y, rows=None):
    nc = k.nc
    row = [k.at(BIG + 4 * T + j * D, D) for j in range(2)]
    turned, copied = k.sem("y_turned"), k.sem("y_copied")
    stored = [k.sem(f"y_stored{j}") for j in range(2)]
    with nc.Block() as block:
        @block.tensor
        def _(pe):
            for n in range(18):
                if n >= 4:
                    pe.wait_ge(copied, n - 3)
                for q in range(4):
                    last = pe.transpose(k.bank(n % 4)[:, q * 128:(q + 1) * 128], k.H[:, 4 * (n % 2) + q, (n // 2) * 128:(n // 2 + 1) * 128], k.ident)
                last.then_inc(turned, 1)

        @block.vector
        def _(dve):
            for n in range(18):
                t = n // 2
                dve.wait_ge(turned, n + 1)
                if t >= 2 and n % 2 == 0:
                    dve.wait_ge(stored[t % 2], 16 * (t // 2))
                dve.tensor_copy(row[t % 2][:, (n % 2) * 512:(n % 2 + 1) * 512], k.bank(n % 4)).then_inc(copied, 1)

        @block.sync
        def _(sp):
            for t in range(9):
                sp.wait_ge(copied, 2 * t + 2)
                dst = Y["y_prompt"][0] if t == 0 else Y["y_sample"][0, (t - 1) * 128:t * 128, :]
                sp.dma_start(dst, row[t % 2]).then_inc(stored[t % 2], 16)
            for j in range(2):
                sp.wait_ge(stored[j], 16 * (5 - j))

QK0, KC0, V0, RW0 = BIG, BIG + 9216, BIG + 14336, BIG + 19968
ADA_ACC0 = BIG + 22272
OA0 = BIG + 19968
PKT = (PAST + NL) // 128


def stage_project(k, A, Y, scratch, norm):
    nc = k.nc
    w = A["ab_w_in"][0].rearrange("(k p) n -> p k n", p=128)
    ada = A["ada_w"].rearrange("l (k p) n -> p l k n", p=128)
    qk = k.tiles(QK0, 8, T)
    stage_gemm(k, "qk", lambda kt: k.H[:, kt, :], KT, w[:, :, 0:1024], 8, WB,
               lambda dve, m, j, tc, acc: dve.tensor_copy(qk[:, m, tc * TC:(tc + 1) * TC], acc),
               ada=(ada[:, 0, :, ADA_FIRST * 512:6 * D], ADA_FIRST), ada_tiles=12 - ADA_FIRST, norm=norm)
    ring = k.tiles(RW0, 2, T)
    rw_d = scratch["rw_d"]
    stage_gemm(k, "rw", lambda kt: k.H[:, kt, :], KT, w[:, :, 1536:AB_IN], RW_TILES, WB,
               lambda dve, m, j, tc, acc: dve.tensor_copy(ring[:, j, tc * TC:(tc + 1) * TC], acc),
               store=lambda act, m, j: (rw_d[ds(m, 1), :, :].rearrange("m p t -> (m p) t"), ring[:, j, :]),
               ada=(ada[:, 1, :, :], 12), ada_tiles=12, x_to=scratch["x_d"])
    wv = k.tiles(KC0, KT, 512)
    v = k.tiles(V0, PKT + 1, 512)
    wv_in, v_ready, v_copied = k.sem("wv_in"), k.sem("v_ready"), k.sem("v_copied")
    ctx_v_in, newv = k.sem("ctx_v_in"), k.sem("new_v_stored")
    with nc.Block() as block:
        @block.sync
        def _(sp):
            sp.dma_start(wv, w[:, :, 1024:1536]).then_inc(wv_in, 16)
            for t in range(PAST // 128):
                sp.dma_start(v[:, t, :].rearrange("p (h d) -> p h d", h=HEADS),
                             A["cache_diff_v"][0, 0, :, t * 128:(t + 1) * 128, :].rearrange("h p d -> p h d")).then_inc(ctx_v_in, 16)
            sp.wait_ge(v_copied, 1)
            sp.dma_start(Y["new_v"][0, 0].rearrange("h p d -> p h d"),
                         v[:, PKT, :].rearrange("p (h d) -> p h d", h=HEADS)).then_inc(newv, 16)
            sp.wait_ge(newv, 16)
            sp.wait_ge(ctx_v_in, 32)

        @block.tensor
        def _(pe):
            pe.wait_ge(wv_in, 16)
            for t in range(9):
                if t >= 2:
                    pe.wait_ge(v_copied, t - 1)
                for kt in range(KT):
                    last = pe.matmul(k.bank(t % 2), k.H[:, kt, t * 128:(t + 1) * 128], wv[:, kt, :],
                                     start=(kt == 0), stop=(kt == KT - 1))
                last.then_inc(v_ready, 1)

        @block.vector
        def _(dve):
            add_ada_bias(k, dve, 4 * ADA_FIRST, 96)
            for t in range(9):
                dve.wait_ge(v_ready, t + 1)
                at = PKT if t == 0 else PAST // 128 + t - 1
                dve.tensor_copy(v[:, at, :], k.bank(t % 2)).then_inc(v_copied, 1)


def stage_keys(k, A, Y, consts):
    nc = k.nc
    qk, kc = k.tiles(QK0, 8, T), k.tiles(KC0, 4, PAST + NL)
    cos, sin = k.at(H0, NL), k.at(H0 + NL, NL)
    cosp = [k.at(H0 + 2 * NL + j * 512, 512) for j in range(2)]
    sinp = [k.at(H0 + 3 * NL + j * 512, 512) for j in range(2)]
    rows = k.tiles(H0 + 4 * NL, 2, 512)
    newk = k.at(H0 + 5 * NL, 512)
    lam_row, lam_p = k.at(H0 + 6 * NL, 128), k.at(H0 + 6 * NL + 128, 64)
    nlam = k.at(SM0, 1)
    lam_e, lam_s = k.at(SM0 + 2, 2), k.at(SM0 + 4, 2)
    tab_in, row_in, lam_in = k.sem("rope_in"), k.sem("key_rows_in"), k.sem("lambda_in")
    turned, copied = k.sem("keys_turned"), k.sem("keys_copied")
    rot_ready, cos_ready, roped = k.sem("rot_ready"), k.sem("cos_ready"), k.sem("roped")
    sin_ready = k.sem("sin_ready")
    lam_bc, lam_dot, lam_exp = k.sem("lambda_rows"), k.sem("lambda_dot"), k.sem("lambda_exp")
    nk_out = k.sem("new_k_stored")
    units = [(m, h) for m in range(8) for h in range(2)]
    with nc.Block() as block:
        @block.sync
        def _(sp):
            sp.dma_start(cos, consts["rope"][0]).then_inc(tab_in, 16)
            sp.dma_start(sin, consts["rope"][1]).then_inc(tab_in, 16)
            for t in range(2):
                sp.dma_start(rows[:, t, :].rearrange("p (g d) -> p g d", g=16),
                             A["cache_diff_k"][0, 0, :, :, t * 128:(t + 1) * 128, :].rearrange("h m p d -> p (h m) d")).then_inc(row_in, 16)
            sp.dma_start(lam_row[0:1, :], A["diff_lambda"].rearrange("l a b -> l (a b)")).then_inc(lam_in, 16)
            sp.wait_ge(copied, 3)
            sp.dma_start(Y["new_k"][0, 0].rearrange("h m p d -> p (h m) d"), newk.rearrange("p (g d) -> p g d", g=16)).then_inc(nk_out, 16)
            sp.wait_ge(nk_out, 16)

        @block.tensor
        def _(pe):
            pe.wait_ge(row_in, 32)
            for t in range(2):
                for q in range(4):
                    last = pe.transpose(k.bank(t)[:, q * 128:(q + 1) * 128], rows[:, t, q * 128:(q + 1) * 128], k.ident)
                last.then_inc(turned, 1)
            for q in range(4):
                last = pe.transpose(k.bank(2)[:, q * 128:(q + 1) * 128], qk[:, 4 + q, 0:NP_], k.ident)
            last.then_inc(turned, 1)
            pe.wait_ge(lam_in, 16)
            pe.matmul(k.bank(3)[:, 0:128], k.ones[0:1, :], lam_row[0:1, :], start=True, stop=True).then_inc(lam_bc, 1)
            for n, (m, h) in enumerate(units):
                if n >= 2:
                    pe.wait_ge(sin_ready, n - 1)
                pe.matmul(k.bank(4 + n % 2), k.const("rot"), qk[:, m, NP_ + 512 * h:NP_ + 512 * (h + 1)],
                          start=True, stop=True).then_inc(rot_ready, 1)

        @block.gpsimd
        def _(pool):
            pool.wait_ge(tab_in, 32)
            for n, (m, h) in enumerate(units):
                if n >= 2:
                    pool.wait_ge(roped, n - 1)
                pool.tensor_tensor(cosp[n % 2], qk[:, m, NP_ + 512 * h:NP_ + 512 * (h + 1)], cos[:, 512 * h:512 * (h + 1)],
                                   ALU.mult).then_inc(cos_ready, 1)

        @block.scalar
        def _(act):
            act.wait_ge(lam_dot, 2)
            act.activation(lam_e, lam_s, ACT.Exp).then_inc(lam_exp, 1)

        @block.vector
        def _(dve):
            for t in range(2):
                dve.wait_ge(turned, t + 1)
                dve.tensor_copy(kc[:, :, t * 128:(t + 1) * 128], k.bank(t).rearrange("p (q n) -> p q n", q=4)).then_inc(copied, 1)
            dve.wait_ge(turned, 3)
            dve.tensor_copy(newk, k.bank(2)).then_inc(copied, 1)
            dve.wait_ge(lam_bc, 1)
            dve.tensor_copy(lam_row, k.bank(3)[:, 0:128])
            dve.drain()
            lv = lam_row.rearrange("p (a b c) -> p a b c", a=2, b=2)
            dve.tensor_tensor(lam_p.rearrange("p (a c) -> p a c", a=2), lv[:, :, 0, :], lv[:, :, 1, :], ALU.mult).then_inc(lam_dot, 1)
            dve.wait_ge(lam_dot, 1)
            dve.tensor_reduce(lam_s, lam_p.rearrange("p (a c) -> p a c", a=2), AX.X, ALU.add).then_inc(lam_dot, 1)
            dve.wait_ge(lam_exp, 1)
            dve.tensor_scalar(nlam, lam_e[:, 1:2], lam_e[:, 0:1], -LAM_INIT, ALU.subtract, ALU.add)
            dve.wait_ge(tab_in, 32)
            for n, (m, h) in enumerate(units):
                dve.wait_ge(rot_ready, n + 1)
                dve.tensor_tensor(sinp[n % 2], k.bank(4 + n % 2), sin[:, 512 * h:512 * (h + 1)], ALU.mult).then_inc(sin_ready, 1)
                dve.wait_ge(sin_ready, n + 1)
                dve.wait_ge(cos_ready, n + 1)
                dst = qk[:, m, NP_ + 512 * h:NP_ + 512 * (h + 1)] if m < 4 else kc[:, m - 4, PAST + 512 * h:PAST + 512 * (h + 1)]
                dve.tensor_tensor(dst, sinp[n % 2], cosp[n % 2], ALU.add).then_inc(roped, 1)


def stage_attend(k, latent):
    nc = k.nc
    tag = "lat" if latent else "ctx"
    qk, kc, v = k.tiles(QK0, 8, T), k.tiles(KC0, 4, PAST + NL), k.tiles(V0, PKT + 1, 512)
    oa = k.tiles(OA0, 4, T)
    steps, nkt, vt0, q0 = (NL // 128, PKT, 0, NP_) if latent else (1, 1, PKT, 0)
    nk = nkt * 128
    spans = [(c, min(512, nk - c)) for c in range(0, nk, 512)]
    groups = [range(g, min(g + 4, nkt)) for g in range(0, nkt, 4)]
    NG = len(groups)
    prob = [[k.at(H0 + (2 * b + m) * 1280, nk) for m in range(2)] for b in range(2)]
    pt = [k.tiles(H0 + 5120 + b * 1280, nkt, 128) for b in range(2)]
    qz = k.tiles(WB, 16, 128)
    st = k.at(SM0 + 8, 16)
    nmax, rsum, rcp = st[:, 0:4], st[:, 4:8], st[:, 8:12]
    nlam = k.at(SM0, 1)
    S = lambda name: k.sem(f"{tag}_{name}")
    q_zeroed, qs_ready, score_ready, max_ready, exp_done = S("q_zeroed"), S("q_scaled"), S("scores"), S("max"), S("exp")
    p_ready, turned, pt_copied, pv_ready, oa_done = S("probs"), S("turned"), S("turned_copied"), S("pv"), S("out_copied")

    def keys(h, m, c, n):
        src = kc[:, h // 2, c:c + n] if latent else qk[:, 4 + h // 2, c:c + n]
        return qz[:, 2 * h + m, :], src

    with nc.Block() as block:
        @block.tensor
        def _(pe):
            def score(i, h, m, span):
                c, n = spans[span]
                if span == 0:
                    pe.wait_ge(exp_done, i * 16 + (2 * h + m + 1))
                last = pe.matmul(k.psum[:, 1536 * m + c:1536 * m + c + n], *keys(h, m, c, n), start=True, stop=True)
                if span == len(spans) - 1:
                    last.then_inc(score_ready, 1)

            def scores(i, h, m):
                for span in range(len(spans)):
                    score(i, h, m, span)

            def turn_and_weigh(i, h, next_scores):
                pe.wait_ge(p_ready, i * 8 + (h + 1))

                def weigh(g):
                    pe.wait_ge(pt_copied, i * 8 * NG + (h * NG + g + 1 + 1))
                    if h == 0 and g == 0:
                        pe.wait_ge(oa_done, i + 1)
                    for kt in groups[g]:
                        last = pe.matmul(k.bank(7)[64 * (h % 2):64 * (h % 2) + 64, (h // 2) * 128:(h // 2 + 1) * 128],
                                         v[:, vt0 + kt, h * DV:(h + 1) * DV], pt[h % 2][:, kt, :],
                                         start=(kt == 0), stop=(kt == nkt - 1))
                    return last
                for g, tiles in enumerate(groups):
                    pe.wait_ge(pt_copied, i * 8 * NG + (h * NG + g + 1))
                    for n, kt in enumerate(tiles):
                        last = pe.transpose(k.bank(6)[:, n * 128:(n + 1) * 128], prob[h % 2][0][:, kt * 128:(kt + 1) * 128], k.ident)
                    last.then_inc(turned, 1)
                    if next_scores:
                        score(i, next_scores, 0, g)
                    if g:
                        weigh(g - 1)
                last = weigh(NG - 1)
                if h == HEADS - 1:
                    last.then_inc(pv_ready, 1)

            with trip(pe, steps) as i:
                pe.wait_ge(qs_ready, i + 1)
                scores(i, 0, 0)
                for h in range(HEADS):
                    scores(i, h, 1)
                    if h == 0:
                        scores(i, 1, 0)
                    else:
                        turn_and_weigh(i, h - 1, h + 1 if h + 1 < HEADS else None)
                turn_and_weigh(i, HEADS - 1, None)

        @block.scalar
        def _(act):
            act.sem_inc(exp_done, 2)
            act.sem_inc(pt_copied, 1)
            act.sem_inc(oa_done, 1)

            def copies(i, h, some):
                for g, tiles in some:
                    act.wait_ge(turned, i * 8 * NG + (h * NG + g + 1))
                    n = len(tiles)
                    act.activation(pt[h % 2][:, tiles[0]:tiles[0] + n, :],
                                   k.bank(6)[:, 0:n * 128].rearrange("p (n q) -> p n q", n=n), ACT.Copy).then_inc(pt_copied, 1)

            def exps(i, h, m):
                at = 2 * (h % 2) + m
                act.wait_ge(max_ready, i * 16 + (2 * h + m + 1))
                act.activation(prob[h % 2][m], k.psum[:, 1536 * m:1536 * m + nk], ACT.Exp, bias=nmax[:, at:at + 1],
                               accum_out=rsum[:, at:at + 1]).then_inc(exp_done, 1)

            act.wait_ge(q_zeroed, 1)
            with trip(act, steps) as i:
                for b in range(4):
                    rows = slice(32 * b, 32 * b + 32)
                    q = qk[rows, 0:4, ds(i * 128 + q0, 128)] if latent else qk[rows, 0:4, 0:128]
                    last = act.activation(qz[rows, b::4, :], q, ACT.Copy, scale=DQ ** -0.5)
                last.then_inc(qs_ready, 1)
                exps(i, 0, 0)
                for h in range(HEADS):
                    if h:
                        copies(i, h - 1, list(enumerate(groups))[:1])
                    exps(i, h, 1)
                    if h:
                        copies(i, h - 1, list(enumerate(groups))[1:])
                    if h + 1 < HEADS:
                        exps(i, h + 1, 0)
                copies(i, HEADS - 1, list(enumerate(groups)))
                act.wait_ge(pv_ready, i + 1)
                dst = oa[:, :, ds(i * 128 + q0, 128)] if latent else oa[:, :, 0:128]
                act.activation(dst, k.bank(7).rearrange("p (t n) -> p t n", t=4), ACT.Copy).then_inc(oa_done, 1)

        @block.vector
        def _(dve):
            dve.memset(qz, 0.0).then_inc(q_zeroed, 1)

            def maximum(i, h, m):
                dve.wait_ge(score_ready, i * 16 + (2 * h + m + 1))
                dve.tensor_reduce(nmax[:, 2 * (h % 2) + m:2 * (h % 2) + m + 1], k.psum[:, 1536 * m:1536 * m + nk], AX.X, ALU.max,
                                  negate=True).then_inc(max_ready, 1)

            def combine(i, h):
                b = 2 * (h % 2)
                dve.wait_ge(exp_done, i * 16 + (2 * h + 4))
                dve.reciprocal(rcp[:, b:b + 2], rsum[:, b:b + 2])
                dve.drain()
                dve.tensor_scalar(rcp[:, b + 1:b + 2], rcp[:, b + 1:b + 2], nlam, None, ALU.mult)
                dve.tensor_scalar(prob[h % 2][0], prob[h % 2][0], rcp[:, b:b + 1], None, ALU.mult)
                dve.drain()
                dve.scalar_tensor_tensor(out=prob[h % 2][0], in0=prob[h % 2][1], scalar=rcp[:, b + 1:b + 2],
                                         in1=prob[h % 2][0], op0=ALU.mult, op1=ALU.add).then_inc(p_ready, 1)

            with trip(dve, steps) as i:
                maximum(i, 0, 0)
                for h in range(HEADS):
                    if h:
                        combine(i, h - 1)
                    maximum(i, h, 1)
                    if h + 1 < HEADS:
                        maximum(i, h + 1, 0)
                combine(i, HEADS - 1)


def stage_head_norm(k):
    nc = k.nc
    oa = k.tiles(OA0, 4, T)
    sq, root, rcp = k.tiles(H0, 4, T), k.at(H0 + 4 * T, T), k.at(H0 + 5 * T, T)
    eps, gain = k.at(SM0 + 1, 1), k.at(SM0 + 6, 1)
    sq_ready, sum_ready, rooted, inv = k.sem("hn_squares"), k.sem("hn_sums"), k.sem("hn_root"), k.sem("hn_inverse")
    eps_set, normed = k.sem("hn_eps"), k.sem("hn_normed")
    with nc.Block() as block:
        @block.scalar
        def _(act):
            for t in range(4):
                act.activation(sq[:, t, :], oa[:, t, :], ACT.Square).then_inc(sq_ready, 1)
            act.wait_ge(eps_set, 2)
            for t in range(4):
                act.wait_ge(sum_ready, t + 1)
                if t:
                    act.wait_ge(inv, t)
                for tc in range(3):
                    last = act.activation(root[:, tc * TC:(tc + 1) * TC], k.bank(3 * (t % 2) + tc, TC), ACT.Sqrt, bias=eps, scale=1.0 / DV)
                last.then_inc(rooted, 1)

        @block.tensor
        def _(pe):
            for t in range(4):
                pe.wait_ge(sq_ready, t + 1)
                if t >= 2:
                    pe.wait_ge(rooted, t - 1)
                for tc in range(3):
                    last = pe.matmul(k.bank(3 * (t % 2) + tc, TC), k.const("blockones"), sq[:, t, tc * TC:(tc + 1) * TC], start=True, stop=True)
                last.then_inc(sum_ready, 1)

        @block.vector
        def _(dve):
            dve.memset(eps, 1e-5).then_inc(eps_set, 1)
            dve.tensor_scalar(gain, k.col("subln"), 1.0 - LAM_INIT, None, ALU.mult).then_inc(eps_set, 1)
            dve.wait_ge(eps_set, 2)
            for t in range(4):
                dve.wait_ge(rooted, t + 1)
                if t:
                    dve.wait_ge(normed, t)
                dve.reciprocal(rcp, root).then_inc(inv, 1)
                dve.wait_ge(inv, t + 1)
                dve.scalar_tensor_tensor(out=oa[:, t, :], in0=oa[:, t, :], scalar=gain, in1=rcp,
                                         op0=ALU.mult, op1=ALU.mult).then_inc(normed, 1)




RS0, KK0, YA0, Z1, Z2 = 0, 16128, 20736, 25344, 43008
U = 8
DECAY = -math.exp(-0.5)


class Steps:

    def __init__(self, sem, names, ahead=()):
        self.sem, self.names, self.per = sem, list(names), len(names)
        self.last_names = [n for n in names if n not in ahead]

    def start(self, eng):
        eng.sem_inc(self.sem, self.per)

    def here(self, i, name, last=False):
        names = self.last_names if last else self.names
        return i * self.per + (self.per + names.index(name) + 1)

    def before(self, i, name):
        return i * self.per + (self.names.index(name) + 1)


def rwkv_bufs(k):
    b, at = {}, Z1
    for name, n in [("sw", 512), ("sa", 512), ("L", 512), ("Lx", 512), ("e1", 512), ("e0", 512), ("ei", 512),
                    ("kd", 512), ("bon", 512), ("bkt", 1024), ("uv", 1024), ("g", 2048), ("m", 512), ("xm", 1024),
                    ("tmp", 512), ("tmp2", 512), ("st", 1024), ("vc", 512), ("lc", 128)]:
        b[name] = k.at(at, n)
        at += n
    assert at <= OA0
    at = Z2
    for name, n in [("wu", 1024), ("ar", 1024), ("bk", 1024), ("w1", 512), ("s", 512)]:
        b[name] = k.at(at, n)
        at += n
    assert at <= CST
    return b


def stage_rwkv_pre(k, A, scratch):
    nc = k.nc
    rs, kk, ya = k.tiles(RS0, RW_TILES, T), k.tiles(KK0, 4, T), k.tiles(YA0, 4, T)
    NR = 7
    raw = k.tiles(Z1, NR, T)
    c0 = k.at(Z1 + 8 * T, RW_TILES)
    sq, root = k.tiles(Z1 + 3 * T, 2, T), k.tiles(Z1 + 5 * T, 2, T)
    b = rwkv_bufs(k)
    wu = b["wu"].rearrange("p (d n) -> p d n", d=2)
    rk = k.at(RK0, 512).rearrange("p (m n) -> p m n", m=4)
    raw_in, wu_in = [k.sem(f"raw_in{j}") for j in range(NR)], k.sem("wu_in")
    c0_set, scaled, shifted = k.sem("c0_set"), k.sem("raw_scaled"), k.sem("raw_shifted")
    kk_raw, kk_sq, kk_sum, kk_root, kk_inv = (k.sem(f"kk_{n}") for n in ("raw", "squares", "sums", "root", "inverse"))
    with nc.Block() as block:
        @block.sync
        def _(sp):
            for j in range(NR):
                sp.dma_start(raw[:, j, :], scratch["rw_d"][j]).then_inc(raw_in[j], 16)
            for d in range(2):
                sp.dma_start(wu[0:64, d, :], A["rwkv_w_up"][0, d]).then_inc(wu_in, 16)
                sp.dma_start(wu[64:128, d, :], A["rwkv_a_up"][0, d]).then_inc(wu_in, 16)
            for m in range(NR, RW_TILES):
                sp.wait_ge(shifted, m - NR + 1)
                sp.dma_start(raw[:, m - NR, :], scratch["rw_d"][m]).then_inc(raw_in[m - NR], 16)
            sp.wait_ge(wu_in, 64)

        @block.scalar
        def _(act):
            act.wait_ge(c0_set, 2)
            with act.Fori(0, RW_TILES // NR) as i:
                for j in range(NR):
                    act.wait_ge(raw_in[j], i * 16 + 16)
                    act.activation(rs[:, i * NR + j, :], raw[:, j, :], ACT.Copy, scale=c0[:, ds(i * NR + j, 1)]).then_inc(scaled, 1)
            act.wait_ge(shifted, RW_TILES)
            act.activation(rs[0:64, 12, :], rs[0:64, 12, :], ACT.Tanh)
            act.activation(rs[:, 13, :], rs[:, 13, :], ACT.Sigmoid)
            for t in range(4):
                if t >= 2:
                    act.wait_ge(kk_sum, t - 1)
                act.wait_ge(kk_raw, t + 1)
                act.activation(sq[:, t % 2, :], kk[:, t, :], ACT.Square).then_inc(kk_sq, 1)
            for t in range(4):
                act.wait_ge(kk_sum, t + 1)
                if t >= 2:
                    act.wait_ge(kk_inv, t - 1)
                for tc in range(3):
                    last = act.activation(root[:, t % 2, tc * TC:(tc + 1) * TC], k.bank(3 * (t % 2) + tc, TC), ACT.Sqrt)
                last.then_inc(kk_root, 1)

        @block.tensor
        def _(pe):
            for t in range(4):
                pe.wait_ge(kk_sq, t + 1)
                if t >= 2:
                    pe.wait_ge(kk_root, t - 1)
                for tc in range(3):
                    last = pe.matmul(k.bank(3 * (t % 2) + tc, TC), k.const("blockones"), sq[:, t % 2, tc * TC:(tc + 1) * TC], start=True, stop=True)
                last.then_inc(kk_sum, 1)

        @block.vector
        def _(dve):
            mu = k.col("mu", 0, 28)
            dve.tensor_tensor(c0, mu[:, 0:14], mu[:, 14:28], ALU.add).then_inc(c0_set, 1)
            dve.wait_ge(c0_set, 1)
            dve.tensor_scalar(c0, c0, -1.0, 1.0, ALU.mult, ALU.add).then_inc(c0_set, 1)
            for t in range(4):
                dve.tensor_scalar(rk[:, t, :], k.const("blockones"), k.col("r_k", t), None, ALU.mult)
            with dve.Fori(0, RW_TILES // NR) as i:
                for j in range(NR):
                    dve.wait_ge(scaled, i * NR + (j + 1))
                    for g, (a, n) in enumerate(GROUPS):
                        dve.scalar_tensor_tensor(out=rs[:, i * NR + j, a + 1:a + n], in0=raw[:, j, a:a + n - 1],
                                                 scalar=k.pv[:, ds(i * NR + (j + COL["mu"]), 1)],
                                                 in1=rs[:, i * NR + j, a + 1:a + n], op0=ALU.mult, op1=ALU.add)
                    dve.drain()
                    for g, (a, n) in enumerate(GROUPS):
                        last = dve.scalar_tensor_tensor(out=rs[:, i * NR + j, a:a + n - 1], in0=raw[:, j, a + 1:a + n],
                                                        scalar=k.pv[:, ds(i * NR + (j + COL["mu"] + 14), 1)],
                                                        in1=rs[:, i * NR + j, a:a + n - 1], op0=ALU.mult, op1=ALU.add)
                    last.then_inc(shifted, 1)
            dve.wait_ge(shifted, RW_TILES)
            for t in range(4):
                dve.tensor_scalar(kk[:, t, :], rs[:, 4 + t, :], k.col("k_k", t), None, ALU.mult).then_inc(kk_raw, 1)
            for t in range(4):
                dve.wait_ge(kk_root, t + 1)
                dve.tensor_scalar(root[:, t % 2, :], root[:, t % 2, :], 1e-12, None, ALU.max)
                dve.drain()
                dve.reciprocal(root[:, t % 2, :], root[:, t % 2, :])
                dve.drain()
                dve.tensor_tensor(kk[:, t, :], kk[:, t, :], root[:, t % 2, :], ALU.mult).then_inc(kk_inv, 1)
            dve.memset(k.at(YA0, 4 * T), 0.0)


def stage_rwkv(k, A, Y, latent):
    nc = k.nc
    tag = "rl" if latent else "rc"
    first, tokens = GROUPS[1] if latent else GROUPS[0]
    chunks = tokens // C
    rs, kk, ya = k.tiles(RS0, RW_TILES, T), k.tiles(KK0, 4, T), k.tiles(YA0, 4, T)
    b = rwkv_bufs(k)
    u64 = lambda v: v.rearrange("p (u t) -> p u t", t=C)
    sw, sa, L, Lx, e1, e0, ei, kd, bon, m, tmp, tmp2, vc, lc, w1, s = (u64(b[n]) for n in (
        "sw", "sa", "L", "Lx", "e1", "e0", "ei", "kd", "bon", "m", "tmp", "tmp2", "vc", "lc", "w1", "s"))
    bkt, uv = u64(b["bkt"]), u64(b["uv"])
    ar, bk, xm, g = (b[n].rearrange("p (u t) -> p u t", t=2 * C) for n in ("ar", "bk", "xm", "g"))
    st = u64(b["st"])
    wu = b["wu"].rearrange("p (d n) -> p d n", d=2)
    rk = k.at(RK0, 512).rearrange("p (m n) -> p m n", m=4)
    m_diag, t_diag = k.tiles(DIAG0, U, 128), k.tiles(DIAG0 + U * 128, U, 128)
    id2, ident = k.const("ident2"), k.ident
    pb = lambda bank, n=1: k.psum[:, bank * 512:(bank + n) * 512]
    half = lambda h: slice(64 * h, 64 * h + 64)
    units = [(u, h) for u in range(U) for h in range(2)]
    of_direction = lambda d: [(u, h) for u in range(4 * d, 4 * d + 4) for h in range(2)]
    turned = lambda bank, u, h: pb(bank + u // 4)[half(h), (u % 4) * C:(u % 4 + 1) * C]
    slot = lambda u, h: 8 * h + u
    b_cols = lambda h: slice(64 * (1 - h), 64 * (1 - h) + 64)
    k_cols = lambda h: slice(64 * h, 64 * h + 64)
    lvl = range(6)

    both = lambda name: [f"{name}_{d}" for d in range(2)]
    pe_s = Steps(k.sem(f"{tag}_pe_step"), ["vturn", "bonus", "n0", "gram", "bkt"] + both("level0") + ["lora"]
                 + [x for n in lvl[1:] for x in both(f"level{n}")] + both("w1") + both("u") + ["y", "s"], ["lora"])
    act_s = Steps(k.sem(f"{tag}_act_step"), ["vcopy", "bktcopy"] + both("m1") + both("m2") + both("m3") + both("m4") + both("m5")
                  + ["sig"] + both("w1") + both("ucopy") + ["exp"], ["sig", "exp"])
    dve_s = Steps(k.sem(f"{tag}_dve_step"), ["ark", "bonus", "n0", "gmask"] + both("x0") + ["bias"] + both("x1")
                  + both("x2") + both("x3") + both("x4") + both("x5") + ["logs", "bon", "s", "y"], ["bias", "logs", "bon"])
    pool_s = Steps(k.sem(f"{tag}_pool_step"), ["v0", "lora0", "v1", "copied"])
    pre_pool, pre_pe, pre_act, pre_dve = (k.sem(f"{tag}_first_{n}") for n in ("copies", "loras", "act_steps", "dve_steps"))
    end = k.at(SM0 + 24, 8).rearrange("p (u o) -> p u o", o=1)
    pe_passed = k.sem(f"{tag}_pe_waits_passed")
    st_in, st_turned, st_set, st_out = (k.sem(f"{tag}_{n}") for n in ("state_in", "state_turned", "state_set", "state_out"))
    fin_turned, fin_copied = k.sem(f"{tag}_final_turned"), k.sem(f"{tag}_final_copied")

    def cols(i, d, ahead=0):
        if d == 0:
            return ds(i * C + (first + ahead * C), C)
        return ds(i * (-C) + (first + tokens - C - ahead * C), C)

    def each_chunk(eng, step):
        with trip(eng, chunks - 1) as i:
            step(i, True)
        step(chunks - 1, False)

    with nc.Block() as block:
        @block.sync
        def _(sp):
            if latent:
                for d, n in enumerate(("state_rwkv_fwd", "state_rwkv_bwd")):
                    sp.dma_start(st[:, 4 * d:4 * d + 4, :], A[n][0, 0].rearrange("(p h) v c -> (h v) p c", h=2)).then_inc(st_in, 16)
            else:
                sp.wait_ge(fin_copied, 1)
                for d, n in enumerate(("new_f", "new_b")):
                    sp.dma_start(Y[n][0, 0].rearrange("(p h) v c -> (h v) p c", h=2), st[:, 4 * d:4 * d + 4, :]).then_inc(st_out, 16)
                sp.wait_ge(st_out, 32)

        @block.gpsimd
        def _(pool):
            def copies(i, ahead, done):
                for d in range(2):
                    pool.tensor_copy(vc[:, 4 * d:4 * d + 4, :], rs[:, 8:12, cols(i, d, ahead)]).then_inc(done, 1)
                    pool.tensor_copy(lc[:, d, :], rs[:, 12, cols(i, d, ahead)]).then_inc(done, 1)

            pool_s.start(pool)
            copies(0, 0, pre_pool)
            with trip(pool, chunks - 1) as i:
                pool.wait_ge(pe_s.sem, pe_s.here(i, "vturn"))
                pool.wait_ge(dve_s.sem, dve_s.here(i, "bonus"))
                copies(i, 1, pool_s.sem)

        @block.tensor
        def _(pe):
            pe_s.start(pe)
            if latent:
                pe.wait_ge(st_in, 32)
                for u, h in units:
                    last = pe.matmul(pb(7)[half(h), u * C:(u + 1) * C], st[half(h), u, :], id2[half(h), :], start=True, stop=True)
                last.then_inc(st_turned, 1)
            pe.wait_ge(st_set, 1)

            def loras():
                for u in range(U):
                    d, p = divmod(u, 4)
                    pe.matmul(pb(2)[:, u * C:(u + 1) * C], wu[0:64, d, p * 128:(p + 1) * 128], lc[0:64, d, :], start=True, stop=True)
                    last = pe.matmul(pb(3)[:, u * C:(u + 1) * C], wu[64:128, d, p * 128:(p + 1) * 128], lc[64:128, d, :], start=True, stop=True)
                return last

            pe.wait_ge(pre_pool, 4)
            loras().then_inc(pre_pe, 1)
            pe.wait_ge(pre_dve, 3)

            def step(i, ahead):
                pe.wait_ge(act_s.sem, act_s.before(i, "ucopy_1"))
                pe.sem_inc(pe_passed, 1)
                for u, h in units:
                    last = pe.matmul(pb(2)[half(h), u * C:(u + 1) * C], vc[half(h), u, :], id2[half(h), :], start=True, stop=True)
                last.then_inc(pe_s.sem, 1)
                pe.wait_ge(dve_s.sem, dve_s.before(i, "y"))
                pe.sem_inc(pe_passed, 1)
                for u in range(U):
                    last = pe.matmul(pb(6)[:, u * C:(u + 1) * C], rk[:, u % 4, :], bon[:, u, :], start=True, stop=True)
                last.then_inc(pe_s.sem, 1)
                pe.wait_ge(dve_s.sem, dve_s.here(i, "ark", not ahead))
                pe.wait_ge(act_s.sem, act_s.before(i, "w1_1"))
                pe.sem_inc(pe_passed, 1)
                for u, h in units:
                    pe.matmul(pb(4)[half(h), u * C:(u + 1) * C], bk[half(h), u, b_cols(h)], ar[half(h), u, 0:C], start=True, stop=True)
                    last = pe.matmul(pb(5)[half(h), u * C:(u + 1) * C], ar[half(h), u, 0:C], bk[half(h), u, b_cols(h)], start=True, stop=True)
                last.then_inc(pe_s.sem, 1)
                pe.wait_ge(act_s.sem, act_s.here(i, "vcopy", not ahead))
                pe.sem_inc(pe_passed, 1)
                for u, h in units:
                    n = slot(u, h)
                    last = pe.matmul(pb(0, 4)[:, n * 128:(n + 1) * 128], bk[half(h), u, :], ar[half(h), u, :], start=True, stop=True)
                last.then_inc(pe_s.sem, 1)
                pe.wait_ge(dve_s.sem, dve_s.here(i, "bonus", not ahead))
                pe.sem_inc(pe_passed, 1)
                for u, h in units:
                    n = slot(u, h)
                    last = pe.transpose(pb(6, 2)[:, n * C:(n + 1) * C], bk[half(h), u, :], id2[half(h), :])
                last.then_inc(pe_s.sem, 1)
                pe.wait_ge(dve_s.sem, dve_s.here(i, "gmask", not ahead))
                pe.sem_inc(pe_passed, 1)
                for n in lvl:
                    lo, hi = (C if n == 0 else 0), (C if n == 5 else 2 * C)
                    for d in range(2):
                        if n:
                            pe.wait_ge(act_s.sem, act_s.here(i, f"m{n}_{d}", not ahead))
                            pe.wait_ge(dve_s.sem, dve_s.here(i, f"x{n - 1}_{d}", not ahead))
                            pe.sem_inc(pe_passed, 1)
                        for u in range(4 * d, 4 * d + 4):
                            last = pe.matmul(pb(0, 2)[:, u * 128 + lo:u * 128 + hi], m_diag[:, u, :], xm[:, u, lo:hi], start=True, stop=True)
                            if n < 5:
                                last = pe.matmul(pb(4 + d)[:, (u % 4) * C:(u % 4 + 1) * C], t_diag[:, u, :], m[:, u, :], start=True, stop=True)
                        last.then_inc(pe_s.sem, 1)
                    if n == 0 and ahead:
                        pe.wait_ge(pool_s.sem, pool_s.here(i, "copied"))
                        pe.sem_inc(pe_passed, 1)
                        loras().then_inc(pe_s.sem, 1)
                for d in range(2):
                    pe.wait_ge(dve_s.sem, dve_s.here(i, f"x5_{d}", not ahead))
                    pe.sem_inc(pe_passed, 1)
                    for u, h in of_direction(d):
                        n = slot(u, h)
                        pe.matmul(turned(4, u, h), g[half(h), n, 0:C], uv[half(h), n, :], start=True, stop=False)
                        last = pe.matmul(turned(4, u, h), ar[half(h), u, 0:C], s[half(h), u, :], start=False, stop=True)
                    last.then_inc(pe_s.sem, 1)
                for d in range(2):
                    pe.wait_ge(act_s.sem, act_s.here(i, f"w1_{d}", not ahead))
                    pe.sem_inc(pe_passed, 1)
                    for u, h in of_direction(d):
                        last = pe.matmul(turned(2, u, 1 - h), xm[half(h), u, 0:C], w1[half(h), u, :], start=True, stop=True)
                    last.then_inc(pe_s.sem, 1)
                for d in range(2):
                    pe.wait_ge(act_s.sem, act_s.here(i, f"ucopy_{d}", not ahead))
                    pe.sem_inc(pe_passed, 1)
                    for u, h in of_direction(d):
                        n = slot(u, h)
                        pe.matmul(pb(6)[half(h), u * C:(u + 1) * C], uv[:, n, :], g[:, n, C:2 * C], start=True, stop=False)
                        last = pe.matmul(pb(6)[half(h), u * C:(u + 1) * C], s[half(h), u, :], ar[half(h), u, C:2 * C], start=False, stop=True)
                last.then_inc(pe_s.sem, 1)
                for u, h in units:
                    n = slot(u, h)
                    last = pe.matmul(pb(7)[half(h), u * C:(u + 1) * C], bkt[:, n, :], uv[:, n, :], start=True, stop=True)
                last.then_inc(pe_s.sem, 1)

            each_chunk(pe, step)
            if not latent:
                pe.wait_ge(dve_s.sem, dve_s.here(chunks - 1, "y", True))
                for u, h in units:
                    last = pe.matmul(pb(7)[half(h), u * C:(u + 1) * C], s[half(h), u, :], id2[half(h), :], start=True, stop=True)
                last.then_inc(fin_turned, 1)

        @block.scalar
        def _(act):
            def sigmoids():
                act.activation(sw, sw, ACT.Sigmoid)
                return act.activation(sa, sa, ACT.Sigmoid)

            def exps():
                act.activation(e1, L, ACT.Exp)
                act.activation(e0, Lx, ACT.Exp)
                return act.activation(ei, L, ACT.Exp, scale=-1.0)

            act_s.start(act)
            act.wait_ge(pre_dve, 1)
            sigmoids().then_inc(pre_act, 1)
            act.wait_ge(pre_dve, 2)
            exps().then_inc(pre_act, 1)

            def step(i, ahead):
                act.wait_ge(pe_s.sem, pe_s.here(i, "vturn", not ahead))
                act.activation(uv[half(0), 0:8, :], u64(pb(2))[half(0), :, :], ACT.Copy)
                act.activation(uv[half(1), 8:16, :], u64(pb(2))[half(1), :, :], ACT.Copy).then_inc(act_s.sem, 1)
                act.wait_ge(pe_s.sem, pe_s.here(i, "bkt", not ahead))
                act.activation(bkt, u64(pb(6, 2)), ACT.Copy).then_inc(act_s.sem, 1)
                for n in range(1, 6):
                    for d in range(2):
                        act.wait_ge(pe_s.sem, pe_s.here(i, f"level{n - 1}_{d}", not ahead))
                        power = u64(pb(4 + d)[:, 0:4 * C])
                        if n < 5:
                            act.activation(m[:, 4 * d:4 * d + 4, :], power, ACT.Copy)
                        for h in range(2):
                            last = act.activation(m_diag[half(h), 4 * d:4 * d + 4, half(h)], power[half(h), :, :], ACT.Copy)
                        last.then_inc(act_s.sem, 1)
                if ahead:
                    act.wait_ge(dve_s.sem, dve_s.here(i, "bias"))
                    sigmoids().then_inc(act_s.sem, 1)
                for d in range(2):
                    act.wait_ge(pe_s.sem, pe_s.here(i, f"w1_{d}", not ahead))
                    act.activation(w1[:, 4 * d:4 * d + 4, :], u64(pb(4 + d)[:, 0:4 * C]), ACT.Copy, scale=-1.0).then_inc(act_s.sem, 1)
                for d in range(2):
                    act.wait_ge(pe_s.sem, pe_s.here(i, f"u_{d}", not ahead))
                    act.activation(uv[half(1), 4 * d:4 * d + 4, :], u64(pb(2 + d)[:, 0:4 * C])[half(1), :, :], ACT.Copy)
                    act.activation(uv[half(0), 8 + 4 * d:12 + 4 * d, :], u64(pb(2 + d)[:, 0:4 * C])[half(0), :, :], ACT.Copy).then_inc(act_s.sem, 1)
                if ahead:
                    act.wait_ge(dve_s.sem, dve_s.here(i, "logs"))
                    exps().then_inc(act_s.sem, 1)

            each_chunk(act, step)

        @block.vector
        def _(dve):
            def bc(col, n=4):
                return col.rearrange("p (u o) -> p u o", o=1).broadcast_to([128, n, C])

            def rows(v, n):
                return v.rearrange("p (o t) -> p o t", o=1).broadcast_to([128, n, v.shape[1]])

            dve_s.start(dve)
            dve.memset(k.at(DIAG0, 2 * U * 128), 0.0)
            if latent:
                dve.wait_ge(st_turned, 1)
                dve.tensor_copy(s, u64(pb(7))).then_inc(st_set, 1)
            else:
                dve.memset(b["s"], 0.0).then_inc(st_set, 1)

            def biases():
                dve.tensor_tensor(sw, u64(pb(2)), bc(k.col("w0", 0, 8), 8), ALU.add)
                return dve.tensor_tensor(sa, u64(pb(3)), bc(k.col("a0", 0, 8), 8), ALU.add)

            def log_decays():
                dve.tensor_scalar(sw, sw, DECAY, None, ALU.mult)
                dve.drain()
                dve.tensor_tensor_scan(b["L"][:, 0:256], k.const("scan"), b["sw"][:, 0:256], 0.0, ALU.mult, ALU.add)
                dve.tensor_tensor_scan(b["L"][:, 511:255:-1], k.const("scan"), b["sw"][:, 511:255:-1], 0.0, ALU.mult, ALU.add)
                dve.drain()
                return dve.tensor_tensor(Lx, L, sw, ALU.subtract)

            def direction_keys(i, ahead):
                for d in range(2):
                    q = slice(4 * d, 4 * d + 4)
                    dve.scalar_tensor_tensor(out=kd[:, q, :], in0=sa[:, q, :], scalar=-1.0, in1=bc(k.col("k_a", 0, 4)), op0=ALU.add, op1=ALU.mult)
                for d in range(2):
                    q = slice(4 * d, 4 * d + 4)
                    dve.tensor_tensor(sa[:, q, :], sa[:, q, :], kk[:, :, cols(i, d, ahead)], ALU.mult)
                dve.drain()
                for d in range(2):
                    q = slice(4 * d, 4 * d + 4)
                    dve.scalar_tensor_tensor(out=kd[:, q, :], in0=kd[:, q, :], scalar=1.0, in1=rs[:, 4:8, cols(i, d, ahead)], op0=ALU.add, op1=ALU.mult)
                dve.drain()
                for d in range(2):
                    q = slice(4 * d, 4 * d + 4)
                    last = dve.tensor_tensor(bon[:, q, :], kd[:, q, :], rs[:, 0:4, cols(i, d, ahead)], ALU.mult)
                return last

            dve.wait_ge(pre_pe, 1)
            biases().then_inc(pre_dve, 1)
            dve.wait_ge(pre_act, 1)
            log_decays().then_inc(pre_dve, 1)
            direction_keys(0, 0).then_inc(pre_dve, 1)
            dve.wait_ge(pre_act, 2)

            def step(i, ahead):
                dve.wait_ge(act_s.sem, act_s.before(i, "exp"))
                for d in range(2):
                    q = slice(4 * d, 4 * d + 4)
                    dve.tensor_copy(end[:, q, :], e1[:, q, C - 1:C] if d == 0 else e1[:, q, 0:1])
                    dve.tensor_tensor(ar[:, q, 0:C], e0[:, q, :], kk[:, :, cols(i, d)], ALU.mult)
                    dve.tensor_tensor(ar[:, q, C:2 * C], e1[:, q, :], rs[:, 0:4, cols(i, d)], ALU.mult)
                for h in range(2):
                    dve.tensor_tensor(bk[half(h), :, b_cols(h)], sa[half(h), :, :], ei[half(h), :, :], ALU.mult)
                    last = dve.tensor_tensor(bk[half(h), :, k_cols(h)], kd[half(h), :, :], ei[half(h), :, :], ALU.mult)
                last.then_inc(dve_s.sem, 1)
                dve.wait_ge(pe_s.sem, pe_s.here(i, "bonus", not ahead))
                dve.tensor_tensor(tmp, u64(pb(6)), vc, ALU.mult)
                for d in range(2):
                    dve.drain()
                    last = dve.tensor_tensor(ya[:, :, cols(i, d)], ya[:, :, cols(i, d)], tmp[:, 4 * d:4 * d + 4, :], ALU.add)
                last.then_inc(dve_s.sem, 1)
                dve.wait_ge(pe_s.sem, pe_s.here(i, "n0", not ahead))
                for d in range(2):
                    q = slice(4 * d, 4 * d + 4)
                    up, low = (k.const("lt"), k.const("gt")) if d == 0 else (k.const("gt"), k.const("lt"))
                    dve.tensor_tensor(m[:, q, :], u64(pb(5))[:, q, :], rows(low, 4), ALU.mult)
                    dve.tensor_tensor(xm[:, q, C:2 * C], u64(pb(4))[:, q, :], rows(up, 4), ALU.mult)
                dve.drain()
                for h in range(2):
                    dve.tensor_copy(m_diag[half(h), :, half(h)], m[half(h), :, :])
                    dve.tensor_copy(t_diag[half(h), :, half(h)], xm[half(h), :, C:2 * C])
                dve.tensor_tensor(xm[:, :, 0:C], xm[:, :, C:2 * C], rows(id2, 8), ALU.add).then_inc(dve_s.sem, 1)
                dve.wait_ge(pe_s.sem, pe_s.here(i, "gram", not ahead))
                for h in range(2):
                    for d in range(2):
                        last = dve.tensor_tensor(g[:, 8 * h + 4 * d:8 * h + 4 * d + 4, :], pb(2 * h + d).rearrange("p (n t) -> p n t", t=128),
                                                 rows(k.const("mask_b" if d else "mask_f"), 4), ALU.mult)
                last.then_inc(dve_s.sem, 1)
                for n in lvl:
                    acc = pb(0, 2).rearrange("p (u t) -> p u t", t=2 * C)
                    for d in range(2):
                        q = slice(4 * d, 4 * d + 4)
                        dve.wait_ge(pe_s.sem, pe_s.here(i, f"level{n}_{d}", not ahead))
                        if n < 5:
                            last = dve.tensor_copy(xm[:, q, C:2 * C], acc[:, q, C:2 * C])
                        if n < 4:
                            for h in range(2):
                                last = dve.tensor_copy(t_diag[half(h), q, half(h)], acc[half(h), q, C:2 * C])
                        if n:
                            last = dve.tensor_tensor(xm[:, q, 0:C], acc[:, q, 0:C], xm[:, q, 0:C], ALU.add)
                        last.then_inc(dve_s.sem, 1)
                    if n == 0 and ahead:
                        dve.wait_ge(pe_s.sem, pe_s.here(i, "lora", not ahead))
                        biases().then_inc(dve_s.sem, 1)
                if ahead:
                    dve.wait_ge(act_s.sem, act_s.here(i, "sig"))
                    log_decays().then_inc(dve_s.sem, 1)
                    direction_keys(i, 1).then_inc(dve_s.sem, 1)
                dve.wait_ge(pe_s.sem, pe_s.here(i, "s", not ahead))
                dve.tensor_tensor(tmp, u64(pb(7)), s, ALU.add)
                dve.drain()
                for d in range(2):
                    q = slice(4 * d, 4 * d + 4)
                    last = dve.tensor_tensor(s[:, q, :], tmp[:, q, :], end[:, q, :].broadcast_to([128, 4, C]), ALU.mult)
                last.then_inc(dve_s.sem, 1)
                for d in range(2):
                    dve.drain()
                    last = dve.tensor_tensor(ya[:, :, cols(i, d)], u64(pb(6))[:, 4 * d:4 * d + 4, :], ya[:, :, cols(i, d)], ALU.add)
                last.then_inc(dve_s.sem, 1)

            each_chunk(dve, step)
            if not latent:
                dve.wait_ge(fin_turned, 1)
                dve.tensor_copy(st[:, 0:8, :], u64(pb(7))).then_inc(fin_copied, 1)


def stage_rwkv_post(k, A, scratch):
    nc = k.nc
    ya, rs = k.tiles(YA0, 4, T), k.tiles(RS0, RW_TILES, T)
    out = k.tiles(OA0 + 4 * T, 4, T)
    gup = k.at(Z1, 512)
    sq, root = k.tiles(Z1 + 1024, 2, T), k.tiles(Z1 + 1024 + 2 * T, 2, T)
    eps = k.at(SM0 + 1, 1)
    S = lambda n: k.sem(f"gn_{n}")
    gup_in, summed, centred, squared, var_ready, rooted, normed, gate_ready, done = (S(n) for n in (
        "gup_in", "summed", "centred", "squared", "var", "root", "normed", "gate", "done"))
    eps_set, scaled = S("eps"), S("scaled")
    with nc.Block() as block:
        @block.sync
        def _(sp):
            sp.dma_start(gup, A["rwkv_g_up"][0]).then_inc(gup_in, 16)

        @block.tensor
        def _(pe):
            pe.wait_ge(gup_in, 16)
            for t in range(4):
                if t:
                    pe.wait_ge(centred, t)
                for tc in range(3):
                    last = pe.matmul(k.bank(tc, TC), k.const("blockones"), ya[:, t, tc * TC:(tc + 1) * TC], start=True, stop=True)
                last.then_inc(summed, 1)
                pe.wait_ge(squared, t + 1)
                if t:
                    pe.wait_ge(done, t)
                for tc in range(3):
                    last = pe.matmul(k.bank(3 + tc, TC), k.const("blockones"), sq[:, t % 2, tc * TC:(tc + 1) * TC], start=True, stop=True)
                last.then_inc(var_ready, 1)
                pe.wait_ge(rooted, t + 1)
                for tc in range(3):
                    last = pe.matmul(k.bank(3 + tc, TC), gup[:, t * 128:(t + 1) * 128], rs[:, 13, tc * TC:(tc + 1) * TC], start=True, stop=True)
                last.then_inc(gate_ready, 1)

        @block.scalar
        def _(act):
            act.wait_ge(eps_set, 1)
            for t in range(4):
                act.wait_ge(centred, t + 1)
                act.activation(sq[:, t % 2, :], ya[:, t, :], ACT.Square).then_inc(squared, 1)
                act.wait_ge(var_ready, t + 1)
                for tc in range(3):
                    last = act.activation(root[:, t % 2, tc * TC:(tc + 1) * TC], k.bank(3 + tc, TC), ACT.Sqrt, bias=eps, scale=1.0 / C)
                last.then_inc(rooted, 1)
                act.wait_ge(normed, t + 1)
                act.activation(ya[:, t, :], ya[:, t, :], ACT.Identity, scale=k.col("ln_g", t), bias=k.col("ln_b", t)).then_inc(scaled, 1)

        @block.vector
        def _(dve):
            dve.memset(eps, 64e-5).then_inc(eps_set, 1)
            for t in range(4):
                dve.wait_ge(summed, t + 1)
                for tc in range(3):
                    v = ya[:, t, tc * TC:(tc + 1) * TC]
                    last = dve.scalar_tensor_tensor(out=v, in0=k.bank(tc, TC), scalar=-1.0 / C, in1=v, op0=ALU.mult, op1=ALU.add)
                last.then_inc(centred, 1)
                dve.wait_ge(rooted, t + 1)
                dve.reciprocal(root[:, t % 2, :], root[:, t % 2, :])
                dve.drain()
                dve.tensor_tensor(ya[:, t, :], ya[:, t, :], root[:, t % 2, :], ALU.mult).then_inc(normed, 1)
                dve.wait_ge(scaled, t + 1)
                dve.wait_ge(gate_ready, t + 1)
                for tc in range(3):
                    c = slice(tc * TC, (tc + 1) * TC)
                    last = dve.tensor_tensor(out[:, t, c], k.bank(3 + tc, TC), ya[:, t, c], ALU.mult)
                last.then_inc(done, 1)


def stage_mixer_out(k, A, scratch):
    heads = k.tiles(OA0, 8, T)
    stage_gemm(k, "mix", lambda kt: heads[:, kt, :], KT, A["ab_w_out"][0].rearrange("(k p) n -> p k n", p=128),
               KT, H0, evac_residual(k, 0, 0), x_from=scratch["x_d"])


HL = NL // 2
HKT = HL // 128
Q = 256
QT = Q // 128
ROUNDS = D // Q
(FT0, IT0, UT0, SS0, DD0, AB0, OC0, UK0, PR0, FB0, WIN0, VX0, U10, TI0, HD0, W30, DQ0, HW0, TC0, PT0, PU0, PS0, PD0, PK0, PA0,
 HY_END) = [int(x) for x in np.cumsum([0, 8192, 8192, 2048, 2048, 2048, 4096, 1024, 2048, 1024, 1024, 512, 6912, 2304, 1024, 1152,
                                        512, 256, 200, 16, 512, 256, 256, 256, 1024, 512])]
assert HY_END <= CST
TWO_PI = 2.0 * math.pi
TWO_PI_HI = 6.28125
TWO_PI_LO = TWO_PI - TWO_PI_HI
MAGIC = 1.5 * 2.0 ** 23


def stage_hyena_in(k, A, scratch, norm):
    raw, z = k.tiles(BIG, 2, T), k.tiles(BIG + 2 * T, 2, T)
    z_d = scratch["z_d"]

    def evac(dve, m, j, tc, acc):
        return dve.tensor_scalar(raw[:, j, tc * TC:(tc + 1) * TC], acc, k.pv[:, ds(m + COL["b_in"], 1)], None, ALU.add)

    def after(dve, m, j):
        tap = lambda n: k.pv[:, ds(m + (COL["conv_w"] + 24 * n), 1)]
        dve.tensor_scalar(z[:, j, :], raw[:, j, :], tap(1), k.pv[:, ds(m + COL["conv_b"], 1)], ALU.mult, ALU.add)
        dve.drain()
        for a, n in GROUPS:
            dve.scalar_tensor_tensor(out=z[:, j, a + 1:a + n], in0=raw[:, j, a:a + n - 1], scalar=tap(0),
                                     in1=z[:, j, a + 1:a + n], op0=ALU.mult, op1=ALU.add)
        dve.drain()
        for a, n in GROUPS:
            last = dve.scalar_tensor_tensor(out=z[:, j, a:a + n - 1], in0=raw[:, j, a + 1:a + n], scalar=tap(2),
                                            in1=z[:, j, a:a + n - 1], op0=ALU.mult, op1=ALU.add)
        return last

    stage_gemm(k, "hz", lambda kt: k.H[:, kt, :], KT, A["hy_w_in"][0].rearrange("(k p) n -> p k n", p=128), 24, WB, evac,
               store=lambda act, m, j: (z_d[ds(m, 1), :, :].rearrange("m p t -> (m p) t"), z[:, j, :]), after=after, norm=norm, x_to=scratch["x_d"])


def stage_filter_features(k, A, consts, scratch):
    nc = k.nc
    feat = k.at(UT0, T)
    arg, turns = k.at(AB0, T), k.at(AB0 + T, T)
    arg2 = k.at(AB0 + 2 * T, T)
    hd = k.at(HD0, T)
    w = [k.at(HW0 + 64 * n, 64) for n in range(3)]
    cols = k.at(HW0 + 192, 6)
    w_in, tab_in = k.sem("filter_w_in"), k.sem("tables_in")
    summed, reduced, sined = k.sem("filter_sums"), k.sem("filter_args"), k.sem("filter_sines")
    with nc.Block() as block:
        @block.sync
        def _(sp):
            sp.dma_start(feat[0:33, :], consts["feat"]).then_inc(w_in, 16)
            for n in range(3):
                sp.dma_start(w[n][0:(33 if n == 0 else 64), :], A[f"hy_f_w{n}"][0]).then_inc(w_in, 16)
                sp.dma_start(cols[0:64, n:n + 1], A[f"hy_f_b{n}"].rearrange("l p -> p l")).then_inc(w_in, 16)
                sp.dma_start(cols[0:64, 3 + n:4 + n], A["hy_f_freq"][:, n, :].rearrange("l p -> p l")).then_inc(w_in, 16)
            sp.dma_start(k.at(FT0, 8192), consts["dft"]).then_inc(tab_in, 16)
            sp.dma_start(k.at(IT0, 8192), consts["idft"]).then_inc(tab_in, 16)
            sp.dma_start(k.at(PT0, 512), consts["pdft"]).then_inc(tab_in, 16)
            sp.dma_start(k.at(TC0, 9), consts["steps"]).then_inc(tab_in, 16)
            sp.wait_ge(tab_in, 64)

        @block.tensor
        def _(pe):
            pe.wait_ge(w_in, 160)
            for n in range(3):
                if n:
                    pe.wait_ge(sined, n)
                src = feat[0:33, :] if n == 0 else hd[0:64, :]
                for tc in range(3):
                    last = pe.matmul(k.bank(tc, TC)[0:64, :], w[n][0:src.shape[0], :], src[:, tc * TC:(tc + 1) * TC], start=True, stop=True)
                last.then_inc(summed, 1)

        @block.scalar
        def _(act):
            for n in range(3):
                act.wait_ge(reduced, n + 1)
                act.activation(hd[0:64, :], arg[0:64, :], ACT.Sin).then_inc(sined, 1)
            act.wait_ge(sined, 3)
            act.activation(hd[64:128, :], hd[0:64, :], ACT.Copy)

        @block.vector
        def _(dve):
            q = slice(0, 64)
            for n in range(3):
                dve.wait_ge(summed, n + 1)
                for tc in range(3):
                    dve.tensor_scalar(arg2[q, tc * TC:(tc + 1) * TC], k.bank(tc, TC)[q, :], cols[q, n:n + 1], cols[q, 3 + n:4 + n], ALU.add, ALU.mult)
                dve.drain()
                dve.tensor_scalar(turns[q, :], arg2[q, :], 1.0 / TWO_PI, MAGIC, ALU.mult, ALU.add)
                dve.drain()
                dve.tensor_scalar(turns[q, :], turns[q, :], -MAGIC, None, ALU.add)
                dve.drain()
                dve.scalar_tensor_tensor(out=arg2[q, :], in0=turns[q, :], scalar=-TWO_PI_HI, in1=arg2[q, :], op0=ALU.mult, op1=ALU.add)
                dve.drain()
                dve.scalar_tensor_tensor(out=arg2[q, :], in0=turns[q, :], scalar=-TWO_PI_LO, in1=arg2[q, :], op0=ALU.mult, op1=ALU.add)
                dve.drain()
                dve.tensor_scalar(arg[q, :], arg2[q, :], 3.1415925, -3.1415925, ALU.min, ALU.max).then_inc(reduced, 1)


def stage_hyena(k, A, consts, scratch):
    nc = k.nc
    ft = k.at(FT0, 8192).rearrange("p (c o k n) -> p c o k n", c=2, o=2, k=HKT)
    it = k.at(IT0, 8192).rearrange("p (c o k n) -> p c o k n", c=2, o=2, k=HKT)
    ptab = k.tiles(PT0, 4, 128)
    ut, ss, dd = k.tiles(UT0, 8, Q), k.tiles(SS0, 8, Q), k.tiles(DD0, 8, Q)
    ab = k.at(AB0, 4096).rearrange("p (c o f n) -> p c o f n", c=2, o=2, f=HKT)
    oc, uk, pr = k.tiles(OC0, 4, Q), k.tiles(UK0, 8, Q), k.tiles(PR0, 4, Q)
    fb = [k.tiles(FB0 + 512 * j, 2, Q) for j in range(2)]
    win = k.tiles(WIN0, 2, Q)
    vx, u1, ti = k.tiles(VX0, 3 * QT, T), k.tiles(U10, QT, T), k.tiles(TI0, 2, 512)
    hd, w3, dq, tcol = k.at(HD0, T), k.tiles(W30, 2, Q), k.at(DQ0, Q), k.at(TC0, 9)
    pu, ps, pd = k.at(PU0, Q), k.at(PS0, Q), k.at(PD0, Q)
    pk, pa = k.tiles(PK0, 4, Q), k.tiles(PA0, 2, Q)
    z_d = scratch["z_d"]
    ACC = ("Co", "Ce", "So", "Se", "Ko", "Ke", "Do", "De")
    pe_n, act_n, dve_n = [], [], []
    for o in range(2):
        pe_n += [f"{o}ptok", f"{o}pfilt", f"{o}pfreq", f"{o}pinv"] + [f"{o}{n}{t}" for t in range(8) for n in ("tok", "filt")]
        pe_n += [f"{o}f{f}{a}" for f in range(HKT) for a in ACC] + [f"{o}inv{n}" for n in range(2 * QT)]
        act_n += [f"{o}pwin", f"{o}ptok"]
        for t in range(8):
            act_n += [f"{o}tok{t}", f"{o}win{t}"]
        act_n += [f"{o}f{f}{a}" for f in range(HKT) for a in ACC[0::2]]
        dve_n += [f"{o}pfilt", f"{o}pfreq", f"{o}pinv"] + [f"{o}filt{t}" for t in range(8)]
        for f in range(HKT):
            dve_n += [f"{o}f{f}{a}" for a in ACC[1::2]] + [f"{o}f{f}ab"]
        dve_n += [f"{o}inv{n}" for n in range(2 * QT)]
    pe_s, act_s, dve_s = Steps(k.sem("hy_pe_step"), pe_n), Steps(k.sem("hy_act_step"), act_n), Steps(k.sem("hy_dve_step"), dve_n)
    passed = k.sem("hy_sp_passed")
    hb = lambda i, o, m: k.pv[:, ds(i * QT + (COL["hbias"] + 8 * o + m), 1)]
    in_sem, stored = k.sem("hy_round_in"), k.sem("hy_stored")
    LOADS = 3 * QT + 2 * 2 + 1
    half = lambda o: slice(64 * o, 64 * o + 64)
    even_odd = lambda a, o: slice(NP_ + o + 2 * a, NP_ + o + 2 * a + 255, 2)
    bank = k.bank

    with nc.Block() as block:
        @block.sync
        def _(sp):
            with sp.Fori(0, ROUNDS) as i:
                c0 = sp.snap(i * Q)
                rows = [sp.snap(i * QT + (m + 8 * part)) for part in (2, 0, 1) for m in range(QT)]
                done = sp.snap(dve_s.here(i, f"1inv{2 * QT - 1}"))
                n_stored = sp.snap(i * (16 * QT) + 16 * QT)
                outs = [sp.snap(i * QT + (m + 16)) for m in range(QT)]
                for n, r in enumerate(rows):
                    sp.dma_start(vx[:, n, :], z_d[ds(r, 1), :, :].rearrange("m p t -> (m p) t")).then_inc(in_sem, 16)
                w3v = A["hy_f_w3"][0].rearrange("p (o d n) -> p o d n", o=2, d=2)
                for o in range(2):
                    for d in range(2):
                        sp.dma_start(w3[half(o), d, :], w3v[:, o, d, ds(c0, Q)]).then_inc(in_sem, 16)
                sp.dma_start(dq, consts["deltas"][:, ds(c0, Q)]).then_inc(in_sem, 16)
                sp.wait_ge(dve_s.sem, done)
                for m in range(QT):
                    sp.dma_start(z_d[ds(outs[m], 1), :, :].rearrange("m p t -> (m p) t"), vx[:, m, :]).then_inc(stored, 16)
                sp.wait_ge(stored, n_stored)
                sp.sem_inc(passed, 1)

        @block.tensor
        def _(pe):
            pe_s.start(pe)
            with pe.Fori(0, ROUNDS) as i:
                pe.wait_ge(in_sem, i * (16 * LOADS) + 16 * LOADS)
                for o in range(2):
                    u = vx if o == 0 else u1
                    if o:
                        pe.wait_ge(dve_s.sem, dve_s.here(i, f"0inv{2 * QT - 1}"))
                    else:
                        pe.wait_ge(dve_s.sem, dve_s.before(i, f"1inv{2 * QT - 1}"))
                    for m in range(QT):
                        last = pe.transpose(bank(0)[:, m * 128:(m + 1) * 128], u[:, m, 0:NP_], k.ident)
                    last.then_inc(pe_s.sem, 1)
                    for d in range(2):
                        last = pe.matmul(bank(1)[:, d * Q:(d + 1) * Q], hd[half(o), 0:NP_], w3[half(o), d, :], start=True, stop=True)
                    last.then_inc(pe_s.sem, 1)
                    pe.wait_ge(act_s.sem, act_s.here(i, f"{o}ptok"))
                    pe.wait_ge(dve_s.sem, dve_s.here(i, f"{o}pfilt"))
                    for n, (tab, v) in enumerate([(0, pu), (1, pu), (0, ps), (1, pd)]):
                        last = pe.matmul(bank(2 + n)[:, 0:Q], ptab[:, tab, :], v, start=True, stop=True)
                    last.then_inc(pe_s.sem, 1)
                    pe.wait_ge(dve_s.sem, dve_s.here(i, f"{o}pfreq"))
                    for m in range(QT):
                        for c in range(2):
                            last = pe.matmul(bank(6)[:, m * 128:(m + 1) * 128], pa[:, c, m * 128:(m + 1) * 128], ptab[:, 2 + c, :],
                                             start=(c == 0), stop=(c == 1))
                    last.then_inc(pe_s.sem, 1)
                    for t in range(8):
                        par, kt = divmod(t, HKT)
                        if t >= 2:
                            pe.wait_ge(act_s.sem, act_s.here(i, f"{o}tok{t - 2}"))
                        elif t == 0:
                            pe.wait_ge(dve_s.sem, dve_s.here(i, f"{o}pfreq"))
                        for m in range(QT):
                            last = pe.transpose(bank(2 + t % 2)[:, m * 128:(m + 1) * 128], u[:, m, even_odd(kt * 128, par)], k.ident)
                        last.then_inc(pe_s.sem, 1)
                        if t >= 2:
                            pe.wait_ge(dve_s.sem, dve_s.here(i, f"{o}filt{t - 2}"))
                        for d in range(2):
                            last = pe.matmul(bank(t % 2)[:, d * Q:(d + 1) * Q], hd[half(o), even_odd(kt * 128, par)], w3[half(o), d, :], start=True, stop=True)
                        last.then_inc(pe_s.sem, 1)
                    pe.wait_ge(act_s.sem, act_s.here(i, f"{o}tok7"))
                    pe.wait_ge(dve_s.sem, dve_s.here(i, f"{o}filt7"))
                    for f in range(HKT):
                        for n, a in enumerate(ACC):
                            if f:
                                s_, nm = (act_s, a) if n % 2 == 0 else (dve_s, a)
                                pe.wait_ge(s_.sem, s_.here(i, f"{o}f{f - 1}{nm}"))
                            c, par = int(a[0] in "SD"), int(a[1] == "o")
                            src = {"C": ut, "S": ut, "K": ss, "D": dd}[a[0]]
                            for kt in range(HKT):
                                last = pe.matmul(bank(n)[:, 0:Q], ft[:, c, par, kt, f * 128:(f + 1) * 128], src[:, par * HKT + kt, :],
                                                 start=(kt == 0), stop=(kt == HKT - 1))
                            last.then_inc(pe_s.sem, 1)
                    pe.wait_ge(dve_s.sem, dve_s.here(i, f"{o}f{HKT - 1}ab"))
                    for n in range(2 * QT):
                        m, par = divmod(n, 2)
                        for c in range(2):
                            for f in range(HKT):
                                last = pe.matmul(bank(n), ab[:, c, par, f, m * 128:(m + 1) * 128], it[:, c, par, f, :],
                                                 start=(c == 0 and f == 0), stop=(c == 1 and f == HKT - 1))
                        last.then_inc(pe_s.sem, 1)

        @block.scalar
        def _(act):
            act_s.start(act)
            with act.Fori(0, ROUNDS) as i:
                act.wait_ge(in_sem, i * (16 * LOADS) + 16 * LOADS)
                for o in range(2):
                    if o:
                        act.wait_ge(dve_s.sem, dve_s.here(i, "0pfilt"))
                    act.activation(win[:, 0, :], dq, ACT.Exp, scale=tcol[:, 8:9]).then_inc(act_s.sem, 1)
                    act.wait_ge(pe_s.sem, pe_s.here(i, f"{o}ptok"))
                    act.activation(pu, bank(0)[:, 0:Q], ACT.Copy).then_inc(act_s.sem, 1)
                    act.wait_ge(dve_s.sem, dve_s.here(i, f"{o}pfilt"))
                    for t in range(8):
                        act.wait_ge(pe_s.sem, pe_s.here(i, f"{o}tok{t}"))
                        act.activation(ut[:, t, :], bank(2 + t % 2)[:, 0:Q], ACT.Copy).then_inc(act_s.sem, 1)
                        if t >= 2:
                            act.wait_ge(dve_s.sem, dve_s.here(i, f"{o}filt{t - 2}"))
                        act.activation(win[:, t % 2, :], dq, ACT.Exp, scale=tcol[:, t:t + 1]).then_inc(act_s.sem, 1)
                    for f in range(HKT):
                        for n, a in enumerate(ACC[0::2]):
                            act.wait_ge(pe_s.sem, pe_s.here(i, f"{o}f{f}{a}"))
                            if f:
                                act.wait_ge(dve_s.sem, dve_s.here(i, f"{o}f{f - 1}{ACC[2 * n + 1]}"))
                            act.activation(oc[:, n, :], bank(2 * n)[:, 0:Q], ACT.Copy).then_inc(act_s.sem, 1)

        @block.vector
        def _(dve):
            tt = dve.tensor_tensor
            dve_s.start(dve)
            with dve.Fori(0, ROUNDS) as i:
                dve.wait_ge(in_sem, i * (16 * LOADS) + 16 * LOADS)
                for o in range(2):
                    u = vx[:, 0:QT, :] if o == 0 else u1
                    out = u1 if o == 0 else vx[:, 0:QT, :]
                    x = vx[:, QT * (1 + o):QT * (2 + o), :]

                    def windowed(psum_bank, w, buf, hs, hdif, first):
                        tt(buf, psum_bank.rearrange("p (d n) -> p d n", d=2),
                           w.rearrange("p (o n) -> p o n", o=1).broadcast_to([128, 2, Q]), ALU.mult)
                        dve.drain()
                        if first:
                            dve.tensor_scalar(buf[:, 1, :], buf[:, 1, :], k.const("nz"), None, ALU.mult)
                            dve.drain()
                        tt(hs, buf[:, 0, :], buf[:, 1, :], ALU.add)
                        return tt(hdif, buf[:, 0, :], buf[:, 1, :], ALU.subtract)

                    dve.wait_ge(pe_s.sem, pe_s.here(i, f"{o}pfilt"))
                    dve.wait_ge(act_s.sem, act_s.here(i, f"{o}pwin"))
                    windowed(bank(1), win[:, 0, :], fb[0], ps, pd, True).then_inc(dve_s.sem, 1)
                    dve.wait_ge(pe_s.sem, pe_s.here(i, f"{o}pfreq"))
                    for n in range(4):
                        dve.tensor_copy(pk[:, n, :], bank(2 + n)[:, 0:Q])
                    dve.drain()
                    tt(pa[:, 0, :], pk[:, 2, :], pk[:, 0, :], ALU.mult)
                    tt(pr[:, 0, :], pk[:, 3, :], pk[:, 1, :], ALU.mult)
                    tt(pa[:, 1, :], pk[:, 2, :], pk[:, 1, :], ALU.mult)
                    tt(pr[:, 1, :], pk[:, 3, :], pk[:, 0, :], ALU.mult)
                    dve.drain()
                    tt(pa[:, 0, :], pa[:, 0, :], pr[:, 0, :], ALU.subtract)
                    tt(pa[:, 1, :], pa[:, 1, :], pr[:, 1, :], ALU.add).then_inc(dve_s.sem, 1)
                    dve.wait_ge(pe_s.sem, pe_s.here(i, f"{o}pinv"))
                    for m in range(QT):
                        dve.scalar_tensor_tensor(out=ti[:, m, 0:NP_], in0=u[:, m, 0:NP_], scalar=hb(i, o, m), in1=bank(6)[:, m * 128:(m + 1) * 128],
                                                 op0=ALU.mult, op1=ALU.add)
                    dve.drain()
                    for m in range(QT):
                        last = tt(out[:, m, 0:NP_], ti[:, m, 0:NP_], x[:, m, 0:NP_], ALU.mult)
                    last.then_inc(dve_s.sem, 1)

                    for t in range(8):
                        dve.wait_ge(pe_s.sem, pe_s.here(i, f"{o}filt{t}"))
                        dve.wait_ge(act_s.sem, act_s.here(i, f"{o}win{t}"))
                        windowed(bank(t % 2), win[:, t % 2, :], fb[t % 2], ss[:, t, :], dd[:, t, :], t == 0).then_inc(dve_s.sem, 1)
                    for f in range(HKT):
                        for n, a in enumerate(ACC[1::2]):
                            dve.wait_ge(act_s.sem, act_s.here(i, f"{o}f{f}{ACC[2 * n]}"))
                            dve.wait_ge(pe_s.sem, pe_s.here(i, f"{o}f{f}{a}"))
                            ev, od = bank(2 * n + 1)[:, 0:Q], oc[:, n, :]
                            tt(uk[:, 2 * n, :], ev, od, ALU.add)
                            if a[0] in "CK":
                                last = tt(uk[:, 2 * n + 1, :], ev, od, ALU.subtract)
                            else:
                                last = dve.scalar_tensor_tensor(out=uk[:, 2 * n + 1, :], in0=ev, scalar=-1.0, in1=od, op0=ALU.mult, op1=ALU.add)
                            last.then_inc(dve_s.sem, 1)
                        dve.drain()
                        uc, us, kc, dk = (uk[:, 2 * n:2 * n + 2, :] for n in range(4))
                        yc, ys = pr[:, 0:2, :], pr[:, 2:4, :]
                        x1, x2 = fb[0], fb[1]
                        tt(yc, kc, uc, ALU.mult)
                        tt(x1, dk, us, ALU.mult)
                        tt(ys, kc, us, ALU.mult)
                        tt(x2, dk, uc, ALU.mult)
                        dve.drain()
                        tt(yc, yc, x1, ALU.subtract)
                        tt(ys, ys, x2, ALU.add)
                        dve.drain()
                        tt(ab[:, 0, 0, f, :], yc[:, 0, :], yc[:, 1, :], ALU.add)
                        tt(ab[:, 0, 1, f, :], yc[:, 0, :], yc[:, 1, :], ALU.subtract)
                        tt(ab[:, 1, 0, f, :], ys[:, 0, :], ys[:, 1, :], ALU.subtract)
                        tt(ab[:, 1, 1, f, :], ys[:, 0, :], ys[:, 1, :], ALU.add).then_inc(dve_s.sem, 1)
                    for n in range(2 * QT):
                        m, par = divmod(n, 2)
                        st = slice(NP_ + par, NP_ + par + 2 * HL - 1, 2)
                        dve.wait_ge(pe_s.sem, pe_s.here(i, f"{o}inv{n}"))
                        dve.scalar_tensor_tensor(out=ti[:, n % 2, :], in0=u[:, m, st], scalar=hb(i, o, m), in1=bank(n), op0=ALU.mult, op1=ALU.add)
                        dve.drain()
                        tt(out[:, m, st], ti[:, n % 2, :], x[:, m, st], ALU.mult).then_inc(dve_s.sem, 1)


def stage_hyena_out(k, A, scratch):
    stage_gemm(k, "hyo", lambda kt: k.H[:, kt, :], KT, A["hy_w_out"][0].rearrange("(k p) n -> p k n", p=128),
               KT, WB, evac_residual(k, 1, 0, COL["b_out"]), x_from=scratch["x_d"],
               src_from=[(k.H[:, m, :], scratch["z_d"][16 + m]) for m in range(KT)])


def build(nc, A, consts, Y, scratch):
    with ExitStack() as ctx:
        arena = ctx.enter_context(nc.sbuf_tensor("arena", [128, END], F32))
        psum = ctx.enter_context(nc.psum_tensor("acc", [128, 4096], F32))
        k = Kit(nc, ctx, arena, psum)
        stage_setup(k, A, consts)
        stage_project(k, A, Y, scratch, Norm(k, k.col("norm1", 0, 8), 0, 0, k.H, "n1_0"))
        stage_keys(k, A, Y, consts)
        stage_attend(k, latent=False)
        stage_attend(k, latent=True)
        stage_head_norm(k)
        k.reuse_semaphores()
        stage_rwkv_pre(k, A, scratch)
        stage_rwkv(k, A, Y, latent=False)
        stage_rwkv(k, A, Y, latent=True)
        stage_rwkv_post(k, A, scratch)
        k.reuse_semaphores()
        stage_mixer_out(k, A, scratch)
        stage_ffn(k, A, 0, Norm(k, k.col("norm2", 0, 8), 0, 1, k.H, "n2_0"))
        k.reuse_semaphores()
        stage_hyena_in(k, A, scratch, Norm(k, k.col("norm1", 8, 8), 1, 0, k.H, "n1_1"))
        stage_filter_features(k, A, consts, scratch)
        stage_hyena(k, A, consts, scratch)
        k.reuse_semaphores()
        stage_hyena_out(k, A, scratch)
        stage_ffn(k, A, 1, Norm(k, k.col("norm2", 8, 8), 1, 1, k.H, "n2_1"))
        stage_norm(k, Norm(k, k.col("final", 0, 8), None, 0, k.H, "n_f"))
        stage_out(k, A, Y)


_INS = ["x_prompt", "x_sample", "cache_diff_k", "cache_diff_v", "state_rwkv_fwd", "state_rwkv_bwd", "c", "c_ctx",
        "ada_w", "ada_b", "norm1_g", "norm2_g", "ffn_w1", "ffn_w3", "ffn_w2", "final_g",
        "ab_w_in", "ab_w_out", "diff_lambda", "diff_subln_g", "rwkv_mu", "rwkv_w0", "rwkv_w_up", "rwkv_a0", "rwkv_a_up",
        "rwkv_g_up", "rwkv_k_k", "rwkv_k_a", "rwkv_r_k", "rwkv_ln_g", "rwkv_ln_b",
        "hy_w_in", "hy_b_in", "hy_conv_w", "hy_conv_b", "hy_f_w0", "hy_f_b0", "hy_f_w1", "hy_f_b1", "hy_f_w2", "hy_f_b2",
        "hy_f_w3", "hy_f_freq", "hy_bias", "hy_w_out", "hy_b_out"]
_OUTS = [("y_prompt", (1, 128, 1024)), ("y_sample", (1, 1024, 1024)), ("new_k", (1, 1, 8, 2, 128, 32)),
         ("new_v", (1, 1, 8, 128, 64)), ("new_f", (1, 1, 8, 64, 64)), ("new_b", (1, 1, 8, 64, 64))]
_SCRATCH = [("rw_d", (RW_TILES, 128, T)), ("x_d", (128, KT * T)), ("z_d", (24, 128, T))]


def shape_constants():
    c = {}
    blk = np.zeros((128, CW), np.float32)

    def put(name, v):
        o, w = CCOL[name]
        blk[:, o:o + w] = v

    p = np.arange(128)
    put("ident", np.eye(128))
    put("blockones", (p[:, None] // 64 == p[None] // 64))
    s, t = p[:, None] % 64, p[None] % 64
    late = p[None] // 64
    put("mask_f", np.where(late, s <= t, s < t))
    put("mask_b", np.where(late, s >= t, s > t))
    j = np.arange(64)[None]
    put("lt", -1.0 * (p[:, None] % 64 < j))
    put("gt", -1.0 * (p[:, None] % 64 > j))
    put("ident2", p[:, None] % 64 == j)
    put("scan", (np.arange(256)[None] % 64 != 0) * np.ones((128, 1)))
    rot = np.zeros((128, 128))
    for m in range(128):
        if (m // 8) % 2 == 0:
            rot[m + 8, m] = -1.0
        else:
            rot[m - 8, m] = 1.0
    put("rot", rot)
    put("nz", (p[:, None] != 0))
    c["cblk"] = blk
    tt = np.arange(NL)
    inv = 10000.0 ** (-np.arange(8, dtype=np.float32) / 8)
    ar, ac = (tt // 64)[:, None] * inv[None], (tt % 64)[:, None] * inv[None]
    ang = np.concatenate([ar, ar, ac, ac], 1).T.astype(np.float32).astype(np.float64)
    c["rope"] = np.stack([np.tile(np.cos(ang), (4, 1)), np.tile(np.sin(ang), (4, 1))]).astype(np.float32)
    def table(length, steps, freqs):
        phase = (np.outer(steps, 2 * freqs + 1) % (4 * length)) * (math.pi / (2 * length))
        return np.cos(phase), np.sin(phase)

    a, f = np.arange(HL), np.arange(HL)
    fwd = [[None] * 2 for _ in range(2)]
    for par in range(2):
        fwd[0][par], fwd[1][par] = table(NL, 2 * a + par, f)
    lay = lambda m: m.reshape(HKT, 128, HL).transpose(1, 0, 2)
    c["dft"] = np.stack([[lay(fwd[q][par]) for par in range(2)] for q in range(2)]).transpose(2, 0, 1, 3, 4).reshape(128, -1).astype(np.float32)
    c["idft"] = np.stack([[lay(fwd[q][par].T / NL) for par in range(2)] for q in range(2)]).transpose(2, 0, 1, 3, 4).reshape(128, -1).astype(np.float32)
    pc, psn = table(NP_, np.arange(NP_), np.arange(NP_))
    c["pdft"] = np.concatenate([pc, psn, pc.T / NP_, psn.T / NP_], 1).astype(np.float32)
    feat = []
    for length in (NP_, NL):
        t = np.linspace(0.0, 1.0, length)[None]
        wpos = 2.0 * math.pi * np.arange(length)[None] / length
        fr = np.linspace(1e-4, 15, 16)[:, None]
        feat.append(np.concatenate([t, np.cos(fr * wpos), -np.sin(fr * wpos)], 0))
    c["feat"] = np.concatenate(feat, 1).astype(np.float32)
    cols = [-(2 * (128 * (n % HKT) + p) + n // HKT) / (NL - 1) for n in range(8)] + [-p / (NP_ - 1)]
    c["steps"] = np.stack(cols, 1).astype(np.float32)
    lo, hi = math.log(1e-2) / 1.5, math.log(1e-2) / 0.3
    c["deltas"] = np.broadcast_to(np.abs(np.linspace(lo, hi, D))[None], (128, D)).astype(np.float32)
    return c


def kernel(**inputs):
    import numpy as _np
    import concourse.bacc as _bacc
    from concourse import mybir as _mybir
    from concourse.bass_utils import run_bass_kernel_spmd as _run

    nc = _bacc.Bacc("TRN2", target_bir_lowering=False, num_devices=1)
    f32 = _mybir.dt.float32
    arrays, A, consts, Y, scratch = {}, {}, {}, {}, {}
    for name in _INS:
        a = _np.ascontiguousarray(inputs[name])
        arrays[f"in_{name}"] = a
        A[name] = nc.dram_tensor(f"in_{name}", a.shape, f32, kind="ExternalInput").ap()
    for name, a in shape_constants().items():
        arrays[f"const_{name}"] = a
        consts[name] = nc.dram_tensor(f"const_{name}", a.shape, f32, kind="ExternalInput").ap()
    for name, shape in _OUTS:
        Y[name] = nc.dram_tensor(f"out_{name}", shape, f32, kind="ExternalOutput").ap()
    for name, shape in _SCRATCH:
        scratch[name] = nc.dram_tensor(f"scratch_{name}", shape, f32, kind="Internal").ap()
    build(nc, A, consts, Y, scratch)
    r = _run(nc, [arrays], core_ids=[0])
    return tuple(r.results[0][f"out_{name}"] for name, _ in _OUTS)
```
